# Optimizing a Trainium2 kernel written in Bass

```python
import math
import jax, jax.numpy as jnp
from jax import lax
import numpy as np

D_MODEL = 1024
BATCH = 1
SEQ = 512
DEPTH = 1

HEAD_DIM = 64
FOX_HEADS = 8
FOX_WIDTH = FOX_HEADS * HEAD_DIM
DIFF_HEADS = 4
DIFF_QK_DIM = 64
DIFF_V_DIM = 2 * DIFF_QK_DIM
DIFF_WIDTH = DIFF_HEADS * DIFF_V_DIM
MIX_WIDTH = FOX_WIDTH + DIFF_WIDTH
D_FF = ((8 * D_MODEL + 767) // 768) * 256
BLOCK_Q = 128
EPS = 1e-6
NEG_INF = -1e30

SPLIT_SIZES = (
    FOX_WIDTH,
    FOX_WIDTH,
    FOX_WIDTH,
    FOX_HEADS,
    2 * DIFF_HEADS * DIFF_QK_DIM,
    2 * DIFF_HEADS * DIFF_QK_DIM,
    DIFF_WIDTH,
)
IN_WIDTH = sum(SPLIT_SIZES)


def rms_norm(x, g):
    xf = x.astype(jnp.float32)
    y = xf * lax.rsqrt(jnp.mean(xf * xf, axis=-1, keepdims=True) + EPS)
    return (y * g.astype(jnp.float32)).astype(x.dtype)

def alibi_slopes(n):
    return 2.0 ** (-8.0 * jnp.arange(1, n + 1, dtype=jnp.float32) / n)

def fox_attention(q, k, v, log_f):
    b, h, s_len, d = q.shape
    scale = 1.0 / math.sqrt(d)
    c = jnp.cumsum(log_f, axis=-1)
    pos = jnp.arange(s_len)

    def one_block(i):
        t0 = i * BLOCK_Q
        qb = lax.dynamic_slice_in_dim(q, t0, BLOCK_Q, axis=2)
        cb = lax.dynamic_slice_in_dim(c, t0, BLOCK_Q, axis=2)
        tq = t0 + jnp.arange(BLOCK_Q)
        sc = jnp.einsum('bhqd,bhkd->bhqk', qb, k).astype(jnp.float32) * scale
        sc = sc + (cb[..., :, None] - c[..., None, :])
        sc = jnp.where(pos[None, :] <= tq[:, None], sc, NEG_INF)
        p = jax.nn.softmax(sc, axis=-1)
        return jnp.einsum('bhqk,bhkd->bhqd', p.astype(v.dtype), v)

    out = lax.map(one_block, jnp.arange(s_len // BLOCK_Q))
    return jnp.transpose(out, (1, 2, 0, 3, 4)).reshape(b, h, s_len, d)

def diff_attention(q, k, v, lam, slopes):
    b, h, _, s_len, d = q.shape
    dv = v.shape[-1]
    scale = 1.0 / math.sqrt(d)
    pos = jnp.arange(s_len)

    def one_block(i):
        t0 = i * BLOCK_Q
        qb = lax.dynamic_slice_in_dim(q, t0, BLOCK_Q, axis=3)
        tq = t0 + jnp.arange(BLOCK_Q)
        sc = jnp.einsum('bhcqd,bhckd->bhcqk', qb, k).astype(jnp.float32) * scale
        dist = (tq[:, None] - pos[None, :]).astype(jnp.float32)
        sc = sc - slopes[:, None, None, None] * dist
        sc = jnp.where(pos[None, :] <= tq[:, None], sc, NEG_INF)
        p = jax.nn.softmax(sc, axis=-1)
        a = p[:, :, 0] - lam * p[:, :, 1]
        return jnp.einsum('bhqk,bhkd->bhqd', a.astype(v.dtype), v)

    out = lax.map(one_block, jnp.arange(s_len // BLOCK_Q))
    return jnp.transpose(out, (1, 2, 0, 3, 4)).reshape(b, h, s_len, dv)

def first_inputs(seed: int = 0) -> dict:
    key = jax.random.key(seed)
    ks = jax.random.split(key, 16)
    f32 = jnp.float32
    nrm = lambda k, shape, s: jax.random.normal(k, shape, f32) * s
    x = jax.random.normal(ks[0], (BATCH, SEQ, D_MODEL), f32)
    mix_norm_g = 1.0 + nrm(ks[1], (DEPTH, D_MODEL), 0.02)
    w_in = nrm(ks[2], (DEPTH, D_MODEL, IN_WIDTH), D_MODEL ** -0.5)
    b_forget = 3.0 + nrm(ks[3], (DEPTH, FOX_HEADS), 0.5)
    lambda_q1 = nrm(ks[4], (DEPTH, DIFF_QK_DIM), 0.1)
    lambda_k1 = nrm(ks[5], (DEPTH, DIFF_QK_DIM), 0.1)
    lambda_q2 = nrm(ks[6], (DEPTH, DIFF_QK_DIM), 0.1)
    lambda_k2 = nrm(ks[7], (DEPTH, DIFF_QK_DIM), 0.1)
    diff_norm_g = 1.0 + nrm(ks[8], (DEPTH, DIFF_V_DIM), 0.02)
    w_out = nrm(ks[9], (DEPTH, MIX_WIDTH, D_MODEL), MIX_WIDTH ** -0.5)
    ffn_norm_g = 1.0 + nrm(ks[10], (DEPTH, D_MODEL), 0.02)
    w_gate = nrm(ks[11], (DEPTH, D_MODEL, D_FF), D_MODEL ** -0.5)
    w_up = nrm(ks[12], (DEPTH, D_MODEL, D_FF), D_MODEL ** -0.5)
    w_down = nrm(ks[13], (DEPTH, D_FF, D_MODEL), D_FF ** -0.5)
    final_norm_g = 1.0 + nrm(ks[14], (D_MODEL,), 0.02)
    return {"x": x, "mix_norm_g": mix_norm_g, "w_in": w_in, "b_forget": b_forget,
            "lambda_q1": lambda_q1, "lambda_k1": lambda_k1,
            "lambda_q2": lambda_q2, "lambda_k2": lambda_k2,
            "diff_norm_g": diff_norm_g, "w_out": w_out, "ffn_norm_g": ffn_norm_g,
            "w_gate": w_gate, "w_up": w_up, "w_down": w_down,
            "final_norm_g": final_norm_g}

def first_block(x, mix_norm_g, w_in, b_forget, lambda_q1, lambda_k1, lambda_q2,
              lambda_k2, diff_norm_g, w_out, ffn_norm_g, w_gate, w_up, w_down,
              final_norm_g):
    b, s_len, _ = x.shape
    slopes = alibi_slopes(DIFF_HEADS)
    offsets = list(np.cumsum(SPLIT_SIZES)[:-1])
    for l in range(DEPTH):
        h = rms_norm(x, mix_norm_g[l])
        proj = jnp.einsum('bsd,de->bse', h, w_in[l])
        fq, fk, fv, flog, dq, dk, dv = jnp.split(proj, offsets, axis=-1)

        to_heads = lambda t: jnp.transpose(t.reshape(b, s_len, FOX_HEADS, HEAD_DIM), (0, 2, 1, 3))
        log_f = jax.nn.log_sigmoid(flog.astype(jnp.float32) + b_forget[l].astype(jnp.float32))
        log_f = jnp.transpose(log_f, (0, 2, 1))
        fox_out = fox_attention(to_heads(fq), to_heads(fk), to_heads(fv), log_f)
        fox_out = jnp.transpose(fox_out, (0, 2, 1, 3)).reshape(b, s_len, FOX_WIDTH)

        qk_heads = lambda t: jnp.transpose(t.reshape(b, s_len, DIFF_HEADS, 2, DIFF_QK_DIM), (0, 2, 3, 1, 4))
        dv_h = jnp.transpose(dv.reshape(b, s_len, DIFF_HEADS, DIFF_V_DIM), (0, 2, 1, 3))
        lam_init = 0.8 - 0.6 * math.exp(-0.3 * l)
        lam = (jnp.exp(jnp.sum(lambda_q1[l].astype(jnp.float32) * lambda_k1[l].astype(jnp.float32)))
               - jnp.exp(jnp.sum(lambda_q2[l].astype(jnp.float32) * lambda_k2[l].astype(jnp.float32)))
               + lam_init)
        diff_out = diff_attention(qk_heads(dq), qk_heads(dk), dv_h, lam, slopes)
        diff_out = rms_norm(diff_out, diff_norm_g[l]) * (1.0 - lam_init)
        diff_out = jnp.transpose(diff_out, (0, 2, 1, 3)).reshape(b, s_len, DIFF_WIDTH)

        mixed = jnp.concatenate([fox_out, diff_out], axis=-1)
        x = x + jnp.einsum('bse,ed->bsd', mixed, w_out[l])

        h = rms_norm(x, ffn_norm_g[l])
        g = jnp.einsum('bsd,df->bsf', h, w_gate[l])
        u = jnp.einsum('bsd,df->bsf', h, w_up[l])
        x = x + jnp.einsum('bsf,fd->bsd', jax.nn.silu(g) * u, w_down[l])
    return rms_norm(x, final_norm_g)


GRID_W = 64
NA_HEADS = 8
NA_HEAD_DIM = 64
D_ATTN = NA_HEADS * NA_HEAD_DIM
NA_KH = 8
NA_KW = 16
Q_BLOCK_W = 16
K_BLOCK_W = 2 * NA_KW
N_COL_BLOCKS = GRID_W // Q_BLOCK_W
CONV_CH = 512
CONV_K = 31
D_FF_2 = 2816
FFN_CONV_K = 3
D_IN = 3 * D_ATTN + 2 * CONV_CH + 2 * D_MODEL
NEG = -1e30


def _rmsnorm(x, g):
    xf = x.astype(jnp.float32)
    y = xf * lax.rsqrt(jnp.mean(xf * xf, axis=-1, keepdims=True) + EPS)
    return (y * g.astype(jnp.float32)).astype(x.dtype)

def _layernorm(x, g, b):
    xf = x.astype(jnp.float32)
    mu = jnp.mean(xf, axis=-1, keepdims=True)
    var = jnp.mean(jnp.square(xf - mu), axis=-1, keepdims=True)
    y = (xf - mu) * lax.rsqrt(var + EPS)
    return (y * g.astype(jnp.float32) + b.astype(jnp.float32)).astype(x.dtype)

def _dwconv_centred(x, w, b):
    k = w.shape[0]
    pad = k // 2
    y = lax.conv_general_dilated(
        x, w[:, None, :].astype(x.dtype), window_strides=(1,), padding=[(pad, pad)],
        dimension_numbers=("NWC", "WIO", "NWC"), feature_group_count=x.shape[-1])
    return y + b.astype(x.dtype)

def _neighbourhood_attention(q, k, v, rpb):
    bsz, s, h, dh = q.shape
    rows = s // GRID_W
    kh = min(NA_KH, rows)
    scale = NA_HEAD_DIM ** -0.5
    qg = q.reshape(bsz, rows, GRID_W, h, dh)
    kg = k.reshape(bsz, rows, GRID_W, h, dh)
    vg = v.reshape(bsz, rows, GRID_W, h, dh)

    col = jnp.arange(GRID_W)
    col_start = jnp.clip(col - NA_KW // 2, 0, GRID_W - NA_KW)
    blk_start = jnp.minimum(col_start[jnp.arange(N_COL_BLOCKS) * Q_BLOCK_W],
                            GRID_W - K_BLOCK_W)
    key_col = blk_start[:, None] + jnp.arange(K_BLOCK_W)
    q_col = col.reshape(N_COL_BLOCKS, Q_BLOCK_W)
    cs = col_start.reshape(N_COL_BLOCKS, Q_BLOCK_W)
    kc = key_col[:, None, :]
    in_win = (kc >= cs[..., None]) & (kc < cs[..., None] + NA_KW)
    col_off = jnp.clip(kc - q_col[..., None] + NA_KW - 1, 0, 2 * NA_KW - 2)
    rpb_col = rpb.astype(jnp.float32)[:, :, col_off]
    mask = in_win[None, None, :, :, None, :]

    def one_row(r):
        rs = jnp.clip(r - kh // 2, 0, rows - kh)
        q_r = lax.dynamic_index_in_dim(qg, r, axis=1, keepdims=False)
        q_r = q_r.reshape(bsz, N_COL_BLOCKS, Q_BLOCK_W, h, dh)
        k_r = lax.dynamic_slice_in_dim(kg, rs, kh, axis=1)[:, :, key_col]
        v_r = lax.dynamic_slice_in_dim(vg, rs, kh, axis=1)[:, :, key_col]
        row_off = rs + jnp.arange(kh) - r + NA_KH - 1
        bias = jnp.take(rpb_col, row_off, axis=1).transpose(0, 2, 3, 1, 4)
        sc = jnp.einsum("bnqhd,bknjhd->bhnqkj", q_r, k_r).astype(jnp.float32) * scale
        sc = jnp.where(mask, sc + bias[None], NEG)
        p = jax.nn.softmax(sc.reshape(bsz, h, N_COL_BLOCKS, Q_BLOCK_W, kh * K_BLOCK_W), axis=-1)
        p = p.reshape(sc.shape).astype(v.dtype)
        o = jnp.einsum("bhnqkj,bknjhd->bnqhd", p, v_r)
        return o.reshape(bsz, GRID_W, h * dh)

    out = lax.map(one_row, jnp.arange(rows))
    return out.transpose(1, 0, 2, 3).reshape(bsz, s, h * dh)

def second_inputs(seed: int = 0) -> dict:
    key = jax.random.key(seed)
    ks = jax.random.split(key, 20)
    n = jax.random.normal
    f32 = jnp.float32
    L = DEPTH
    return {
        "x": n(ks[0], (BATCH, SEQ, D_MODEL), f32),
        "norm1_g": 1.0 + 0.05 * n(ks[1], (L, D_MODEL), f32),
        "w_in": n(ks[2], (L, D_MODEL, D_IN), f32) * D_MODEL ** -0.5,
        "b_in": 0.01 * n(ks[3], (L, D_IN), f32),
        "rpb": 0.1 * n(ks[4], (L, NA_HEADS, 2 * NA_KH - 1, 2 * NA_KW - 1), f32),
        "w_na_out": n(ks[5], (L, D_ATTN, D_MODEL), f32) * D_ATTN ** -0.5,
        "conv_dw_w": n(ks[6], (L, CONV_K, CONV_CH), f32) * CONV_K ** -0.5,
        "conv_dw_b": 0.01 * n(ks[7], (L, CONV_CH), f32),
        "conv_ln_g": 1.0 + 0.05 * n(ks[8], (L, CONV_CH), f32),
        "conv_ln_b": 0.01 * n(ks[9], (L, CONV_CH), f32),
        "w_conv_out": n(ks[10], (L, CONV_CH, D_MODEL), f32) * CONV_CH ** -0.5,
        "w_out": n(ks[11], (L, D_MODEL, D_MODEL), f32) * D_MODEL ** -0.5,
        "norm2_g": 1.0 + 0.05 * n(ks[12], (L, D_MODEL), f32),
        "w_up": n(ks[13], (L, D_MODEL, 2 * D_FF_2), f32) * D_MODEL ** -0.5,
        "ffn_dw_w": n(ks[14], (L, FFN_CONV_K, 2 * D_FF_2), f32) * FFN_CONV_K ** -0.5,
        "ffn_dw_b": 0.01 * n(ks[15], (L, 2 * D_FF_2), f32),
        "w_down": n(ks[16], (L, D_FF_2, D_MODEL), f32) * D_FF_2 ** -0.5,
        "norm_f_g": 1.0 + 0.05 * n(ks[17], (D_MODEL,), f32),
    }

def second_block(x, norm1_g, w_in, b_in, rpb, w_na_out, conv_dw_w, conv_dw_b, conv_ln_g,
              conv_ln_b, w_conv_out, w_out, norm2_g, w_up, ffn_dw_w, ffn_dw_b, w_down,
              norm_f_g):
    bsz, s, _ = x.shape
    splits = np.cumsum([D_ATTN, D_ATTN, D_ATTN, CONV_CH, CONV_CH, D_MODEL]).tolist()
    for l in range(DEPTH):
        h = _rmsnorm(x, norm1_g[l])
        z = h @ w_in[l] + b_in[l]
        q, k, v, c_a, c_b, g_a, g_b = jnp.split(z, splits, axis=-1)
        qh = q.reshape(bsz, s, NA_HEADS, NA_HEAD_DIM)
        kh = k.reshape(bsz, s, NA_HEADS, NA_HEAD_DIM)
        vh = v.reshape(bsz, s, NA_HEADS, NA_HEAD_DIM)
        br_a = _neighbourhood_attention(qh, kh, vh, rpb[l]) @ w_na_out[l]
        u = c_a * jax.nn.sigmoid(c_b)
        u = _dwconv_centred(u, conv_dw_w[l], conv_dw_b[l])
        u = jax.nn.silu(_layernorm(u, conv_ln_g[l], conv_ln_b[l]))
        br_b = u @ w_conv_out[l]
        merged = jax.nn.sigmoid(g_a) * br_a + jax.nn.sigmoid(g_b) * br_b
        x = x + merged @ w_out[l]
        h2 = _rmsnorm(x, norm2_g[l])
        up = _dwconv_centred(h2 @ w_up[l], ffn_dw_w[l], ffn_dw_b[l])
        gate, val = jnp.split(up, 2, axis=-1)
        x = x + (jax.nn.gelu(gate, approximate=False) * val) @ w_down[l]
    return _rmsnorm(x, norm_f_g)


def setup_inputs(seed=0):
    out = dict(first_inputs(seed))
    for name, value in second_inputs(seed + 1).items():
        if name != "x":
            out[name + "_2"] = value
    return out


def reference(
    x, mix_norm_g, w_in, b_forget, lambda_q1, lambda_k1, lambda_q2, lambda_k2, diff_norm_g,
    w_out, ffn_norm_g, w_gate, w_up, w_down, final_norm_g, norm1_g_2, w_in_2, b_in_2, rpb_2,
    w_na_out_2, conv_dw_w_2, conv_dw_b_2, conv_ln_g_2, conv_ln_b_2, w_conv_out_2, w_out_2,
    norm2_g_2, w_up_2, ffn_dw_w_2, ffn_dw_b_2, w_down_2, norm_f_g_2,
):
    x = first_block(
        x, mix_norm_g, w_in, b_forget, lambda_q1, lambda_k1, lambda_q2, lambda_k2, diff_norm_g,
        w_out, ffn_norm_g, w_gate, w_up, w_down, final_norm_g,
    )
    return second_block(
        x, norm1_g_2, w_in_2, b_in_2, rpb_2, w_na_out_2, conv_dw_w_2, conv_dw_b_2, conv_ln_g_2,
        conv_ln_b_2, w_conv_out_2, w_out_2, norm2_g_2, w_up_2, ffn_dw_w_2, ffn_dw_b_2, w_down_2,
        norm_f_g_2,
    )


_drawn_inputs = setup_inputs


def setup_inputs(seed=0):
    import zlib

    import numpy as np

    out = dict(_drawn_inputs(seed))
    spreads = {}
    factors = {'lambda_k1': 2.77,
     'lambda_q2': 2.911,
     'diff_norm_g': 4.305,
     'ffn_norm_g': 3.79,
     'b_in_2': 7.908,
     'rpb_2': 7.176,
     'conv_dw_b_2': 8.0,
     'conv_ln_g_2': 2.676,
     'conv_ln_b_2': 21.683,
     'ffn_dw_b_2': 7.623}
    for name, (base, spread) in spreads.items():
        noise = np.random.default_rng([zlib.crc32(name.encode()), seed]).standard_normal(out[name].shape)
        drawn = base * np.exp(spread * noise) if base else spread * noise
        out[name] = __import__('jax').numpy.asarray(drawn.astype(out[name].dtype))
    for name, factor in factors.items():
        out[name] = (out[name] * factor).astype(out[name].dtype)
    return out
```

```python
from contextlib import ExitStack

import numpy as np

import concourse.bass as bass
from concourse import mybir

F32 = mybir.dt.float32
F32R = mybir.dt.float32r
BF16 = mybir.dt.bfloat16
I32 = mybir.dt.int32
ALU = mybir.AluOpType
ACT = mybir.ActivationFunctionType
AX = mybir.AxisListType.X

P = 128
S = 512
D = 1024
KD = D // P
TC = S // P
FF = 2816
KF = FF // P
HD = 64
EPS = 1e-6
NEG = -1e30
UNIT = 1024
LAM_INIT = 0.2
GRID = 64
ROWS = S // GRID
RH, CW = 8, 16
RPR, RPC = 2 * RH - 1, 2 * CW - 1
TAPS = 31
WIN = 48


def plan_units():
    u = []
    v = lambda m, c0: [(m, 4 * k, 4, c0 + 256 * h, 256) for h in range(2) for k in range(2)]
    col = lambda m, c0: [(m, 0, 8, c0, 128)]
    FOX_Q, FOX_K, FOX_V, DQ, DK, DV = 0, 512, 1024, 1544, 2056, 2568
    u += v("w_in", FOX_V)
    for j in range(4):
        u += col("w_in", FOX_Q + P * j) + col("w_in", FOX_K + P * j)
    u += col("w_in", DQ) + col("w_in", DK)
    u += v("w_in", DV)
    for j in range(1, 4):
        u += col("w_in", DQ + P * j) + col("w_in", DK + P * j)
    for c in range(KD):
        u += col("w_out", P * c)
    marks = {"ffn1": len(u)}
    for j in range(KF):
        u += col("w_gate", P * j) + col("w_up", P * j)
    marks["down1"] = len(u)
    for c in range(KD):
        u += [("w_down", 0, 8, P * c, P), ("w_down", 8, 8, P * c, P), ("w_down", 16, 6, P * c, P)]
    NQ, NK, NV, CA, CB, GA, GB = 0, 512, 1024, 1536, 2048, 2560, 3584
    for j in range(4):
        u += col("w_in_2", CA + P * j) + col("w_in_2", CB + P * j)
    u += v("w_in_2", NV)
    for j in range(4):
        u += col("w_in_2", NQ + P * j) + col("w_in_2", NK + P * j)
    marks["gates"] = len(u)
    for c in range(2 * KD):
        u += col("w_in_2", GA + P * c)
    marks["na_out"] = len(u)
    u += [("w_na_out_2", 0, 4, 256 * c, 256) for c in range(4)]
    u += [("w_conv_out_2", 0, 4, 256 * c, 256) for c in range(4)]
    for c in range(KD):
        u += col("w_out_2", P * c)
    marks["ffn2"] = len(u)
    for j in range(KF):
        u += col("w_up_2", P * j) + col("w_up_2", FF + P * j)
    marks["down2"] = len(u)
    for c in range(KD):
        u += [("w_down_2", 0, 8, P * c, P), ("w_down_2", 8, 8, P * c, P), ("w_down_2", 16, 6, P * c, P)]
    marks["end"] = len(u)
    return u, marks


VECS = [("conv_dw_w_2", 4 * TAPS), ("ffn_dw_w_2", 3 * 2 * KF), ("ffn_dw_b_2", 2 * KF), ("b_in_2", 36),
        ("mix_norm_g", 8), ("ffn_norm_g", 8), ("final_norm_g", 8), ("norm1_g_2", 8), ("norm2_g_2", 8),
        ("norm_f_g_2", 8), ("conv_dw_b_2", 4), ("conv_ln_g_2", 4), ("conv_ln_b_2", 4), ("diff_norm_g", 1)]


def plan_vectors():
    at, loads, n = {}, [], 0
    for name, rows in VECS:
        at[name] = n
        done = 0
        while done < rows:
            k = min(rows - done, P - n % P)
            loads.append((name, done, k, n))
            done += k
            n += k
    return at, loads, n


def program(nc, d):
    units, marks = plan_units()
    NU = len(units)
    vec_at, vec_loads, n_vec = plan_vectors()
    ctx = ExitStack()
    base = 16512

    def at(name, off, shape, dt):
        return nc.alloc_sbuf_tensor_at(name, shape, dt, offset=base + off)

    XH = at("XH", 0, [P, KD, S], F32R)
    XL = at("XL", 16384, [P, KD, S], F32R)
    YF = at("YF", 0, [P, KD, S], F32)
    OUT = at("OUT", 16384, [P, TC, D], F32)
    WH = at("WH", 32768, [P, 4, UNIT], F32R)
    WL = at("WL", 49152, [P, 4, UNIT], F32R)
    RAW = at("RAW", 65536, [P, 2, UNIT], F32)
    X = at("X", 73728, [P, KD, S], F32)
    T = at("T", 90112, [P, 4, 520], F32)
    R = at("R", 98432, [P, S], F32)
    RP = at("RP", 100480, [P, S], F32)
    SS = at("SS", 102528, [P, 2, S], F32)
    SQ = at("SQ", 106624, [P, 2, S], F32)
    small = [110720]

    def tiny(name, shape, dt):
        n = int(np.prod(shape[1:])) * (2 if dt == BF16 else 4)
        o = small[0]
        small[0] += (n + 31) // 32 * 32
        assert small[0] <= 117760, name
        return at(name, o, shape, dt)

    PR = at("PR", 117760, [P, 4, S], F32)
    OD = at("OD", 102528, [P, S], F32)
    BVB = at("BVB", 102528, [P, S], F32)
    HH = at("HH", 117760, [P, KF, S], F32R)
    HL = at("HL", 117760 + 45056, [P, KF, S], F32R)
    BIG = 125952
    XTM = at("XTM", BIG, [P, TC, D], F32)
    MH = at("MH", BIG, [P, KD, S], F32R)
    ML = at("ML", BIG + 16384, [P, KD, S], F32R)

    def heads_memory(tag, o):
        return dict(VH=at("VH" + tag, o, [P, TC, S], F32R), VL=at("VL" + tag, o + 8192, [P, TC, S], F32R),
                    QH=at("QH" + tag, o + 16384, [P, 2, S], F32R), QL=at("QL" + tag, o + 20480, [P, 2, S], F32R),
                    KH=at("KH" + tag, o + 24576, [P, 2, S], F32R), KL=at("KL" + tag, o + 28672, [P, 2, S], F32R),
                    PTH=at("PTH" + tag, o + 32768, [P, TC, S], F32R), PTL=at("PTL" + tag, o + 40960, [P, TC, S], F32R))

    M1 = heads_memory("1", BIG + 32768)
    CR = at("CR", BIG + 81920, [P, S], F32R)
    TRI = at("TRI", BIG + 65536, [P, 896], F32R)
    LFH = at("LFH", BIG + 65536 + 3584, [P, TC, P], F32R)
    LFL = at("LFL", BIG + 65536 + 5632, [P, TC, P], F32R)
    CT = at("CT", BIG + 73728, [P, S], F32R)
    STG = at("STG", BIG + 73728 + 2048, [P, 896], F32)
    ROWV = at("ROWV", 117760, [P, 4, P], F32)
    WFR = at("WFR", 119808, [P, KD, 8], F32)
    WFH = at("WFH", 120064, [P, KD, 8], F32R)
    WFL = at("WFL", 120320, [P, KD, 8], F32R)
    Z = at("Z", 120576, [P, 4, TC * 8], F32)
    LAMV = at("LAMV", 121088, [P, 4, HD], F32)
    MKS = at("MKS", 125952 + 32768, [P, 4, 384], F32)
    KC = at("KC", 125952 + 32768 + 6144, [P, 384], F32)
    NAH = at("NAH", BIG, [P, 4, S], F32R)
    NAL = at("NAL", BIG + 8192, [P, 4, S], F32R)
    BN = at("BN", BIG + 16384, [P, ROWS, 8, WIN], F32)
    UW = 544
    UO = 16
    U = at("U", BIG + 28672, [P, 4, UW], F32)
    M2 = heads_memory("2", BIG + 37376)
    SG = at("SG", BIG + 37376, [P, 2 * KD, S], F32)
    Y = at("Y", BIG + 70144, [P, 4, S], F32)
    CH = at("CH", BIG + 28672, [P, 4, S], F32R)
    CL = at("CL", BIG + 78336, [P, 4, S], F32R)
    MH2 = at("MH2", BIG - 8192, [P, KD, S], F32R)
    ML2 = at("ML2", BIG + 8192, [P, KD, S], F32R)

    IDF = tiny("IDF", [P, P], F32)
    ONE = tiny("ONE", [P, P], F32)
    IDB = tiny("IDB", [P, P], BF16)
    CMB = tiny("CMB", [P, P], BF16)
    NMB = tiny("NMB", [P, 3, 384], BF16)
    VEC = tiny("VEC", [P, n_vec], F32)
    SELF = tiny("SELF", [P, 12], F32)
    SEL = tiny("SEL", [P, 12], F32R)
    BFG = tiny("BFG", [P, 8], F32)
    NM = tiny("NM", [P, 4], F32)
    RS = tiny("RS", [P, 4], F32)
    RI = tiny("RI", [P, 4], F32)
    RT = tiny("RT", [P, TC], F32)
    LAM = tiny("LAM", [P, 8], F32)
    GG = tiny("GG", [P, 8], F32)
    B8 = tiny("B8", [P, 4], F32)
    GD = tiny("GD", [P, 1], F32)
    QC = tiny("QC", [P, 1], F32)
    QI = tiny("QI", [P, 2], I32)
    BT = tiny("BT", [P, 1], F32)
    RPP = at("RPP", BIG + 79872, [P, GRID], F32)
    CST = at("CST", BIG + 79360, [P, P], F32)
    POS = at("POS", BIG + 32768 + 7680, [P, S], F32)
    CZ = [[at("CZ00", 100480, [P, S], F32), at("CZ01", 104576, [P, S], F32)],
          [at("CZ10", 106624, [P, S], F32), at("CZ11", 108672, [P, S], F32)]]
    SHIFT = 56
    scratch = nc.dram_tensor("rpb_shifted", [8, 8 * RPR, SHIFT], F32, kind="Internal").ap()

    PS = ctx.enter_context(nc.psum_tensor("PS", [P, 8, S], F32))
    ACC, SCO, TRB, OB = 0, 2, 4, 6

    def vcol(name, c, n=1):
        return VEC[:, vec_at[name] + c:vec_at[name] + c + n]

    sems = {}

    def sem(name):
        sems[name] = ctx.enter_context(nc.semaphore(name))
        return sems[name]

    x_in = sem("x_in")
    consts_in = sem("consts_in")
    rows_in = sem("rows_in")
    wf_in = sem("wf_in")
    rpb_in = sem("rpb_in")
    rpb_out = sem("rpb_out")
    bias_in = sem("bias_in")
    bv_in = sem("bv_in")
    w_landed = [sem(f"w_landed{i}") for i in range(2)]
    w_hi = sem("w_hi")
    w_lo = sem("w_lo")
    w_used = sem("w_used")
    pool_made = sem("pool_made")
    dve_made = sem("dve_made")
    vec_t = sem("vec_t")
    vec_ready = sem("vec_ready")
    part_ready = sem("part_ready")
    acc_free = sem("acc_free")
    prod = sem("prod")
    act_done = sem("act_done")
    low_done = sem("low_done")
    sq_ready = sem("sq_ready")
    ss_done = sem("ss_done")
    norm_ps = sem("norm_ps")
    ln_done = sem("ln_done")
    r_ready = sem("r_ready")
    rt_ps = sem("rt_ps")
    rt_ready = sem("rt_ready")
    r_mix = sem("r_mix")
    fl_ps = sem("fl_ps")
    fl_step = sem("fl_step")
    fl_act = sem("fl_act")
    lf_ready = sem("lf_ready")
    cum_ps = sem("cum_ps")
    cr_act = sem("cr_act")
    cr_dve = sem("cr_dve")
    wf_split = sem("wf_split")
    sc_ready = sem("sc_ready")
    biased = sem("biased")
    xg_ready = sem("xg_ready")
    merged = sem("merged")
    cz_mid = sem("cz_mid")
    cz_tap = sem("cz_tap")
    cz_taps = sem("cz_taps")
    gelu_done = sem("gelu_done")
    glu_ready = sem("glu_ready")
    hid_hi = sem("hid_hi")
    x1_done = sem("x1_done")
    lam_ready = sem("lam_ready")
    max_ready = sem("max_ready")
    exp_ready = sem("exp_ready")
    rinv_done = sem("rinv_done")
    p_half = sem("p_half")
    p_ready = sem("p_ready")
    tr_ready = sem("tr_ready")
    pth_done = sem("pth_done")
    ptl_done = sem("ptl_done")
    pv_ready = sem("pv_ready")
    oh_done = sem("oh_done")
    o_free = sem("o_free")
    od_copy = sem("od_copy")
    od_sq = sem("od_sq")
    od_ps = sem("od_ps")
    od_r = sem("od_r")
    od_scaled = sem("od_scaled")
    conv_done = sem("conv_done")
    ln_sum = sem("ln_sum")
    ln_ps = sem("ln_ps")
    ln_d = sem("ln_d")
    ln_r = sem("ln_r")
    ln_n = sem("ln_n")
    silu_done = sem("silu_done")
    ch_done = sem("ch_done")
    cl_done = sem("cl_done")
    out_ps = sem("out_ps")
    out_ready = sem("out_ready")
    stored = sem("stored")

    def perm_of(ap):
        return ap.rearrange("p (r g c) -> p g r c", r=ROWS, c=8)

    def natural_of(ap):
        return ap.rearrange("p (g r c) -> p r g c", r=ROWS, c=8)

    def grid3(ap, order):
        a, b = (GRID // 8, ROWS) if order == "perm" else (ROWS, GRID // 8)
        return ap.rearrange("p (a b c) -> p a b c", a=a, b=b)

    TL = {}
    n_tile = 0
    for name, n in [("init", 8), ("v1", 8), ("fox0", 2), ("foxf", 8), ("v2", 8), ("difff", 6), ("out1", 8),
                    ("ffn1", 44), ("down1", 8), ("cab", 8), ("v3", 8), ("na0", 2), ("naf", 6), ("gates", 16),
                    ("na_out", 8), ("conv_out", 8), ("out2", 8), ("ffn2", 44), ("down2", 8)]:
        TL[name] = n_tile
        n_tile += n
    UN = {"v1": 0, "fox0": 4, "foxf": 6, "v2": 14, "difff": 18, "out1": 24, "ffn1": marks["ffn1"],
          "down1": marks["down1"], "cab": marks["down1"] + 24, "v3": marks["down1"] + 32,
          "na0": marks["down1"] + 36, "naf": marks["down1"] + 38, "gates": marks["gates"],
          "na_out": marks["na_out"], "conv_out": marks["na_out"] + 4, "out2": marks["na_out"] + 8,
          "ffn2": marks["ffn2"], "down2": marks["down2"]}
    assert UN["out1"] + 8 == UN["ffn1"] and UN["naf"] + 6 == UN["gates"]

    PT0, n_part = {}, 0
    for name in TL:
        PT0[name] = n_part
        n_part += {"init": 8, "v": 6, "na_out": 4, "conv_out": 4}.get("v" if name[0] == "v" else name, 0)

    per = {"init": (8, 8), "v1": (8, 8), "fox0": (2, 2), "foxf": (8, 8), "v2": (8, 8), "difff": (6, 6),
           "out1": (8, 8), "ffn1": (44, 22), "down1": (8, 8), "cab": (8, 4), "v3": (8, 8), "na0": (2, 2),
           "naf": (6, 6), "gates": (16, 0), "na_out": (0, 0), "conv_out": (8, 8), "out2": (8, 8),
           "ffn2": (0, 22), "down2": (0, 8)}
    H0, L0 = {}, {}
    h = l = 0
    for name in TL:
        H0[name], L0[name] = h, l
        h += per[name][0]
        l += per[name][1]

    def src_of(spec):
        m, k0, nk, c0, nc_ = spec
        return d[m].rearrange("(k p) n -> p k n", p=P)[:, k0:k0 + nk, c0:c0 + nc_]

    block = ctx.enter_context(nc.Block())

    @block.sync
    def _(sp):
        def load(n, s, src, width=UNIT, ncols=P):
            u = 4 * n + s
            if not (isinstance(n, int) and u < 2):
                sp.wait_ge(w_lo, u - 1)
            dst = RAW[:, s % 2, 0:width].rearrange("p (k n) -> p k n", n=ncols)
            sp.dma_start(dst, src).then_inc(w_landed[s % 2], 16)

        def load_units(lo, hi):
            for u in range(lo, hi):
                m, k0, nk, c0, ncol = units[u]
                load(u // 4, u % 4, src_of(units[u]), nk * ncol, ncol)

        for t in range(TC):
            sp.dma_start(XTM[:, t, :], d["x"][t * P:(t + 1) * P, :]).then_inc(x_in, 16)
        load_units(0, 2)
        sp.dma_start(WFR[:, :, :], d["w_in"].rearrange("(k p) n -> p k n", p=P)[:, :, 1536:1544]).then_inc(wf_in, 16)
        sp.wait_ge(pool_made, 1)
        for o in range(RPR):
            sp.dma_start(RPP[8 * o:8 * o + 8, 16:16 + RPC], d["rpb_2"][:, o, :]).then_inc(rpb_in, 16)
        sp.wait_ge(rpb_in, 16 * RPR)
        for cq in range(8):
            sp.dma_start(scratch[cq], RPP[0:8 * RPR, 7 - cq:7 - cq + SHIFT]).then_inc(rpb_out, 16)
        load_units(2, marks["ffn1"])

        def looped(lo, count, mats):
            with sp.Fori(0, count) as i:
                for s, (m, off, step) in enumerate(mats):
                    src = d[m].rearrange("(k p) n -> p k n", p=P)[:, 0:KD, bass.ds(i * step + off, P)]
                    load(i + lo // 4, s, src)

        looped(marks["ffn1"], KF // 2, [("w_gate", 0, 256), ("w_up", 0, 256), ("w_gate", P, 256), ("w_up", P, 256)])
        load_units(marks["down1"], marks["down1"] + 28)
        sp.wait_ge(w_used, UN["down1"] + 24)
        sp.wait_ge(rpb_out, 16 * 8)
        for gq in range(2):
            for qr in range(ROWS):
                off = (RH - 1 - qr) * 8 * SHIFT + 8 - 8 * gq
                src = bass.AP(tensor=scratch.tensor, offset=off,
                              ap=[[8 * RPR * SHIFT, 8], [SHIFT, ROWS * 8], [1, WIN]])
                q0 = gq * 64 + qr * 8
                sp.dma_start(BN[q0:q0 + 8, :, :, :].rearrange("p r h c -> p (r h) c"), src).then_inc(bias_in, 16)
        sp.wait_ge(norm_ps, 4)
        sp.dma_start(BVB[:, :], d["b_in_2"][1024:1536].partition_broadcast(P)).then_inc(bv_in, 16)
        load_units(marks["down1"] + 28, marks["gates"])
        looped(marks["gates"], 4, [("w_in_2", 2560 + P * s, 512) for s in range(4)])
        load_units(marks["na_out"], marks["ffn2"])
        looped(marks["ffn2"], KF // 2, [("w_up_2", 0, 256), ("w_up_2", FF, 256), ("w_up_2", P, 256), ("w_up_2", FF + P, 256)])
        load_units(marks["down2"], NU)
        for t in range(TC):
            sp.wait_ge(out_ready, 2 * t + 2)
            sp.dma_start(d["out"][t * P:(t + 1) * P, :], OUT[:, t, :]).then_inc(stored, 16)
        sp.wait_ge(stored, 16 * TC)

    @block.gpsimd
    def _(pool):
        made = [0]

        def step(ins, wait=True):
            made[0] += 1
            ins.then_inc(pool_made, 1)
            if wait:
                pool.wait_ge(pool_made, made[0])

        step(pool.memset(RPP[:, :], 0.0))
        step(pool.memset(IDF[:, :], 0.0))
        step(pool.affine_select(out=IDF[:, :], in_=IDF[:, :], compare_op=ALU.not_equal, fill=1.0, base=0,
                                pattern=[[-1, P]], channel_multiplier=1))
        step(pool.memset(ONE[:, :], 1.0))
        step(pool.memset(SELF[:, :], 0.0))
        for b in (0, -32):
            step(pool.affine_select(out=SELF[:, 0:8], in_=SELF[:, 0:8], compare_op=ALU.not_equal, fill=1.0, base=b,
                                    pattern=[[-1, 8]], channel_multiplier=1))
        for j in range(4):
            step(pool.memset(SELF[64:65, 8 + j:9 + j], 2.0 ** (-2 * (j + 1))))
        step(pool.memset(STG[:, :], 0.0))
        step(pool.affine_select(out=STG[:, :], in_=STG[:, :], compare_op=ALU.is_gt, fill=1.0, base=384,
                                pattern=[[-1, 896]], channel_multiplier=1))
        step(pool.memset(CST[:, :], 0.0))
        step(pool.affine_select(out=CST[:, :], in_=CST[:, :], compare_op=ALU.is_ge, fill=NEG, base=0,
                                pattern=[[-1, P]], channel_multiplier=1))
        step(pool.iota(POS[:, :], [[1, S]], base=0, channel_multiplier=0, allow_small_or_imprecise_dtypes=True))
        step(pool.iota(KC[:, :].rearrange("p (g r c) -> p g r c", g=6, r=ROWS), [[8, 6], [0, ROWS], [1, 8]], base=0,
                       channel_multiplier=0, allow_small_or_imprecise_dtypes=True))
        step(pool.iota(QI[:, 0:1], [[0, 1]], base=0, channel_multiplier=1))

        def lo_part(n, s, width=UNIT):
            u = 4 * n + s
            pool.wait_ge(w_hi, u + 1)
            if not (isinstance(n, int) and n == 0):
                pool.wait_ge(w_used, u - 3)
            pool.tensor_tensor(WL[:, s, 0:width], RAW[:, s % 2, 0:width], WH[:, s, 0:width].bitcast(F32),
                               ALU.subtract).then_inc(w_lo, 1)

        def lo_parts(g0, g1):
            if g0 == 0:
                for s in range(4):
                    lo_part(0, s)
                g0 = 1
            with pool.Fori(g0, g1) as i:
                for s in range(4):
                    lo_part(i, s)

        def lo_down(u0):
            for u in range(u0, u0 + 24):
                lo_part(u // 4, u % 4, units[u][2] * P)

        lo_parts(0, marks["down1"] // 4)
        lo_down(marks["down1"])
        lo_parts(marks["down1"] // 4 + 6, marks["down2"] // 4)
        lo_down(marks["down2"])

    NA_KEYS = [(0, 2), (0, 3), (1, 4), (2, 4)]

    def family(kind):
        if kind == "diff":
            sc = [(hd, comp, qb) for hd in range(4) for qb in range(4) for comp in range(2)]
            tr = [(hd, qb) for hd in range(4) for qb in range(4)]
            ready_after = {2 * i + 1: i for i in range(16)}
        else:
            sc = [(hd, hd % 2, qb) for hd in range(8) for qb in range(4)]
            tr = [(hd, qb) for hd in range(8) for qb in range(4)]
            ready_after = {i: i for i in range(32)}
        return sc, tr, ready_after

    FAM = {"fox": dict(mem=M1, fill="foxf", nfill=8, s0=0, t0=0, o0=0),
           "diff": dict(mem=M1, fill="difff", nfill=6, s0=32, t0=32, o0=8),
           "na": dict(mem=M2, fill="naf", nfill=6, s0=64, t0=48, o0=12)}

    def keys_of(kind, qb):
        return NA_KEYS[qb] if kind == "na" else (0, qb + 1)

    def filler_steps(f):
        s = 8 * (f // 2) + 3 * (f % 2)
        return range(s, s + 3)

    def filler_done(kind, step):
        return [f for f in range(FAM[kind]["nfill"]) if filler_steps(f)[-1] == step]

    def pair_index(kind, hd):
        return hd if kind == "diff" else hd // 2

    def slot_free(kind, i):
        t0 = FAM[kind]["t0"]
        if i < 4:
            return t0
        return t0 + ((i - 4) // 2 + 1 if kind == "diff" else i - 3)

    def parity_of_filler(kind, f):
        return (f // 2 + 1) % 2

    @block.tensor
    def _(pe):
        def mm3(out, ah, al, bh, bl, start, stop):
            pe.matmul(out, ah, bh, start=start, stop=False)
            pe.matmul(out, ah, bl, start=False, stop=False)
            return pe.matmul(out, al, bh, start=False, stop=stop)

        def need_acc(a):
            if not (isinstance(a, int) and a < 2):
                pe.wait_ge(acc_free, a - 1)

        def fm_chunks(n, s, bank, k0, ks, bh, bl, start, stop, ncols=P, c0=0):
            for k in ks:
                w0 = k * ncols + c0
                ins = mm3(PS[:, ACC + bank, :], WH[:, s, w0:w0 + P], WL[:, s, w0:w0 + P],
                          bh[:, k0 + k, :], bl[:, k0 + k, :], start and k == ks[0], stop and k == ks[-1])
            return ins

        def fm_tile(n, s, a, bh=XH, bl=XL, chunk_ready=None):
            pe.wait_ge(w_lo, 4 * n + s + 1)
            need_acc(a)
            for k in range(KD):
                if chunk_ready:
                    chunk_ready(k)
                ins = fm_chunks(n, s, s % 2, 0, [k], bh, bl, k == 0, k == KD - 1)
            ins.then_inc(w_used, 1)

        def low(base):
            return lambda k: pe.wait_ge(low_done, base + k + 1)

        def v_tiles(u0, a0, hook=None):
            for half in range(2):
                pe.wait_ge(w_lo, u0 + 2 * half + 2)
                for t in range(TC):
                    a = a0 + TC * half + t
                    need_acc(a)
                    for k in range(KD):
                        u = u0 + 2 * half + k // 4
                        w = slice((k % 4) * 256, (k % 4) * 256 + 256)
                        ins = mm3(PS[:, ACC + a % 2, 0:256], XH[:, k, t * P:(t + 1) * P], XL[:, k, t * P:(t + 1) * P],
                                  WH[:, u % 4, w], WL[:, u % 4, w], k == 0, k == KD - 1)
                    if t == TC - 1:
                        ins.then_inc(w_used, 2)
                    else:
                        ins.then_inc(part_ready, 1)
                    if hook:
                        hook(TC * half + t)

        def norm_sum(ss, which=0):
            pe.wait_ge(ss_done, ss)
            pe.matmul(PS[:, SCO + which, :], ONE[:, :], SS[:, which, :], start=True, stop=True).then_inc(norm_ps, 1)

        def rt_transposes(src):
            for t in range(TC):
                ins = pe.transpose(PS[:, SCO + 1, t * P:(t + 1) * P], src[:, t * P:(t + 1) * P], IDF[:, :])
            ins.then_inc(rt_ps, 1)

        pe.wait_ge(pool_made, 4)
        pe.wait_ge(x_in, 16 * TC)
        for c in range(KD):
            need_acc(c)
            for t in range(TC):
                ins = pe.transpose(PS[:, ACC + c % 2, t * P:(t + 1) * P], XTM[:, t, c * P:(c + 1) * P], IDF[:, :])
            ins.then_inc(part_ready, 1)
            if c == 0:
                pe.wait_ge(rows_in, 16 * len(vec_loads))
                for i in range(4):
                    r = min(P, n_vec - i * P)
                    ins = pe.transpose(PS[:, OB, i * P:i * P + r], ROWV[0:r, i, :], IDF[0:r, 0:r])
                ins.then_inc(vec_t, 1)

        def behind_first_v(i):
            if i != 1:
                return
            norm_sum(8)
            pe.wait_ge(wf_split, 2)
            for t in range(TC):
                for k in range(KD):
                    ins = mm3(PS[:, TRB, t * 8:t * 8 + 8], XH[:, k, t * P:(t + 1) * P], XL[:, k, t * P:(t + 1) * P],
                              WFH[:, k, :], WFL[:, k, :], k == 0, k == KD - 1)
            ins.then_inc(fl_ps, 1)
            pe.wait_ge(r_ready, 1)
            rt_transposes(R)

        pe.wait_ge(low_done, L0["v1"])
        v_tiles(UN["v1"], TL["v1"], behind_first_v)
        for i in range(2):
            u = UN["fox0"] + i
            fm_tile(u // 4, u % 4, TL["fox0"] + i)
        pe.wait_ge(lf_ready, 2)
        for t in range(TC):
            for i, part in enumerate((LFH, LFL)):
                ins = pe.matmul(PS[:, TRB + 1, :], part[:, t, :], TRI[:, 384 - P * t:896 - P * t],
                                start=(t == 0 and i == 0), stop=(t == TC - 1 and i == 1))
        ins.then_inc(cum_ps, 1)

        def attention(kind):
            f = FAM[kind]
            sc, tr, ready_after = family(kind)
            mem, s0, t0, o0, a0 = f["mem"], f["s0"], f["t0"], f["o0"], TL[f["fill"]]
            u0 = UN[f["fill"]]
            first_low = L0[f["fill"]]
            pending_pv = []

            def scores(i):
                hd, half, qb = sc[i]
                g = s0 + i
                pair = pair_index(kind, hd)
                pe.wait_ge(low_done, first_low + 2 * pair)
                if g >= 2:
                    pe.wait_ge(exp_ready, g - 1)
                if i == 0 and kind == "fox":
                    pe.wait_ge(cr_act, 2)
                    pe.wait_ge(cr_dve, 2)
                k0, k1 = keys_of(kind, qb)
                n = (k1 - k0) * P
                out = PS[:, SCO + g % 2, 0:n]
                r = slice(half * HD, half * HD + HD)
                q = slice(qb * P, qb * P + P)
                ks = slice(k0 * P, k1 * P)
                par = pair % 2
                pe.matmul(out, mem["QH"][r, par, q], mem["KH"][r, par, ks], start=True, stop=False)
                pe.matmul(out, mem["QH"][r, par, q], mem["KL"][r, par, ks], start=False, stop=False)
                pe.matmul(out, mem["QL"][r, par, q], mem["KH"][r, par, ks], start=False, stop=False)
                if kind == "na":
                    m = {0: 1, 1: 0, 2: 0, 3: 2}[qb]
                    ins = pe.matmul(out, IDB[:, :], NMB[:, m, 0:n], start=False, stop=True)
                else:
                    c = hd if kind == "fox" else 8 + hd
                    col = SEL[:, c:c + 1]
                    sel = bass.AP(tensor=col.tensor, offset=col.offset, ap=[list(col.ap[0]), [0, P]])
                    pe.matmul(out, sel, CR[:, 0:n], start=False, stop=False)
                    ins = pe.matmul(PS[:, SCO + g % 2, n - P:n], IDB[:, :], CMB[:, :], start=False, stop=True)
                ins.then_inc(sc_ready, 1)

            def transposes(j):
                hd, qb = tr[j]
                g = t0 + j
                pe.wait_ge(p_ready, g + 1)
                if g >= 2:
                    pe.wait_ge(ptl_done, g - 1)
                k0, k1 = keys_of(kind, qb)
                i = [k for k, v in ready_after.items() if v == j][0]
                slot = (s0 + i - (1 if kind == "diff" else 0)) % 4
                for k in range(k1 - k0):
                    ins = pe.transpose(PS[:, TRB + g % 2, k * P:(k + 1) * P], PR[:, slot, k * P:(k + 1) * P], IDF[:, :])
                ins.then_inc(tr_ready, 1)

            def pv(hd):
                g = o0 + hd
                pe.wait_ge(ptl_done, t0 + 4 * hd + 4)
                if g >= 2:
                    pe.wait_ge(o_free, g - 1)
                vc = slice(hd * P, hd * P + P) if kind == "diff" else slice((hd // 2) * P, (hd // 2) * P + P)
                for n, kc in enumerate((1, 0, 2, 3) if kind == "na" else range(4)):
                    qs = [qb for qb in range(4) if keys_of(kind, qb)[0] <= kc < keys_of(kind, qb)[1]]
                    q = slice(0, S) if n == 0 else slice(qs[0] * P, (qs[-1] + 1) * P)
                    ins = mm3(PS[:, OB + g % 2, q], mem["VH"][:, kc, vc], mem["VL"][:, kc, vc],
                              mem["PTH"][:, kc, q], mem["PTL"][:, kc, q], n == 0, n == 3)
                ins.then_inc(pv_ready, 1)

            def odsum(hd):
                pe.wait_ge(od_sq, hd + 1)
                g = o0 + hd
                pe.matmul(PS[:, OB + g % 2, :], ONE[:, :], SQ[:, 0, :], start=True, stop=True).then_inc(od_ps, 1)

            n = len(sc)
            odq = []
            for i in range(n + 3):
                if i < n:
                    scores(i)
                for fl in range(f["nfill"]):
                    st = filler_steps(fl)
                    if i in st:
                        u = u0 + fl
                        bank = (a0 + fl) % 2
                        j = i - st[0]
                        if j == 0:
                            pe.wait_ge(w_lo, u + 1)
                            need_acc(a0 + fl)
                        ks = [range(0, 3), range(3, 6), range(6, 8)][j]
                        ins = fm_chunks(u // 4, u % 4, bank, 0, ks, XH, XL, j == 0, j == 2)
                        if j == 2:
                            ins.then_inc(w_used, 1)
                for hd in odq:
                    odsum(hd)
                odq = []
                if i - 3 in ready_after and ready_after[i - 3] % 4 == 3:
                    hd = ready_after[i - 3] // 4
                    pv(hd)
                    if kind == "diff":
                        odq = [hd]
                if i - 2 in ready_after:
                    transposes(ready_after[i - 2])
            for hd in odq:
                odsum(hd)

        attention("fox")
        v_tiles(UN["v2"], TL["v2"])
        attention("diff")

        def mixed_ready(k):
            n = 2 * k + 2 if k < 4 else 4 + k + 1
            pe.wait_ge(oh_done, n)
            pe.wait_ge(o_free, n)

        for c in range(KD):
            u = UN["out1"] + c
            fm_tile(u // 4, u % 4, TL["out1"] + c, MH, ML, mixed_ready if c == 0 else None)

        def pairs_with_norm(name, ss, base):
            for s in range(4):
                fm_tile(UN[name] // 4, s, TL[name] + s, chunk_ready=low(base) if s == 0 else None)
                if s == 0:
                    norm_sum(ss)
            with pe.Fori(1, KF // 2) as i:
                for s in range(4):
                    fm_tile(i + UN[name] // 4, s, 4 * i + s + TL[name])

        def down(name, base):
            for c in range(KD):
                a = TL[name] + c
                for j in range(3):
                    u = UN[name] + 3 * c + j
                    pe.wait_ge(w_lo, u + 1)
                    if j == 0:
                        need_acc(a)
                    nk = units[u][2]
                    for k in range(nk):
                        if c == 0:
                            pe.wait_ge(low_done, base + 8 * j + k + 1)
                        ins = fm_chunks(u // 4, u % 4, a % 2, 8 * j, [k], HH, HL, j == 0 and k == 0, j == 2 and k == nk - 1)
                    ins.then_inc(w_used, 1)

        pairs_with_norm("ffn1", 16, L0["out1"])
        down("down1", L0["ffn1"])

        for i in range(8):
            u = UN["cab"] + i
            fm_tile(u // 4, u % 4, TL["cab"] + i, chunk_ready=low(L0["down1"]) if i == 0 else None)
            if i == 0:
                norm_sum(32, 0)
                norm_sum(32, 1)

        def behind_second_v(i):
            if i == 0:
                pe.wait_ge(r_mix, 4)
                rt_transposes(RP)

        v_tiles(UN["v3"], TL["v3"], behind_second_v)
        for i in range(2):
            u = UN["na0"] + i
            fm_tile(u // 4, u % 4, TL["na0"] + i)
        attention("na")
        with pe.Fori(0, 4) as i:
            for s in range(4):
                fm_tile(i + UN["gates"] // 4, s, 4 * i + s + TL["gates"])

        def half_units(name, bh, bl, hook=None, chunk_ready=None):
            for c in range(8):
                u, a = UN[name] + c // 2, TL[name] + c
                pe.wait_ge(w_lo, u + 1)
                need_acc(a)
                for k in range(4):
                    if c == 0 and chunk_ready:
                        chunk_ready(k)
                    ins = fm_chunks(u // 4, u % 4, a % 2, 0, [k], bh, bl, k == 0, k == 3, 256, P * (c % 2))
                ins.then_inc(w_used if c % 2 else part_ready, 1)
                if hook:
                    hook(c)

        def layernorm_sums(c):
            if c == 1:
                pe.wait_ge(ln_sum, 3)
                pe.matmul(PS[:, SCO, :], ONE[:, :], SS[:, 0, :], start=True, stop=True).then_inc(ln_ps, 1)
            if c == 5:
                pe.wait_ge(ss_done, 36)
                pe.matmul(PS[:, SCO + 1, :], ONE[:, :], SS[:, 0, :], start=True, stop=True).then_inc(ln_ps, 1)

        pe.wait_ge(oh_done, 20)
        pe.wait_ge(o_free, 20)
        half_units("na_out", NAH, NAL, layernorm_sums)
        half_units("conv_out", CH, CL, chunk_ready=lambda k: pe.wait_ge(cl_done, k + 1))
        for c in range(KD):
            u = UN["out2"] + c
            fm_tile(u // 4, u % 4, TL["out2"] + c, MH2, ML2, low(L0["conv_out"]) if c == 0 else None)
        pairs_with_norm("ffn2", 44, L0["out2"])
        down("down2", L0["ffn2"])
        norm_sum(52)
        for g in range(8):
            t, half = g // 2, g % 2
            if g >= 4:
                pe.wait_ge(out_ready, g - 3)
            for c in range(4):
                if g < 2:
                    pe.wait_ge(low_done, L0["down2"] + 4 * half + c + 1)
                ins = pe.transpose(PS[:, 4 + g % 4, c * P:(c + 1) * P], YF[:, 4 * half + c, t * P:(t + 1) * P], IDF[:, :])
            ins.then_inc(out_ps, 1)
            if g == 3:
                pe.wait_ge(r_ready, 6)
                rt_transposes(R)

    @block.scalar
    def _(act):
        def hi_part(n, s, width=UNIT):
            u = 4 * n + s
            act.wait_ge(w_landed[s % 2], 16 * (2 * n + s // 2 + 1))
            if not (isinstance(n, int) and n == 0):
                act.wait_ge(w_used, u - 3)
            act.activation(WH[:, s, 0:width], RAW[:, s % 2, 0:width], ACT.Copy).then_inc(w_hi, 1)

        def hi_next(u):
            if u + 4 < NU:
                hi_part(u // 4 + 1, u % 4, units[u + 4][2] * units[u + 4][4])

        def rstd(dst, k, scale, psum):
            act.wait_ge(norm_ps, k)
            act.activation(dst, psum, ACT.Ln, bias=BT[:, 0:1], scale=scale).then_inc(ln_done, 1)
            act.wait_ge(ln_done, k)
            act.activation(dst, dst, ACT.Exp, scale=-0.5).then_inc(r_ready, 1)

        def tile_t(a, n=S):
            return T[:, a % 4, 4:4 + n]

        def gain_and_square(a, c, gain, sq0, i):
            act.activation(XH[:, c, :], X[:, c, :], ACT.Copy, scale=gain).then_inc(act_done, 1)
            if i >= 2:
                act.wait_ge(ss_done, sq0 + i - 1)
            act.activation(SQ[:, i % 2, :], X[:, c, :], ACT.Square).then_inc(sq_ready, 1)

        for name, r0, k, n in vec_loads:
            act.dma_start(ROWV[n % P:n % P + k, n // P, :],
                          d[name].rearrange("(a b) -> a b", b=P)[r0:r0 + k, :]).then_inc(rows_in, 16)
        act.dma_start(BFG[:, :], d["b_forget"].partition_broadcast(P)).then_inc(consts_in, 16)
        for i, name in enumerate(("lambda_q1", "lambda_k1", "lambda_q2", "lambda_k2")):
            act.dma_start(LAMV[:, i, :], d[name].partition_broadcast(P)).then_inc(consts_in, 16)
        for s in range(2):
            hi_part(0, s)
        act.wait_ge(vec_ready, 1)
        act.wait_ge(dve_made, 1)
        for c in range(KD):
            act.wait_ge(acc_free, c + 1)
            gain_and_square(c, c, vcol("mix_norm_g", c), 0, c)
            if c == 1:
                for s in range(2, 4):
                    hi_part(0, s)

        def v_parts(name, mem, n_pv):
            if n_pv:
                act.wait_ge(pv_ready, n_pv)
            for i in range(8):
                a = TL[name] + i
                act.wait_ge(acc_free, a + 1)
                c0 = 256 * (i // 4)
                act.activation(mem["VH"][:, i % 4, c0:c0 + 256], tile_t(a, 256), ACT.Copy).then_inc(act_done, 1)
                if i % 4 == 3:
                    hi_next(UN[name] + 2 * (i // 4))
                    hi_next(UN[name] + 2 * (i // 4) + 1)

        def qk_part(kind, a, par, i, bias=None):
            buf = FAM[kind]["mem"]["QH" if i % 2 == 0 else "KH"]
            act.wait_ge(acc_free, a + 1)
            if bias is None:
                act.activation(buf[:, par, :], tile_t(a), ACT.Copy).then_inc(act_done, 1)
            else:
                act.activation(buf[:, par, :], tile_t(a), ACT.Identity, bias=bias).then_inc(act_done, 1)

        def na_bias(i, pair):
            return B8[:, pair:pair + 1] if i % 2 == 0 else vcol("b_in_2", 4 + pair)

        rstd(R[:, :], 1, 1.0 / D, PS[:, SCO, :])
        act.wait_ge(wf_in, 16)
        act.activation(WFH[:, :, :], WFR[:, :, :], ACT.Copy).then_inc(wf_split, 1)
        v_parts("v1", M1, 0)
        act.wait_ge(fl_step, 2)
        act.activation(LAM[:, 2:4], LAM[:, 0:2], ACT.Exp).then_inc(fl_act, 1)
        for i in range(2):
            qk_part("fox", TL["fox0"] + i, 0, i)
            hi_next(UN["fox0"] + i)
        act.wait_ge(fl_step, 8)
        act.activation(Z[:, 2, :], Z[:, 1, :], ACT.Exp, scale=-1.0).then_inc(fl_act, 1)
        act.wait_ge(fl_act, 2)
        act.activation(Z[:, 2, :], Z[:, 2, :], ACT.Ln, bias=1.0).then_inc(fl_act, 1)
        act.wait_ge(cum_ps, 1)
        act.wait_ge(cr_dve, 1)
        act.activation(CR[0:8, :], PS[0:8, TRB + 1, :], ACT.Copy).then_inc(cr_act, 1)
        act.activation(CT[32:40, :], PS[32:40, TRB + 1, :], ACT.Copy).then_inc(cr_act, 1)

        def attention(kind):
            f = FAM[kind]
            sc, tr, ready_after = family(kind)
            mem, s0, t0, o0, a0 = f["mem"], f["s0"], f["t0"], f["o0"], TL[f["fill"]]
            n = len(sc)
            norm_q = []
            for i in range(n + 4):
                if i < n:
                    hd, half, qb = sc[i]
                    g = s0 + i
                    k0, k1 = keys_of(kind, qb)
                    w = (k1 - k0) * P
                    act.wait_ge(max_ready, g + 1)
                    if slot_free(kind, i):
                        act.wait_ge(tr_ready, slot_free(kind, i))
                    src = PR[:, g % 4, 0:w] if kind == "na" else PS[:, SCO + g % 2, 0:w]
                    act.activation(PR[:, g % 4, 0:w], src, ACT.Exp, bias=NM[:, g % 4:g % 4 + 1],
                                   accum_out=RS[:, g % 4:g % 4 + 1]).then_inc(exp_ready, 1)
                for fl in filler_done(kind, i):
                    par = parity_of_filler(kind, fl)
                    bias = na_bias(fl, fl // 2 + 1) if kind == "na" else None
                    qk_part(kind, a0 + fl, par, fl, bias)
                    hi_next(UN[f["fill"]] + fl)
                if i - 2 in ready_after:
                    j = ready_after[i - 2]
                    hd, qb = tr[j]
                    g = t0 + j
                    k0, k1 = keys_of(kind, qb)
                    act.wait_ge(tr_ready, g + 1)
                    if o0 + hd > 0:
                        act.wait_ge(pv_ready, o0 + hd)
                    act.activation(mem["PTH"][:, k0:k1, qb * P:(qb + 1) * P],
                                   PS[:, TRB + g % 2, 0:(k1 - k0) * P].rearrange("p (k q) -> p k q", q=P),
                                   ACT.Copy).then_inc(pth_done, 1)
                for hd in norm_q:
                    act.wait_ge(od_ps, hd + 1)
                    act.activation(SQ[:, 1, :], PS[:, OB + (o0 + hd) % 2, :], ACT.Ln, bias=BT[:, 0:1],
                                   scale=1.0 / P).then_inc(od_r, 1)
                    act.wait_ge(od_r, 2 * hd + 1)
                    act.activation(SQ[:, 1, :], SQ[:, 1, :], ACT.Exp, scale=-0.5).then_inc(od_r, 1)
                    act.wait_ge(od_scaled, hd + 1)
                    act.activation(MH[:, 4 + hd, :], OD[:, :], ACT.Copy, scale=GD[:, 0:1]).then_inc(oh_done, 1)
                norm_q = []
                if i - 3 in ready_after and ready_after[i - 3] % 4 == 3:
                    hd = ready_after[i - 3] // 4
                    if kind == "diff":
                        norm_q = [hd]
                    else:
                        act.wait_ge(pv_ready, o0 + hd + 1)
                        r = slice((hd % 2) * HD, (hd % 2) * HD + HD)
                        src = PS[r, OB + (o0 + hd) % 2, :]
                        if kind == "fox":
                            dst = MH[r, hd // 2, :]
                        else:
                            dst, src = grid3(NAH[r, hd // 2, :], "natural"), natural_of(src)
                        act.activation(dst, src, ACT.Copy).then_inc(oh_done, 1)

        attention("fox")
        v_parts("v2", M1, 8)
        attention("diff")

        def residual_tiles(name, gain, sq0, per_tile_units):
            for c in range(KD):
                for u in per_tile_units(c):
                    hi_next(u)
                act.wait_ge(acc_free, TL[name] + c + 1)
                gain_and_square(TL[name] + c, c, vcol(gain, c), sq0, c)

        residual_tiles("out1", "ffn_norm_g", 8, lambda c: [UN["out1"] + c])
        def swiglu_group(i):
            for j in range(2):
                a, b = 2 * j, 2 * j + 1
                t = 4 * i + TL["ffn1"]
                hi_part(i + UN["ffn1"] // 4 + 1, a)
                act.wait_ge(acc_free, t + a + 1)
                act.activation(T[:, a, 4:4 + S], T[:, a, 4:4 + S], ACT.Silu).then_inc(act_done, 1)
                hi_part(i + UN["ffn1"] // 4 + 1, b)
                act.wait_ge(prod, 2 * i + j + 1)
                act.activation(HH[:, bass.ds(2 * i + j, 1), :], T[:, b, 4:4 + S], ACT.Copy).then_inc(act_done, 1)

        def swiglu_last(i):
            for j in range(2):
                a, b = 2 * j, 2 * j + 1
                t = 4 * i + TL["ffn1"]
                hi_next(UN["ffn1"] + 4 * i + a)
                act.wait_ge(acc_free, t + a + 1)
                act.activation(T[:, a, 4:4 + S], T[:, a, 4:4 + S], ACT.Silu).then_inc(act_done, 1)
                hi_next(UN["ffn1"] + 4 * i + b)
                act.wait_ge(prod, 2 * i + j + 1)
                act.activation(HH[:, 2 * i + j, :], T[:, b, 4:4 + S], ACT.Copy).then_inc(act_done, 1)

        rstd(R[:, :], 2, 1.0 / D, PS[:, SCO, :])
        with act.Fori(0, KF // 2 - 1) as i:
            swiglu_group(i)
        swiglu_last(KF // 2 - 1)
        for c in range(KD):
            for j in range(3):
                hi_next(UN["down1"] + 3 * c + j)
            a = TL["down1"] + c
            act.wait_ge(acc_free, a + 1)
            if c >= 4:
                act.wait_ge(low_done, L0["down1"] + c - 3)
            act.activation(grid3(tile_t(a), "perm"), perm_of(X[:, c, :]), ACT.Copy,
                           scale=GG[:, c:c + 1]).then_inc(xg_ready, 1)
            act.wait_ge(xg_ready, c + 1)
            act.activation(XH[:, c, :], tile_t(a), ACT.Copy).then_inc(act_done, 1)
            act.wait_ge(ss_done, 16 + 2 * c)
            act.activation(SQ[:, 0, :], X[:, c, :], ACT.Square).then_inc(sq_ready, 1)
            act.activation(SQ[:, 1, :], X[:, c, :], ACT.Square, scale=vcol("final_norm_g", c)).then_inc(sq_ready, 1)

        rstd(R[:, :], 3, 1.0 / D, PS[:, SCO, :])
        act.wait_ge(r_mix, 2)
        act.activation(RP[:, :], SQ[:, 0, :], ACT.Ln, bias=BT[:, 0:1], scale=1.0 / D).then_inc(ln_done, 1)
        act.wait_ge(ln_done, 4)
        act.activation(RP[:, :], RP[:, :], ACT.Exp, scale=-0.5).then_inc(r_ready, 1)
        for i in range(8):
            a = TL["cab"] + i
            hi_next(UN["cab"] + i)
            act.wait_ge(acc_free, a + 1)
            func = ACT.Sigmoid if i % 2 else ACT.Identity
            act.activation(tile_t(a), tile_t(a), func,
                           bias=vcol("b_in_2", (12 if i % 2 == 0 else 16) + i // 2)).then_inc(act_done, 1)
        v_parts("v3", M2, 0)
        for i in range(2):
            qk_part("na", TL["na0"] + i, 0, i, na_bias(i, 0))
            hi_next(UN["na0"] + i)
        attention("na")
        with act.Fori(0, 4) as i:
            for s in range(4):
                hi_part(i + UN["gates"] // 4 + 1, s)
                act.wait_ge(acc_free, 4 * i + s + TL["gates"] + 1)
                act.activation(SG[:, bass.ds(4 * i + s, 1), :], T[:, s, 4:4 + S], ACT.Sigmoid,
                               bias=VEC[:, bass.ds(4 * i + s + vec_at["b_in_2"] + 20, 1)]).then_inc(act_done, 1)
        for c in range(4):
            hi_next(UN["na_out"] + c)
            if c == 1:
                for k in range(4):
                    act.wait_ge(ln_d, k + 1)
                    if k >= 2:
                        act.wait_ge(ss_done, 32 + k - 1)
                    act.activation(SQ[:, k % 2, :], Y[:, k, :], ACT.Square).then_inc(sq_ready, 1)
        act.wait_ge(ln_ps, 2)
        act.activation(R[:, :], PS[:, SCO + 1, :], ACT.Ln, bias=BT[:, 0:1], scale=1.0 / S).then_inc(ln_r, 1)
        act.wait_ge(ln_r, 1)
        act.activation(R[:, :], R[:, :], ACT.Exp, scale=-0.5).then_inc(ln_r, 1)
        for k in range(4):
            act.wait_ge(ln_n, k + 1)
            act.activation(Y[:, k, :], Y[:, k, :], ACT.Silu, scale=vcol("conv_ln_g_2", k),
                           bias=vcol("conv_ln_b_2", k)).then_inc(silu_done, 1)
            act.wait_ge(silu_done, k + 1)
            act.activation(CH[:, k, :], Y[:, k, :], ACT.Copy).then_inc(ch_done, 1)
        for c in range(8):
            if c % 2:
                hi_next(UN["conv_out"] + c // 2)
            act.wait_ge(merged, c + 1)
            act.activation(MH2[:, c, :], tile_t(TL["conv_out"] + c), ACT.Copy).then_inc(act_done, 1)
        residual_tiles("out2", "norm2_g_2", 36, lambda c: [UN["out2"] + c])
        rstd(R[:, :], 5, 1.0 / D, PS[:, SCO, :])

        def geglu_group(i, static):
            for j in range(2):
                for v in range(2):
                    s = 2 * j + v
                    if static:
                        hi_next(UN["ffn2"] + 4 * i + s)
                        wcol = vcol("ffn_dw_w_2", 44 + 22 * v + 2 * i + j)
                        bcol = vcol("ffn_dw_b_2", 22 * v + 2 * i + j)
                    else:
                        hi_part(i + UN["ffn2"] // 4 + 1, s)
                        wcol = VEC[:, bass.ds(2 * i + j + vec_at["ffn_dw_w_2"] + 44 + 22 * v, 1)]
                        bcol = VEC[:, bass.ds(2 * i + j + vec_at["ffn_dw_b_2"] + 22 * v, 1)]
                    act.wait_ge(acc_free, 4 * i + s + TL["ffn2"] + 1)
                    if not (static and i == 0):
                        act.wait_ge(low_done, 2 * i + j + L0["ffn2"] - 1)
                    act.activation(CZ[j][v][:, :], T[:, s, 4:4 + S], ACT.Identity, scale=wcol, bias=bcol).then_inc(cz_mid, 1)
                act.wait_ge(cz_taps, 4 * i + 2 * j + 1)
                act.activation(CZ[j][0][:, :], CZ[j][0][:, :], ACT.Gelu).then_inc(gelu_done, 1)
                act.wait_ge(glu_ready, 2 * i + j + 1)
                dst = HH[:, 2 * i + j, :] if static else HH[:, bass.ds(2 * i + j, 1), :]
                act.activation(dst, CZ[j][1][:, :], ACT.Copy).then_inc(hid_hi, 1)

        geglu_group(0, True)
        with act.Fori(1, KF // 2 - 1) as i:
            geglu_group(i, False)
        geglu_group(KF // 2 - 1, True)
        for c in range(KD):
            for j in range(3):
                hi_next(UN["down2"] + 3 * c + j)
            act.wait_ge(acc_free, TL["down2"] + c + 1)
            if c >= 2:
                act.wait_ge(ss_done, 44 + c - 1)
            act.activation(SQ[:, c % 2, :], X[:, c, :], ACT.Square).then_inc(sq_ready, 1)
        rstd(R[:, :], 6, 1.0 / D, PS[:, SCO, :])

    @block.vector
    def _(dve):
        made = [0]

        def step(ins):
            made[0] += 1
            ins.then_inc(dve_made, 1)
            dve.wait_ge(dve_made, made[0])

        def tile_t(a, n=S):
            return T[:, a % 4, 4:4 + n]

        def ps(a, n=S):
            return PS[:, ACC + a % 2, 0:n]

        def tile_ready(name, i):
            if name == "init":
                dve.wait_ge(part_ready, i + 1)
            elif name[0] == "v":
                half, t = i // 4, i % 4
                if t < 3:
                    dve.wait_ge(part_ready, PT0[name] + 3 * half + t + 1)
                else:
                    dve.wait_ge(w_used, UN[name] + 2 * half + 2)
            elif name in ("na_out", "conv_out"):
                if i % 2 == 0:
                    dve.wait_ge(part_ready, PT0[name] + i // 2 + 1)
                else:
                    dve.wait_ge(w_used, UN[name] + i // 2 + 1)
            elif name[:4] == "down":
                dve.wait_ge(w_used, UN[name] + 3 * i + 3)
            else:
                dve.wait_ge(w_used, UN[name] + i + 1)

        def slots_drained(name):
            dve.wait_ge(act_done, H0[name])
            dve.wait_ge(low_done, L0[name])

        step(dve.memset(BT[:, :], EPS))
        step(dve.memset(T[:, :, 0:4], 0.0))
        step(dve.memset(T[:, :, 516:520], 0.0))
        step(dve.memset(CR[:, :].bitcast(F32), 0.0))
        dve.wait_ge(pool_made, 18)
        step(dve.tensor_copy(IDB[:, :], IDF[:, :]))
        step(dve.tensor_copy(CMB[:, :], CST[:, :]))
        step(dve.tensor_copy(SEL[:, :], SELF[:, :]))
        step(dve.tensor_copy(CR[64:65, :], POS[64:65, :]))

        def add_square(k, i, which=0, slot=0):
            dve.wait_ge(sq_ready, k)
            if i == 0:
                dve.tensor_copy(SS[:, which, :], SQ[:, slot, :]).then_inc(ss_done, 1)
            else:
                dve.wait_ge(ss_done, k - 1)
                dve.tensor_tensor(SS[:, which, :], SS[:, which, :], SQ[:, slot, :], ALU.add).then_inc(ss_done, 1)

        def low_of_gain(name, gain, c):
            dve.wait_ge(act_done, H0[name] + c + 1)
            dve.scalar_tensor_tensor(out=XL[:, c, :], in0=X[:, c, :], scalar=vcol(gain, c), in1=XH[:, c, :].bitcast(F32),
                                     op0=ALU.mult, op1=ALU.subtract).then_inc(low_done, 1)

        for c in range(KD):
            tile_ready("init", c)
            dve.tensor_copy(X[:, c, :], ps(c)).then_inc(acc_free, 1)
            if c == 0:
                dve.wait_ge(vec_t, 1)
                dve.tensor_copy(VEC[:, :], PS[:, OB, 0:n_vec]).then_inc(vec_ready, 1)
                dve.wait_ge(vec_ready, 1)
            else:
                low_of_gain("init", "mix_norm_g", c - 1)
                add_square(c, c - 1, 0, (c - 1) % 2)
        low_of_gain("init", "mix_norm_g", KD - 1)
        add_square(KD, KD - 1, 0, 1)
        dve.wait_ge(wf_split, 1)
        dve.tensor_tensor(WFL[:, :, :], WFR[:, :, :], WFH[:, :, :].bitcast(F32), ALU.subtract).then_inc(wf_split, 1)
        dve.wait_ge(consts_in, 16 * 5)
        for i in range(2):
            dve.tensor_tensor_reduce(out=LAMV[:, 2 * i, :], in0=LAMV[:, 2 * i, :], in1=LAMV[:, 2 * i + 1, :], scale=1.0,
                                     scalar=0.0, op0=ALU.mult, op1=ALU.add, accum_out=LAM[:, i:i + 1]).then_inc(fl_step, 1)
        step(dve.tensor_tensor(GG[:, :], vcol("final_norm_g", 0, 8), vcol("norm1_g_2", 0, 8), ALU.mult))
        step(dve.tensor_scalar(B8[:, :], vcol("b_in_2", 0, 4), 0.125, None, ALU.mult))
        step(dve.tensor_scalar(GD[:, :], vcol("diff_norm_g", 0), 1.0 - LAM_INIT, None, ALU.mult))
        step(dve.tensor_copy(TRI[:, :], STG[:, :]))
        step(dve.memset(LFH[:, :, :].bitcast(F32), 0.0))
        step(dve.memset(LFL[:, :, :].bitcast(F32), 0.0))
        step(dve.tensor_scalar(QI[:, 1:2], QI[:, 0:1], 7, None, ALU.bitwise_and))
        step(dve.tensor_copy(QC[:, :], QI[:, 1:2]))
        step(dve.tensor_scalar(QC[64:128, :], QC[64:128, :], 8.0, None, ALU.add))
        step(dve.tensor_scalar(MKS[:, 0, :], KC[:, :], QC[:, 0:1], None, ALU.subtract))

        def clause(dst, src, op, bound):
            step(dve.tensor_scalar(MKS[:, dst, :], src, bound, None, op))

        def combine(dst, other, op):
            step(dve.tensor_tensor(MKS[:, dst, :], MKS[:, dst, :], MKS[:, other, :], op))

        def as_mask(m):
            step(dve.tensor_scalar(NMB[:, m, :], MKS[:, 1, :], -NEG, NEG, ALU.mult, ALU.add))

        diff_, keyc = MKS[:, 0, :], KC[:, :]
        clause(1, diff_, ALU.is_ge, 8.0)
        clause(2, diff_, ALU.is_le, 23.0)
        combine(1, 2, ALU.mult)
        as_mask(0)
        clause(1, diff_, ALU.is_ge, -8.0)
        clause(2, diff_, ALU.is_le, 7.0)
        clause(3, keyc, ALU.is_le, 15.0)
        combine(2, 3, ALU.max)
        combine(1, 2, ALU.mult)
        as_mask(1)
        clause(1, diff_, ALU.is_ge, 8.0)
        clause(3, keyc, ALU.is_ge, 16.0)
        combine(1, 3, ALU.max)
        clause(2, diff_, ALU.is_le, 23.0)
        combine(1, 2, ALU.mult)
        as_mask(2)

        def rt_copy(k):
            dve.wait_ge(rt_ps, k)
            dve.tensor_copy(RT[:, :], PS[:, SCO + 1, :].rearrange("p (t q) -> p t q", q=P)[:, :, 0]).then_inc(rt_ready, 1)
            dve.wait_ge(rt_ready, k)

        def v_phase(name, mem, bias, extra=None):
            slots_drained(name)
            for i in range(8 + 1):
                if i < 8:
                    a, c0, t = TL[name] + i, 256 * (i // 4), i % 4
                    tile_ready(name, i)
                    if i >= 4:
                        dve.wait_ge(low_done, L0[name] + i - 3)
                    if bias:
                        dve.scalar_tensor_tensor(out=tile_t(a, 256), in0=ps(a, 256), scalar=RT[:, t:t + 1],
                                                 in1=BVB[:, c0:c0 + 256], op0=ALU.mult, op1=ALU.add).then_inc(acc_free, 1)
                    else:
                        dve.tensor_scalar(tile_t(a, 256), ps(a, 256), RT[:, t:t + 1], None, ALU.mult).then_inc(acc_free, 1)
                if i >= 1:
                    a, c0, t = TL[name] + i - 1, 256 * ((i - 1) // 4), (i - 1) % 4
                    dve.wait_ge(act_done, H0[name] + i)
                    dve.tensor_tensor(mem["VL"][:, t, c0:c0 + 256], tile_t(a, 256), mem["VH"][:, t, c0:c0 + 256].bitcast(F32),
                                      ALU.subtract).then_inc(low_done, 1)
                if extra:
                    extra(i)

        def qk_take(name, i, r):
            a = TL[name] + i
            tile_ready(name, i)
            if i >= 4:
                dve.wait_ge(low_done, L0[name] + i - 3)
            if i % 2 == 0:
                ins = dve.scalar_tensor_tensor(out=tile_t(a), in0=ps(a), scalar=HD ** -0.5, in1=r, op0=ALU.mult, op1=ALU.mult)
            else:
                ins = dve.tensor_tensor(tile_t(a), ps(a), r, ALU.mult)
            ins.then_inc(acc_free, 1)

        def qk_low(name, i, par, mem, pair=None):
            a = TL[name] + i
            hi, lo = (mem["QH"], mem["QL"]) if i % 2 == 0 else (mem["KH"], mem["KL"])
            dve.wait_ge(act_done, H0[name] + i + 1)
            if pair is None:
                ins = dve.tensor_tensor(lo[:, par, :], tile_t(a), hi[:, par, :].bitcast(F32), ALU.subtract)
            else:
                b = B8[:, pair:pair + 1] if i % 2 == 0 else vcol("b_in_2", 4 + pair)
                ins = dve.scalar_tensor_tensor(out=lo[:, par, :], in0=tile_t(a), scalar=b, in1=hi[:, par, :].bitcast(F32),
                                               op0=ALU.add, op1=ALU.subtract)
            ins.then_inc(low_done, 1)

        def log_forget(i):
            if i == 1:
                dve.wait_ge(fl_ps, 1)
                for t in range(TC):
                    dve.scalar_tensor_tensor(out=Z[:, 0, 8 * t:8 * t + 8], in0=PS[:, TRB, 8 * t:8 * t + 8],
                                             scalar=RT[:, t:t + 1], in1=BFG[:, :], op0=ALU.mult,
                                             op1=ALU.add).then_inc(fl_step, 1)
                dve.wait_ge(fl_step, 6)
                dve.scalar_tensor_tensor(out=Z[:, 1, :], in0=Z[:, 0, :], scalar=-1.0, in1=Z[:, 0, :], op0=ALU.mult,
                                         op1=ALU.max).then_inc(fl_step, 1)
                dve.tensor_scalar(Z[:, 3, :], Z[:, 0, :], 0.0, None, ALU.min).then_inc(fl_step, 1)

        rt_copy(1)
        v_phase("v1", M1, False, log_forget)
        dve.wait_ge(fl_act, 1)
        dve.tensor_tensor(LAM[:, 4:5], LAM[:, 3:4], LAM[:, 2:3], ALU.subtract).then_inc(lam_ready, 1)
        dve.wait_ge(lam_ready, 1)
        dve.tensor_scalar(LAM[:, 5:6], LAM[:, 4:5], LAM_INIT, None, ALU.subtract).then_inc(lam_ready, 1)
        slots_drained("fox0")
        for i in range(2):
            qk_take("fox0", i, R[:, :])
            qk_low("fox0", i, 0, M1)
        dve.wait_ge(fl_act, 3)
        dve.tensor_tensor(Z[:, 2, :], Z[:, 2, :], Z[:, 3, :], ALU.subtract).then_inc(fl_step, 1)
        dve.wait_ge(fl_step, 9)
        nlf = Z[:, 2, :].rearrange("p (t h) -> p t h", h=8)
        for i, c in enumerate((0, 32)):
            dve.tensor_copy(LFH[:, :, c:c + 8], nlf).then_inc(fl_step, 1)
            dve.wait_ge(fl_step, 10 + i)
            dve.tensor_tensor(LFL[:, :, c:c + 8], nlf, LFH[:, :, c:c + 8].bitcast(F32), ALU.subtract).then_inc(lf_ready, 1)
        dve.wait_ge(cum_ps, 1)
        dve.tensor_copy(RI[:, 0:1], BT[:, :]).then_inc(cr_dve, 1)
        dve.wait_ge(cr_act, 2)
        dve.tensor_tensor(CR[32:40, :], PS[32:40, TRB + 1, :], CT[32:40, :].bitcast(F32), ALU.subtract).then_inc(cr_dve, 1)
        dve.wait_ge(rpb_out, 16 * 8)

        def attention(kind, r):
            f = FAM[kind]
            sc, tr, ready_after = family(kind)
            mem, s0, t0, o0, name = f["mem"], f["s0"], f["t0"], f["o0"], f["fill"]
            n = len(sc)
            late = []
            slots_drained(name)
            for i in range(n + 4):
                if i < n:
                    hd, half, qb = sc[i]
                    g = s0 + i
                    k0, k1 = keys_of(kind, qb)
                    w = (k1 - k0) * P
                    dve.wait_ge(sc_ready, g + 1)
                    src = PS[:, SCO + g % 2, 0:w]
                    if kind == "na":
                        if slot_free(kind, i):
                            dve.wait_ge(tr_ready, slot_free(kind, i))
                        if i == 0:
                            dve.wait_ge(bias_in, 16 * 16)
                        g0 = 2 if qb == 0 else 0
                        bias = BN[:, :, hd, 8 * g0:8 * g0 + w // ROWS].rearrange("p r (g c) -> p g r c", c=8)
                        view = lambda ap: ap.rearrange("p (g r c) -> p g r c", r=ROWS, c=8)
                        dve.tensor_tensor(view(PR[:, g % 4, 0:w]), view(src), bias, ALU.add).then_inc(biased, 1)
                        dve.wait_ge(biased, i + 1)
                        src = PR[:, g % 4, 0:w]
                    if g >= 4:
                        dve.wait_ge(exp_ready, g - 3)
                    dve.tensor_reduce(NM[:, g % 4:g % 4 + 1], src, AX, ALU.max, negate=True).then_inc(max_ready, 1)
                if 1 <= i <= n:
                    g = s0 + i - 1
                    hd, half, qb = sc[i - 1]
                    k0, k1 = keys_of(kind, qb)
                    w = (k1 - k0) * P
                    dve.wait_ge(exp_ready, g + 1)
                    if g >= 4:
                        dve.wait_ge(p_ready, t0 if i - 1 < 4 else slot_free(kind, i - 1))
                    dve.reciprocal(RI[:, g % 4:g % 4 + 1], RS[:, g % 4:g % 4 + 1]).then_inc(rinv_done, 1)
                    ri = RI[:, g % 4:g % 4 + 1]
                    if kind == "diff" and half == 1:
                        dve.wait_ge(rinv_done, g + 1)
                        dve.tensor_tensor(ri, ri, LAM[:, 5:6], ALU.mult).then_inc(lam_ready, 1)
                        dve.wait_ge(lam_ready, 2 + i // 2)
                        dve.wait_ge(p_half, i // 2)
                        dve.scalar_tensor_tensor(out=PR[:, (g - 1) % 4, 0:w], in0=PR[:, g % 4, 0:w], scalar=ri,
                                                 in1=PR[:, (g - 1) % 4, 0:w], op0=ALU.mult,
                                                 op1=ALU.add).then_inc(p_ready, 1)
                    else:
                        dve.wait_ge(rinv_done, g + 1)
                        dve.tensor_scalar(PR[:, g % 4, 0:w], PR[:, g % 4, 0:w], ri, None,
                                          ALU.mult).then_inc(p_half if kind == "diff" else p_ready, 1)
                for fl in filler_done(kind, i):
                    qk_take(name, fl, r)
                if i - 2 in ready_after:
                    j = ready_after[i - 2]
                    hd, qb = tr[j]
                    g = t0 + j
                    k0, k1 = keys_of(kind, qb)
                    dve.wait_ge(pth_done, g + 1)
                    q = slice(qb * P, (qb + 1) * P)
                    dve.tensor_tensor(mem["PTL"][:, k0:k1, q],
                                      PS[:, TRB + g % 2, 0:(k1 - k0) * P].rearrange("p (k q) -> p k q", q=P),
                                      mem["PTH"][:, k0:k1, q].bitcast(F32), ALU.subtract).then_inc(ptl_done, 1)
                for fl in filler_done(kind, i):
                    qk_low(name, fl, parity_of_filler(kind, fl), mem, fl // 2 + 1 if kind == "na" else None)
                for hd in late:
                    dve.wait_ge(od_r, 2 * hd + 2)
                    dve.tensor_tensor(OD[:, :], OD[:, :], SQ[:, 1, :], ALU.mult).then_inc(od_scaled, 1)
                    dve.wait_ge(oh_done, o0 + hd + 1)
                    dve.scalar_tensor_tensor(out=ML[:, 4 + hd, :], in0=OD[:, :], scalar=GD[:, 0:1],
                                             in1=MH[:, 4 + hd, :].bitcast(F32), op0=ALU.mult,
                                             op1=ALU.subtract).then_inc(o_free, 1)
                late = []
                if i - 3 in ready_after and ready_after[i - 3] % 4 == 3:
                    hd = ready_after[i - 3] // 4
                    bank = PS[:, OB + (o0 + hd) % 2, :]
                    if kind == "diff":
                        dve.wait_ge(pv_ready, o0 + hd + 1)
                        if hd:
                            dve.wait_ge(o_free, o0 + hd)
                        dve.tensor_copy(OD[:, :], bank).then_inc(od_copy, 1)
                        dve.wait_ge(od_copy, hd + 1)
                        dve.tensor_tensor(SQ[:, 0, :], OD[:, :], OD[:, :], ALU.mult).then_inc(od_sq, 1)
                        late = [hd]
                    else:
                        dve.wait_ge(oh_done, o0 + hd + 1)
                        rr = slice((hd % 2) * HD, (hd % 2) * HD + HD)
                        if kind == "fox":
                            dve.tensor_tensor(ML[rr, hd // 2, :], bank[rr, :], MH[rr, hd // 2, :].bitcast(F32),
                                              ALU.subtract).then_inc(o_free, 1)
                        else:
                            dve.tensor_tensor(grid3(NAL[rr, hd // 2, :], "natural"), natural_of(bank[rr, :]),
                                              grid3(NAH[rr, hd // 2, :].bitcast(F32), "natural"),
                                              ALU.subtract).then_inc(o_free, 1)

        attention("fox", R[:, :])
        v_phase("v2", M1, False)
        attention("diff", R[:, :])

        def residual(name, gain, sq0):
            for c in range(KD + 1):
                if c < KD:
                    tile_ready(name, c)
                    dve.tensor_tensor(X[:, c, :], ps(TL[name] + c), X[:, c, :], ALU.add).then_inc(acc_free, 1)
                if c:
                    low_of_gain(name, gain, c - 1)
                    add_square(sq0 + c, c - 1, 0, (c - 1) % 2)

        residual("out1", "ffn_norm_g", 8)

        def swiglu_low(q, dst, src, b):
            dve.wait_ge(act_done, 2 * q + 2 + H0["ffn1"])
            dve.tensor_tensor(dst, T[:, b, 4:4 + S], src.bitcast(F32), ALU.subtract).then_inc(low_done, 1)

        def swiglu_pair(i, j, first):
            q = 2 * i + j
            for v in range(2):
                s = 2 * j + v
                dve.wait_ge(w_used, 4 * i + s + UN["ffn1"] + 1)
                if not first:
                    dve.wait_ge(low_done, q - 1 + L0["ffn1"])
                dve.tensor_tensor(T[:, s, 4:4 + S], PS[:, ACC + s % 2, :], R[:, :], ALU.mult).then_inc(acc_free, 1)
                if v == 0 and not (first and j == 0):
                    if isinstance(i, int):
                        swiglu_low(q - 1, HL[:, q - 1, :], HH[:, q - 1, :], (s - 1) % 4)
                    else:
                        swiglu_low(q - 1, HL[:, bass.ds(q - 1, 1), :], HH[:, bass.ds(q - 1, 1), :], (s - 1) % 4)
            dve.wait_ge(act_done, 4 * i + 2 * j + 1 + H0["ffn1"])
            dve.wait_ge(acc_free, 4 * i + 2 * j + 2 + TL["ffn1"])
            dve.tensor_tensor(T[:, 2 * j + 1, 4:4 + S], T[:, 2 * j + 1, 4:4 + S], T[:, 2 * j, 4:4 + S],
                              ALU.mult).then_inc(prod, 1)

        dve.wait_ge(r_ready, 2)
        for j in range(2):
            swiglu_pair(0, j, True)
        with dve.Fori(1, KF // 2) as i:
            for j in range(2):
                swiglu_pair(i, j, False)
        swiglu_low(KF - 1, HL[:, KF - 1, :], HH[:, KF - 1, :], 3)

        for c in range(KD + 1):
            if c < KD:
                tile_ready("down1", c)
                dve.tensor_tensor(X[:, c, :], ps(TL["down1"] + c), X[:, c, :], ALU.add).then_inc(acc_free, 1)
            if c:
                k = c - 1
                dve.wait_ge(act_done, H0["down1"] + k + 1)
                dve.tensor_tensor(XL[:, k, :], tile_t(TL["down1"] + k), XH[:, k, :].bitcast(F32),
                                  ALU.subtract).then_inc(low_done, 1)
                add_square(16 + 2 * k + 1, k, 0, 0)
                add_square(16 + 2 * k + 2, k, 1, 1)
        dve.wait_ge(r_ready, 3)
        dve.wait_ge(norm_ps, 4)
        dve.tensor_tensor(SQ[:, 0, :], PS[:, SCO + 1, :], R[:, :], ALU.mult).then_inc(r_mix, 1)
        dve.wait_ge(r_mix, 1)
        dve.tensor_tensor(SQ[:, 0, :], SQ[:, 0, :], R[:, :], ALU.mult).then_inc(r_mix, 1)
        dve.wait_ge(r_ready, 4)
        RN2 = SS[:, 1, :]
        dve.tensor_tensor(RN2, R[:, :], RP[:, :], ALU.mult).then_inc(r_mix, 1)
        dve.wait_ge(r_mix, 3)
        dve.tensor_copy(grid3(RP[:, :], "perm"), perm_of(RN2)).then_inc(r_mix, 1)

        slots_drained("cab")
        step(dve.memset(U[:, :, 0:UO], 0.0))
        step(dve.memset(U[:, :, UO + S:UW], 0.0))
        for part in ("PTH", "PTL"):
            step(dve.memset(M2[part][:, 1, 3 * P:S].bitcast(F32), 0.0))
        for i in range(8 + 1):
            if i < 8:
                a = TL["cab"] + i
                tile_ready("cab", i)
                if i >= 4:
                    dve.wait_ge(low_done, L0["cab"] + (i - 4) // 2 + 1)
                dve.tensor_tensor(grid3(tile_t(a), "natural"), natural_of(ps(a)), grid3(RN2, "natural"),
                                  ALU.mult).then_inc(acc_free, 1)
                dve.scalar_tensor_tensor(out=X[:, i, :], in0=X[:, i, :], scalar=vcol("final_norm_g", i), in1=R[:, :],
                                         op0=ALU.mult, op1=ALU.mult).then_inc(x1_done, 1)
            if i >= 2 and i % 2 == 0:
                c, a = i // 2 - 1, TL["cab"] + i - 1
                dve.wait_ge(act_done, H0["cab"] + i)
                dve.tensor_tensor(U[:, c, UO:UO + S], tile_t(a - 1), tile_t(a), ALU.mult).then_inc(low_done, 1)

        rt_copy(2)
        dve.wait_ge(bv_in, 16)
        v_phase("v3", M2, True)
        slots_drained("na0")
        for i in range(2):
            qk_take("na0", i, RP[:, :])
            qk_low("na0", i, 0, M2, 0)
        attention("na", RP[:, :])

        taps = [(t, c) for t in range(TAPS) for c in range(4)]

        def conv_tap(k):
            t, c = taps[k]
            src = U[:, c, UO - TAPS // 2 + t:UO - TAPS // 2 + t + S]
            w = vcol("conv_dw_w_2", 4 * t + c)
            if t == 0:
                dve.tensor_scalar(Y[:, c, :], src, w, vcol("conv_dw_b_2", c), ALU.mult, ALU.add).then_inc(conv_done, 1)
            else:
                dve.wait_ge(conv_done, k - 3)
                dve.scalar_tensor_tensor(out=Y[:, c, :], in0=src, scalar=w, in1=Y[:, c, :], op0=ALU.mult,
                                         op1=ALU.add).then_inc(conv_done, 1)

        slots_drained("gates")
        for i in range(16):
            a = TL["gates"] + i
            tile_ready("gates", i)
            if i >= 4:
                dve.wait_ge(act_done, H0["gates"] + i - 3)
            dve.tensor_tensor(grid3(tile_t(a), "natural"), natural_of(ps(a)), grid3(RN2, "natural"),
                              ALU.mult).then_inc(acc_free, 1)
            for k in range(len(taps) * i // 16, len(taps) * (i + 1) // 16):
                conv_tap(k)
        dve.wait_ge(conv_done, len(taps))
        dve.tensor_tensor(SS[:, 0, :], Y[:, 0, :], Y[:, 1, :], ALU.add).then_inc(ln_sum, 1)
        for k in (2, 3):
            dve.wait_ge(ln_sum, k - 1)
            dve.tensor_tensor(SS[:, 0, :], SS[:, 0, :], Y[:, k, :], ALU.add).then_inc(ln_sum, 1)

        def na_out_take(c):
            tile_ready("na_out", c)
            if c == 0:
                dve.wait_ge(act_done, H0["na_out"])
            dve.tensor_tensor(SG[:, c, :], ps(TL["na_out"] + c), SG[:, c, :], ALU.mult).then_inc(acc_free, 1)

        na_out_take(0)
        na_out_take(1)
        dve.wait_ge(ln_ps, 1)
        for k in range(4):
            dve.scalar_tensor_tensor(out=Y[:, k, :], in0=PS[:, SCO, :], scalar=-1.0 / S, in1=Y[:, k, :], op0=ALU.mult,
                                     op1=ALU.add).then_inc(ln_d, 1)
        na_out_take(2)
        na_out_take(3)
        for k in range(4):
            add_square(32 + k + 1, k, 0, k % 2)
        na_out_take(4)
        na_out_take(5)
        dve.wait_ge(ln_r, 2)
        for k in range(4):
            dve.tensor_tensor(Y[:, k, :], Y[:, k, :], R[:, :], ALU.mult).then_inc(ln_n, 1)
        na_out_take(6)
        na_out_take(7)
        for k in range(4):
            dve.wait_ge(ch_done, k + 1)
            dve.tensor_tensor(CL[:, k, :], Y[:, k, :], CH[:, k, :].bitcast(F32), ALU.subtract).then_inc(cl_done, 1)
        for c in range(8 + 1):
            if c < 8:
                a = TL["conv_out"] + c
                tile_ready("conv_out", c)
                if c >= 4:
                    dve.wait_ge(low_done, L0["conv_out"] + c - 3)
                dve.tensor_tensor(tile_t(a), ps(a), SG[:, 8 + c, :], ALU.mult).then_inc(acc_free, 1)
                dve.wait_ge(acc_free, a + 1)
                dve.tensor_tensor(tile_t(a), tile_t(a), SG[:, c, :], ALU.add).then_inc(merged, 1)
            if c:
                a = TL["conv_out"] + c - 1
                dve.wait_ge(act_done, H0["conv_out"] + c)
                dve.tensor_tensor(ML2[:, c - 1, :], tile_t(a), MH2[:, c - 1, :].bitcast(F32),
                                  ALU.subtract).then_inc(low_done, 1)
        dve.wait_ge(x1_done, 8)
        residual("out2", "norm2_g_2", 36)

        def geglu_low(q, dst, src, j):
            dve.wait_ge(hid_hi, q + 1)
            dve.tensor_tensor(dst, CZ[j][1][:, :], src.bitcast(F32), ALU.subtract).then_inc(low_done, 1)

        def geglu_pair(i, j, first):
            q = 2 * i + j
            static = isinstance(i, int)
            for v in range(2):
                s = 2 * j + v
                dve.wait_ge(w_used, 4 * i + s + UN["ffn2"] + 1)
                if not first:
                    dve.wait_ge(cz_taps, 4 * i + s - 3)
                dve.tensor_tensor(T[:, s, 4:4 + S], PS[:, ACC + s % 2, :], R[:, :], ALU.mult).then_inc(acc_free, 1)
                if v == 0 and not (first and j == 0):
                    if static:
                        geglu_low(q - 1, HL[:, q - 1, :], HH[:, q - 1, :], 1 - j)
                    else:
                        geglu_low(q - 1, HL[:, bass.ds(q - 1, 1), :], HH[:, bass.ds(q - 1, 1), :], 1 - j)
                z = CZ[j][v][:, :]

                def w(tap):
                    c = 2 * i + (j + vec_at["ffn_dw_w_2"] + 2 * KF * tap + KF * v)
                    return VEC[:, c:c + 1] if static else VEC[:, bass.ds(c, 1)]

                dve.wait_ge(cz_mid, 4 * i + s + 1)
                dve.scalar_tensor_tensor(out=z, in0=T[:, s, 3:3 + S], scalar=w(0), in1=z, op0=ALU.mult,
                                         op1=ALU.add).then_inc(cz_tap, 1)
                dve.wait_ge(cz_tap, 4 * i + s + 1)
                dve.scalar_tensor_tensor(out=z, in0=T[:, s, 5:5 + S], scalar=w(2), in1=z, op0=ALU.mult,
                                         op1=ALU.add).then_inc(cz_taps, 1)
            dve.wait_ge(gelu_done, q + 1)
            dve.wait_ge(cz_taps, 4 * i + 2 * j + 2)
            dve.tensor_tensor(CZ[j][1][:, :], CZ[j][1][:, :], CZ[j][0][:, :], ALU.mult).then_inc(glu_ready, 1)

        dve.wait_ge(r_ready, 5)
        slots_drained("ffn2")
        for j in range(2):
            geglu_pair(0, j, True)
        with dve.Fori(1, KF // 2) as i:
            for j in range(2):
                geglu_pair(i, j, False)
        geglu_low(KF - 1, HL[:, KF - 1, :], HH[:, KF - 1, :], 1)

        for c in range(KD + 1):
            if c < KD:
                a = TL["down2"] + c
                tile_ready("down2", c)
                dve.tensor_tensor(X[:, c, :], ps(a), X[:, c, :], ALU.add).then_inc(acc_free, 1)
                dve.wait_ge(acc_free, a + 1)
                dve.tensor_scalar(YF[:, c, :], X[:, c, :], vcol("norm_f_g_2", c), None, ALU.mult).then_inc(low_done, 1)
            if c:
                add_square(44 + c, c - 1, 0, (c - 1) % 2)
        rt_copy(3)
        for g in range(8):
            t, half = g // 2, g % 2
            dve.wait_ge(out_ps, g + 1)
            dve.tensor_scalar(OUT[:, t, half * S:half * S + S], PS[:, 4 + g % 4, :], RT[:, t:t + 1], None,
                              ALU.mult).then_inc(out_ready, 1)

    ctx.close()


_INS = {"x": (S, D), "w_in": None, "b_forget": (8,), "lambda_q1": (HD,), "lambda_k1": (HD,), "lambda_q2": (HD,),
        "lambda_k2": (HD,), "mix_norm_g": (D,), "diff_norm_g": (P,), "w_out": None, "ffn_norm_g": (D,),
        "w_gate": None, "w_up": None, "w_down": None, "final_norm_g": (D,), "norm1_g_2": (D,), "w_in_2": None,
        "b_in_2": (36 * P,), "rpb_2": (8, RPR, RPC), "w_na_out_2": None, "conv_dw_w_2": (TAPS * 4 * P,),
        "conv_dw_b_2": (4 * P,), "conv_ln_g_2": (4 * P,), "conv_ln_b_2": (4 * P,), "w_conv_out_2": None,
        "w_out_2": None, "norm2_g_2": (D,), "w_up_2": None, "ffn_dw_w_2": (3 * 2 * FF,), "ffn_dw_b_2": (2 * FF,),
        "w_down_2": None, "norm_f_g_2": (D,)}


def kernel(**inputs):
    import concourse.bacc as bacc
    from concourse.bass_utils import run_bass_kernel_spmd

    nc = bacc.Bacc("TRN2", target_bir_lowering=False, num_devices=1)
    arrays, d = {}, {}
    for name, shape in _INS.items():
        a = np.ascontiguousarray(inputs[name])
        a = a.reshape(shape or a.shape[1:])
        arrays["in_" + name] = a
        d[name] = nc.dram_tensor("in_" + name, a.shape, mybir.dt.from_np(a.dtype), kind="ExternalInput").ap()
    d["out"] = nc.dram_tensor("out_x", (S, D), F32, kind="ExternalOutput").ap()
    program(nc, d)
    r = run_bass_kernel_spmd(nc, [arrays], core_ids=[0])
    return r.results[0]["out_x"].reshape(inputs["x"].shape)
```

```python
from contextlib import ExitStack

import numpy as np

import concourse.bass as bass
from concourse import mybir

F32 = mybir.dt.float32
F32R = mybir.dt.float32r
BF16 = mybir.dt.bfloat16
I32 = mybir.dt.int32
ALU = mybir.AluOpType
ACT = mybir.ActivationFunctionType
AX = mybir.AxisListType.X

P = 128
S = 512
D = 1024
KD = D // P
TC = S // P
FF = 2816
KF = FF // P
HD = 64
EPS = 1e-6
NEG = -1e30
UNIT = 1024
LAM_INIT = 0.2
GRID = 64
ROWS = S // GRID
RH, CW = 8, 16
RPR, RPC = 2 * RH - 1, 2 * CW - 1
TAPS = 31
WIN = 48


def plan_units():
    u = []
    v = lambda m, c0: [(m, 4 * k, 4, c0 + 256 * h, 256) for h in range(2) for k in range(2)]
    col = lambda m, c0: [(m, 0, 8, c0, 128)]
    FOX_Q, FOX_K, FOX_V, DQ, DK, DV = 0, 512, 1024, 1544, 2056, 2568
    u += col("w_in", FOX_Q) + col("w_in", FOX_K)
    u += v("w_in", FOX_V)
    for j in range(1, 4):
        u += col("w_in", FOX_Q + P * j) + col("w_in", FOX_K + P * j)
    u += col("w_in", DQ) + col("w_in", DK)
    u += v("w_in", DV)
    out_a = [("w_out", 0, 4, 256 * c, 256) for c in range(4)]
    for j in range(1, 4):
        u += col("w_in", DQ + P * j) + col("w_in", DK + P * j)
        if j == 2:
            u += out_a[:1]
    u += out_a[1:]
    u += [("w_out", 4, 4, 256 * c, 256) for c in range(4)]
    marks = {"ffn1": len(u)}
    for j in range(KF):
        u += col("w_gate", P * j) + col("w_up", P * j)
    marks["down1"] = len(u)
    for c in range(KD):
        u += [("w_down", 0, 8, P * c, P), ("w_down", 8, 8, P * c, P), ("w_down", 16, 6, P * c, P)]
    NQ, NK, NV, CA, CB, GA, GB = 0, 512, 1024, 1536, 2048, 2560, 3584
    for j in range(4):
        u += col("w_in_2", CA + P * j) + col("w_in_2", CB + P * j)
    u += v("w_in_2", NV)
    for j in range(4):
        u += col("w_in_2", NQ + P * j) + col("w_in_2", NK + P * j)
    marks["gates"] = len(u)
    for c in range(KD):
        u += col("w_in_2", GB + P * c)
    for c in range(KD):
        u += col("w_in_2", GA + P * c)
    marks["na_out"] = len(u)
    u += [("w_na_out_2", 0, 4, 256 * c, 256) for c in range(4)]
    u += [("w_conv_out_2", 0, 4, 256 * c, 256) for c in range(4)]
    for c in range(KD):
        u += col("w_out_2", P * c)
    marks["ffn2"] = len(u)
    for j in range(KF):
        u += col("w_up_2", P * j) + col("w_up_2", FF + P * j)
    marks["down2"] = len(u)
    for c in range(KD):
        u += [("w_down_2", 0, 8, P * c, P), ("w_down_2", 8, 8, P * c, P), ("w_down_2", 16, 6, P * c, P)]
    marks["end"] = len(u)
    return u, marks


VECS = [("conv_dw_w_2", 4 * TAPS), ("ffn_dw_w_2", 3 * 2 * KF), ("ffn_dw_b_2", 2 * KF), ("b_in_2", 36),
        ("mix_norm_g", 8), ("ffn_norm_g", 8), ("final_norm_g", 8), ("norm1_g_2", 8), ("norm2_g_2", 8),
        ("norm_f_g_2", 8), ("conv_dw_b_2", 4), ("conv_ln_g_2", 4), ("conv_ln_b_2", 4), ("diff_norm_g", 1)]


def plan_vectors():
    at, loads, n = {}, [], 0
    for name, rows in VECS:
        at[name] = n
        done = 0
        while done < rows:
            k = min(rows - done, P - n % P)
            loads.append((name, done, k, n))
            done += k
            n += k
    return at, loads, n


def program(nc, d):
    units, marks = plan_units()
    NU = len(units)
    vec_at, vec_loads, n_vec = plan_vectors()
    ctx = ExitStack()
    base = 16512

    def at(name, off, shape, dt):
        return nc.alloc_sbuf_tensor_at(name, shape, dt, offset=base + off)

    XH = at("XH", 0, [P, KD, S], F32R)
    XL = at("XL", 16384, [P, KD, S], F32R)
    YF = at("YF", 0, [P, KD, S], F32)
    OUT = at("OUT", 16384, [P, TC, D], F32)
    WH = at("WH", 32768, [P, 4, UNIT], F32R)
    WL = at("WL", 49152, [P, 4, UNIT], F32R)
    RAW = at("RAW", 65536, [P, 2, UNIT], F32)
    X = at("X", 73728, [P, KD, S], F32)
    T = at("T", 90112, [P, 4, 520], F32)
    R = at("R", 98432, [P, S], F32)
    RP = at("RP", 100480, [P, S], F32)
    SS = at("SS", 102528, [P, 2, S], F32)
    SQ = at("SQ", 106624, [P, 2, S], F32)
    small = [110720]

    def tiny(name, shape, dt):
        n = int(np.prod(shape[1:])) * (2 if dt == BF16 else 4)
        o = small[0]
        small[0] += (n + 31) // 32 * 32
        assert small[0] <= 117760, name
        return at(name, o, shape, dt)

    PR = at("PR", 117760, [P, 4, S], F32)
    OD = at("OD", 102528, [P, S], F32)
    BVB = at("BVB", 102528, [P, S], F32)
    HH = at("HH", 117760, [P, KF, S], F32R)
    HL = at("HL", 117760 + 45056, [P, KF, S], F32R)
    BIG = 125952
    XTM = at("XTM", BIG, [P, TC, D], F32)
    MH = at("MH", BIG, [P, KD, S], F32R)
    ML = at("ML", BIG + 16384, [P, KD, S], F32R)

    def heads_memory(tag, o):
        return dict(VH=at("VH" + tag, o, [P, TC, S], F32R), VL=at("VL" + tag, o + 8192, [P, TC, S], F32R),
                    QH=at("QH" + tag, o + 16384, [P, 2, S], F32R), QL=at("QL" + tag, o + 20480, [P, 2, S], F32R),
                    KH=at("KH" + tag, o + 24576, [P, 2, S], F32R), KL=at("KL" + tag, o + 28672, [P, 2, S], F32R),
                    PTH=at("PTH" + tag, o + 32768, [P, TC, S], F32R), PTL=at("PTL" + tag, o + 40960, [P, TC, S], F32R))

    M1 = heads_memory("1", BIG + 32768)
    CR = at("CR", BIG + 81920, [P, S], F32R)
    TRI = at("TRI", BIG + 65536, [P, 896], F32R)
    LFH = at("LFH", BIG + 65536 + 3584, [P, TC, P], F32R)
    LFL = at("LFL", BIG + 65536 + 5632, [P, TC, P], F32R)
    CT = at("CT", BIG + 73728, [P, S], F32R)
    STG = at("STG", BIG + 73728 + 2048, [P, 896], F32)
    ROWV = at("ROWV", 117760, [P, 4, P], F32)
    WFR = at("WFR", 119808, [P, KD, 8], F32)
    WFH = at("WFH", 120064, [P, KD, 8], F32R)
    WFL = at("WFL", 120320, [P, KD, 8], F32R)
    Z = at("Z", 120576, [P, 4, TC * 8], F32)
    LAMV = at("LAMV", 121088, [P, 4, HD], F32)
    MKS = at("MKS", BIG + 32768, [P, 4, 384], F32)
    KC = at("KC", BIG + 83968, [P, 384], F32)
    NAH = at("NAH", BIG, [P, 4, S], F32R)
    NAL = at("NAL", BIG + 8192, [P, 4, S], F32R)
    BN = at("BN", BIG + 16384, [P, 8, WIN * ROWS], F32)
    BNR = at("BNR", BIG + 70144, [P, ROWS, 8, WIN], F32)
    UW = 544
    UO = 16
    U = at("U", BIG + 28672, [P, 4, UW], F32)
    M2 = heads_memory("2", BIG + 37376)
    SG = at("SG", BIG + 37376, [P, 2 * KD, S], F32)
    LSQ = at("LSQ", BIG + 70144, [P, 2, S], F32)
    LSUM = at("LSUM", BIG + 70144 + 4096, [P, S], F32)
    LR = at("LR", BIG + 70144 + 6144, [P, S], F32)
    CH = at("CH", BIG + 28672, [P, 4, S], F32R)
    CL = at("CL", BIG + 78336, [P, 4, S], F32R)
    MH2 = at("MH2", BIG - 8192, [P, KD, S], F32R)
    ML2 = at("ML2", BIG + 8192, [P, KD, S], F32R)

    IDF = tiny("IDF", [P, P], F32)
    ONE = tiny("ONE", [P, P], F32)
    IDB = tiny("IDB", [P, P], BF16)
    CMB = tiny("CMB", [P, P], BF16)
    NMB = tiny("NMB", [P, 3, 384], BF16)
    VEC = tiny("VEC", [P, n_vec], F32)
    SELF = tiny("SELF", [P, 12], F32)
    SEL = tiny("SEL", [P, 12], F32R)
    BFG = tiny("BFG", [P, 8], F32)
    NM = tiny("NM", [P, 4], F32)
    RS = tiny("RS", [P, 4], F32)
    RI = tiny("RI", [P, 4], F32)
    RT = tiny("RT", [P, TC], F32)
    LAM = tiny("LAM", [P, 8], F32)
    GG = tiny("GG", [P, 8], F32)
    B8 = tiny("B8", [P, 4], F32)
    GD = tiny("GD", [P, 1], F32)
    QC = tiny("QC", [P, 1], F32)
    QI = tiny("QI", [P, 2], I32)
    BT = tiny("BT", [P, 1], F32)
    RPP = at("RPP", BIG + 79872, [P, GRID], F32)
    CST = at("CST", BIG + 79360, [P, P], F32)
    POS = at("POS", BIG + 32768 + 7680, [P, S], F32)
    CZ = [[at("CZ00", 100480, [P, S], F32), at("CZ01", 104576, [P, S], F32)],
          [at("CZ10", 106624, [P, S], F32), at("CZ11", 108672, [P, S], F32)]]
    SHIFT = 56
    scratch = nc.dram_tensor("rpb_shifted", [8, 8 * RPR, SHIFT], F32, kind="Internal").ap()

    Y = [SQ[:, 0, :], SQ[:, 1, :], R[:, :], SS[:, 0, :]]
    RN2 = SS[:, 1, :]

    PS = ctx.enter_context(nc.psum_tensor("PS", [P, 8, S], F32))
    ACC, SCO, TRB, OB = 0, 2, 4, 6

    def vcol(name, c, n=1):
        return VEC[:, vec_at[name] + c:vec_at[name] + c + n]

    sems = {}

    def sem(name):
        sems[name] = ctx.enter_context(nc.semaphore(name))
        return sems[name]

    x_in = sem("x_in")
    consts_in = sem("consts_in")
    rows_in = sem("rows_in")
    wf_in = sem("wf_in")
    rpb_in = sem("rpb_in")
    rpb_negated = sem("rpb_negated")
    rpb_out = sem("rpb_out")
    bias_in = sem("bias_in")
    bias_ready = sem("bias_ready")
    bv_in = sem("bv_in")
    w_landed = [sem(f"w_landed{i}") for i in range(2)]
    w_hi = sem("w_hi")
    w_lo = sem("w_lo")
    w_used = sem("w_used")
    pool_made = sem("pool_made")
    dve_made = sem("dve_made")
    vec_t = sem("vec_t")
    vec_ready = sem("vec_ready")
    part_ready = sem("part_ready")
    acc_free = sem("acc_free")
    prod = sem("prod")
    act_done = sem("act_done")
    low_done = sem("low_done")
    sq_ready = sem("sq_ready")
    ss_done = sem("ss_done")
    norm_ps = sem("norm_ps")
    ln_done = sem("ln_done")
    r_ready = sem("r_ready")
    rt_ps = sem("rt_ps")
    rt_ready = sem("rt_ready")
    r_mix = sem("r_mix")
    fl_ps = sem("fl_ps")
    fl_step = sem("fl_step")
    fl_act = sem("fl_act")
    lf_ready = sem("lf_ready")
    cum_ps = sem("cum_ps")
    cr_act = sem("cr_act")
    cr_dve = sem("cr_dve")
    wf_split = sem("wf_split")
    sc_ready = sem("sc_ready")
    xg_ready = sem("xg_ready")
    merged = sem("merged")
    cz_mid = sem("cz_mid")
    cz_tap = sem("cz_tap")
    cz_taps = sem("cz_taps")
    gelu_done = sem("gelu_done")
    glu_ready = sem("glu_ready")
    hid_hi = sem("hid_hi")
    x1_done = sem("x1_done")
    lam_ready = sem("lam_ready")
    max_ready = sem("max_ready")
    exp_ready = sem("exp_ready")
    rinv_done = sem("rinv_done")
    p_half = sem("p_half")
    p_ready = sem("p_ready")
    tr_ready = sem("tr_ready")
    pth_done = sem("pth_done")
    ptl_done = sem("ptl_done")
    pv_ready = sem("pv_ready")
    oh_done = sem("oh_done")
    o_free = sem("o_free")
    od_copy = sem("od_copy")
    od_sq = sem("od_sq")
    od_ps = sem("od_ps")
    od_r = sem("od_r")
    od_scaled = sem("od_scaled")
    conv_done = sem("conv_done")
    gate_ready = sem("gate_ready")
    ln_sum = sem("ln_sum")
    ln_ps = sem("ln_ps")
    ln_d = sem("ln_d")
    ln_r = sem("ln_r")
    ln_n = sem("ln_n")
    silu_done = sem("silu_done")
    ch_done = sem("ch_done")
    cl_done = sem("cl_done")
    out_ps = sem("out_ps")
    out_ready = sem("out_ready")
    stored = sem("stored")

    def perm_of(ap):
        return ap.rearrange("p (r g c) -> p g r c", r=ROWS, c=8)

    def natural_of(ap):
        return ap.rearrange("p (g r c) -> p r g c", r=ROWS, c=8)

    def grid3(ap, order):
        a, b = (GRID // 8, ROWS) if order == "perm" else (ROWS, GRID // 8)
        return ap.rearrange("p (a b c) -> p a b c", a=a, b=b)

    TL = {}
    n_tile = 0
    for name, n in [("init", 8), ("fox0", 2), ("v1", 8), ("foxf", 8), ("v2", 8), ("difff", 14), ("out1", 8),
                    ("ffn1", 44), ("down1", 8), ("cab", 8), ("v3", 8), ("na0", 2), ("naf", 6), ("gates_b", 8),
                    ("gates_a", 8),
                    ("na_out", 8), ("conv_out", 8), ("out2", 8), ("ffn2", 44), ("down2", 8)]:
        TL[name] = n_tile
        n_tile += n
    UN = {"fox0": 0, "v1": 2, "foxf": 6, "v2": 14, "difff": 18, "out1": 28, "ffn1": marks["ffn1"],
          "down1": marks["down1"], "cab": marks["down1"] + 24, "v3": marks["down1"] + 32,
          "na0": marks["down1"] + 36, "naf": marks["down1"] + 38, "gates_b": marks["gates"], "gates_a": marks["gates"] + 8,
          "na_out": marks["na_out"], "conv_out": marks["na_out"] + 4, "out2": marks["na_out"] + 8,
          "ffn2": marks["ffn2"], "down2": marks["down2"]}
    assert UN["out1"] + 4 == UN["ffn1"] and UN["naf"] + 6 == UN["gates_b"]

    PT0, n_part = {}, 0
    for name in TL:
        PT0[name] = n_part
        n_part += {"init": 8, "v": 6, "difff": 4, "out1": 4, "na_out": 4, "conv_out": 4}.get("v" if name[0] == "v" else name, 0)

    per = {"init": (8, 8), "v1": (8, 8), "fox0": (2, 2), "foxf": (8, 8), "v2": (8, 8), "difff": (6, 6),
           "out1": (8, 8), "ffn1": (44, 22), "down1": (8, 8), "cab": (8, 4), "v3": (8, 8), "na0": (2, 2),
           "naf": (6, 6), "gates_b": (8, 0), "gates_a": (8, 0), "na_out": (0, 0), "conv_out": (8, 8), "out2": (8, 8),
           "ffn2": (0, 22), "down2": (0, 8)}
    H0, L0 = {}, {}
    h = l = 0
    for name in TL:
        H0[name], L0[name] = h, l
        h += per[name][0]
        l += per[name][1]

    def src_of(spec):
        m, k0, nk, c0, nc_ = spec
        return d[m].rearrange("(k p) n -> p k n", p=P)[:, k0:k0 + nk, c0:c0 + nc_]

    block = ctx.enter_context(nc.Block())

    @block.sync
    def _(sp):
        def load(n, s, src, width=UNIT, ncols=P):
            u = 4 * n + s
            if not (isinstance(n, int) and u < 2):
                sp.wait_ge(w_lo, u - 1)
            dst = RAW[:, s % 2, 0:width].rearrange("p (k n) -> p k n", n=ncols)
            sp.dma_start(dst, src).then_inc(w_landed[s % 2], 16)

        def load_units(lo, hi):
            for u in range(lo, hi):
                m, k0, nk, c0, ncol = units[u]
                load(u // 4, u % 4, src_of(units[u]), nk * ncol, ncol)

        for t in range(TC):
            sp.dma_start(XTM[:, t, :], d["x"][t * P:(t + 1) * P, :]).then_inc(x_in, 16)
        load_units(0, 2)
        sp.dma_start(WFR[:, :, :], d["w_in"].rearrange("(k p) n -> p k n", p=P)[:, :, 1536:1544]).then_inc(wf_in, 16)
        sp.wait_ge(pool_made, 1)
        for o in range(RPR):
            sp.dma_start(RPP[8 * o:8 * o + 8, 16:16 + RPC], d["rpb_2"][:, o, :]).then_inc(rpb_in, 16)
        load_units(2, 6)
        sp.wait_ge(rpb_negated, 1)
        for cq in range(8):
            sp.dma_start(scratch[cq], RPP[0:8 * RPR, 7 - cq:7 - cq + SHIFT]).then_inc(rpb_out, 16)
        load_units(6, marks["ffn1"])

        def looped(lo, count, mats):
            with sp.Fori(0, count) as i:
                for s, (m, off, step) in enumerate(mats):
                    src = d[m].rearrange("(k p) n -> p k n", p=P)[:, 0:KD, bass.ds(i * step + off, P)]
                    load(i + lo // 4, s, src)

        looped(marks["ffn1"], KF // 2, [("w_gate", 0, 256), ("w_up", 0, 256), ("w_gate", P, 256), ("w_up", P, 256)])
        load_units(marks["down1"], marks["down1"] + 28)
        sp.wait_ge(w_used, UN["down1"] + 24)
        sp.wait_ge(rpb_out, 16 * 8)
        for gq in range(2):
            for qr in range(ROWS):
                off = (RH - 1 - qr) * 8 * SHIFT + 8 - 8 * gq
                src = bass.AP(tensor=scratch.tensor, offset=off,
                              ap=[[8 * RPR * SHIFT, 8], [SHIFT, ROWS * 8], [1, WIN]])
                q0 = gq * 64 + qr * 8
                sp.dma_start(BNR[q0:q0 + 8, :, :, :].rearrange("p r h c -> p (r h) c"), src).then_inc(bias_in, 16)
        sp.wait_ge(norm_ps, 4)
        sp.dma_start(BVB[:, :], d["b_in_2"][1024:1536].partition_broadcast(P)).then_inc(bv_in, 16)
        load_units(marks["down1"] + 28, UN["gates_a"])
        looped(UN["gates_a"], 2, [("w_in_2", 2560 + P * s, 512) for s in range(4)])
        load_units(marks["na_out"], marks["ffn2"])
        looped(marks["ffn2"], KF // 2, [("w_up_2", 0, 256), ("w_up_2", FF, 256), ("w_up_2", P, 256), ("w_up_2", FF + P, 256)])
        load_units(marks["down2"], NU)
        for t in range(TC):
            sp.wait_ge(out_ready, 2 * t + 2)
            sp.dma_start(d["out"][t * P:(t + 1) * P, :], OUT[:, t, :]).then_inc(stored, 16)
        sp.wait_ge(stored, 16 * TC)

    @block.gpsimd
    def _(pool):
        made = [0]

        def step(ins, wait=True):
            made[0] += 1
            ins.then_inc(pool_made, 1)
            if wait:
                pool.wait_ge(pool_made, made[0])

        step(pool.memset(RPP[:, :], 0.0))
        step(pool.memset(IDF[:, :], 0.0))
        step(pool.affine_select(out=IDF[:, :], in_=IDF[:, :], compare_op=ALU.not_equal, fill=1.0, base=0,
                                pattern=[[-1, P]], channel_multiplier=1))
        step(pool.memset(ONE[:, :], 1.0))
        step(pool.memset(SELF[:, :], 0.0))
        for b in (0, -32):
            step(pool.affine_select(out=SELF[:, 0:8], in_=SELF[:, 0:8], compare_op=ALU.not_equal, fill=1.0, base=b,
                                    pattern=[[-1, 8]], channel_multiplier=1))
        for j in range(4):
            step(pool.memset(SELF[64:65, 8 + j:9 + j], 2.0 ** (-2 * (j + 1))))
        step(pool.memset(STG[:, :], 0.0))
        step(pool.affine_select(out=STG[:, :], in_=STG[:, :], compare_op=ALU.is_gt, fill=1.0, base=384,
                                pattern=[[-1, 896]], channel_multiplier=1))
        step(pool.memset(CST[:, :], 0.0))
        step(pool.affine_select(out=CST[:, :], in_=CST[:, :], compare_op=ALU.is_ge, fill=NEG, base=0,
                                pattern=[[-1, P]], channel_multiplier=1))
        step(pool.iota(POS[:, :], [[1, S]], base=0, channel_multiplier=0, allow_small_or_imprecise_dtypes=True))
        step(pool.iota(KC[:, :].rearrange("p (g r c) -> p g r c", g=6, r=ROWS), [[8, 6], [0, ROWS], [1, 8]], base=0,
                       channel_multiplier=0, allow_small_or_imprecise_dtypes=True))
        step(pool.iota(QI[:, 0:1], [[0, 1]], base=0, channel_multiplier=1))

        def lo_part(n, s, width=UNIT):
            u = 4 * n + s
            pool.wait_ge(w_hi, u + 1)
            if not (isinstance(n, int) and n == 0):
                pool.wait_ge(w_used, u - 3)
            pool.tensor_tensor(WL[:, s, 0:width], RAW[:, s % 2, 0:width], WH[:, s, 0:width].bitcast(F32),
                               ALU.subtract).then_inc(w_lo, 1)

        def lo_parts(g0, g1):
            if g0 == 0:
                for s in range(4):
                    lo_part(0, s)
                g0 = 1
            with pool.Fori(g0, g1) as i:
                for s in range(4):
                    lo_part(i, s)

        def lo_down(u0):
            for u in range(u0, u0 + 24):
                lo_part(u // 4, u % 4, units[u][2] * P)

        lo_parts(0, marks["down1"] // 4)
        lo_down(marks["down1"])
        lo_parts(marks["down1"] // 4 + 6, marks["down2"] // 4)
        lo_down(marks["down2"])

    NA_KEYS = [(0, 2), (0, 3), (1, 4), (2, 4)]

    def family(kind):
        if kind == "diff":
            sc = [(hd, comp, qb) for hd in range(4) for qb in range(4) for comp in range(2)]
            tr = [(hd, qb) for hd in range(4) for qb in range(4)]
            ready_after = {2 * i + 1: i for i in range(16)}
        else:
            sc = [(hd, hd % 2, qb) for hd in range(8) for qb in range(4)]
            tr = [(hd, qb) for hd in range(8) for qb in range(4)]
            ready_after = {i: i for i in range(32)}
        return sc, tr, ready_after

    FAM = {"fox": dict(mem=M1, fill="foxf", s0=0, t0=0, o0=0),
           "diff": dict(mem=M1, fill="difff", s0=32, t0=32, o0=8),
           "na": dict(mem=M2, fill="naf", s0=64, t0=48, o0=12)}
    N_SCORES = 32

    def fill_plan(kind):
        items = []

        def add(what, idx, a, unit, s0, s1, ends=True, part=0):
            items.append(dict(what=what, idx=idx, a=a, unit=unit, s0=s0, s1=s1, ends=ends, part=part))

        a, u = TL[FAM[kind]["fill"]], UN[FAM[kind]["fill"]]
        qk_steps = [(max(4 * f - 1, 0), 4 * f + 2) for f in range(8)]
        if kind == "fox":
            for f in range(8):
                add("qk", f, a + f, u + f, *qk_steps[f])
            for i in range(3):
                add("v", i, TL["v2"] + i, UN["v2"], N_SCORES + i, N_SCORES + i, False, PT0["v2"] + i + 1)
        elif kind == "na":
            for f in range(6):
                add("qk", f, a + f, u + f, *qk_steps[f])
            for c in range(6):
                s0 = N_SCORES - 8 + 2 * c
                add("gb", c, TL["gates_b"] + c, UN["gates_b"] + c, s0, min(s0 + 1, N_SCORES + 2))
        else:
            order = [("qk", 0, 0, 2), ("qk", 1, 3, 6), ("qk", 2, 7, 9), ("qk", 3, 10, 12), ("oa", 0, 13, 13),
                     ("oa", 1, 14, 14), ("qk", 4, 15, 18), ("qk", 5, 19, 22), ("oa", 2, 23, 24), ("oa", 3, 25, 26),
                     ("oa", 4, 27, 28), ("oa", 5, 29, 30), ("oa", 6, 31, 32), ("oa", 7, 33, 34)]
            for what, idx, s0, s1 in order:
                ends = what == "qk" or idx % 2 == 1
                add(what, idx, a, u, s0, s1, ends, PT0["difff"] + idx // 2 + 1)
                a += 1
                u += ends
        return items

    def fills_done(kind, step):
        return [it for it in fill_plan(kind) if it["s1"] == step]

    def fill_chunks(it, step, n):
        k = it["s1"] - it["s0"] + 1
        i = step - it["s0"]
        return range(n * i // k, n * (i + 1) // k)

    def gate_place(c):
        return KD + 2 * c if c < 4 else KD + 1 + 2 * (c - 4)

    def early_bank(s):
        return (ACC, ACC + 1, OB, OB + 1)[s]

    def keys_of(kind, qb):
        return NA_KEYS[qb] if kind == "na" else (0, qb + 1)

    def pair_index(kind, hd):
        return hd if kind == "diff" else hd // 2

    def slot_free(kind, i):
        t0 = FAM[kind]["t0"]
        if i < 4:
            return t0
        return t0 + ((i - 4) // 2 + 1 if kind == "diff" else i - 3)

    def parity_of_filler(kind, f):
        return (f // 2 + 1) % 2

    @block.tensor
    def _(pe):
        def mm3(out, ah, al, bh, bl, start, stop):
            pe.matmul(out, ah, bh, start=start, stop=False)
            pe.matmul(out, ah, bl, start=False, stop=False)
            return pe.matmul(out, al, bh, start=False, stop=stop)

        def need_acc(a):
            if not (isinstance(a, int) and a < 2):
                pe.wait_ge(acc_free, a - 1)

        def fm_chunks(n, s, bank, k0, ks, bh, bl, start, stop, ncols=P, c0=0):
            for k in ks:
                w0 = k * ncols + c0
                ins = mm3(PS[:, ACC + bank, :], WH[:, s, w0:w0 + P], WL[:, s, w0:w0 + P],
                          bh[:, k0 + k, :], bl[:, k0 + k, :], start and k == ks[0], stop and k == ks[-1])
            return ins

        def fm_tile(n, s, a, bh=XH, bl=XL, bank=None):
            pe.wait_ge(w_lo, 4 * n + s + 1)
            need_acc(a)
            bank = s % 2 if bank is None else bank
            fm_chunks(n, s, bank, 0, range(KD), bh, bl, True, True).then_inc(w_used, 1)

        def first_pair(u, a, bh, bl, chunk_ready):
            for s in range(2):
                need_acc(a + s)
            pe.wait_ge(w_lo, u + 2)
            for k in range(KD):
                chunk_ready(k)
                for s in range(2):
                    ins = fm_chunks((u + s) // 4, (u + s) % 4, s, 0, [k], bh, bl, k == 0, k == KD - 1)
                    if k == KD - 1:
                        ins.then_inc(w_used, 1)

        def low(base):
            return lambda k: pe.wait_ge(low_done, base + k + 1)

        def v_tile(name, i):
            half, t, a = i // TC, i % TC, TL[name] + i
            pe.wait_ge(w_lo, UN[name] + 2 * half + 2)
            need_acc(a)
            for k in range(KD):
                u = UN[name] + 2 * half + k // 4
                w = slice((k % 4) * 256, (k % 4) * 256 + 256)
                ins = mm3(PS[:, ACC + a % 2, 0:256], XH[:, k, t * P:(t + 1) * P], XL[:, k, t * P:(t + 1) * P],
                          WH[:, u % 4, w], WL[:, u % 4, w], k == 0, k == KD - 1)
            if t == TC - 1:
                ins.then_inc(w_used, 2)
            else:
                ins.then_inc(part_ready, 1)

        def norm_sum(ss, which=0):
            pe.wait_ge(ss_done, ss)
            pe.matmul(PS[:, SCO + which, :], ONE[:, :], SS[:, which, :], start=True, stop=True).then_inc(norm_ps, 1)

        def rt_transposes(src):
            for t in range(TC):
                ins = pe.transpose(PS[:, SCO + 1, t * P:(t + 1) * P], src[:, t * P:(t + 1) * P], IDF[:, :])
            ins.then_inc(rt_ps, 1)

        pe.wait_ge(pool_made, 4)
        pe.wait_ge(x_in, 16 * TC)
        for c in range(KD):
            need_acc(c)
            for t in range(TC):
                ins = pe.transpose(PS[:, TRB + c % 2, t * P:(t + 1) * P], XTM[:, t, c * P:(c + 1) * P], IDF[:, :])
            ins.then_inc(part_ready, 1)
            if c == 0:
                pe.wait_ge(rows_in, 16 * len(vec_loads))
                for i in range(4):
                    r = min(P, n_vec - i * P)
                    ins = pe.transpose(PS[:, OB, i * P:i * P + r], ROWV[0:r, i, :], IDF[0:r, 0:r])
                ins.then_inc(vec_t, 1)

        pe.wait_ge(w_lo, 2)
        for k in range(KD):
            pe.wait_ge(low_done, k + 1)
            for i in range(2):
                ins = fm_chunks(0, i, i, 0, [k], XH, XL, k == 0, k == KD - 1)
                if k == KD - 1:
                    ins.then_inc(w_used, 1)
        norm_sum(8)
        pe.wait_ge(wf_split, 2)
        for t in range(TC):
            for k in range(KD):
                ins = mm3(PS[:, TRB, t * 8:t * 8 + 8], XH[:, k, t * P:(t + 1) * P], XL[:, k, t * P:(t + 1) * P],
                          WFH[:, k, :], WFL[:, k, :], k == 0, k == KD - 1)
        ins.then_inc(fl_ps, 1)
        pe.wait_ge(r_ready, 1)
        rt_transposes(R)
        for i in range(8):
            v_tile("v1", i)
        pe.wait_ge(lf_ready, 2)
        for t in range(TC):
            for i, part in enumerate((LFH, LFL)):
                ins = pe.matmul(PS[:, TRB + 1, :], part[:, t, :], TRI[:, 384 - P * t:896 - P * t],
                                start=(t == 0 and i == 0), stop=(t == TC - 1 and i == 1))
        ins.then_inc(cum_ps, 1)

        def attention(kind):
            f = FAM[kind]
            sc, tr, ready_after = family(kind)
            mem, s0, t0, o0 = f["mem"], f["s0"], f["t0"], f["o0"]
            first_low = L0[f["fill"]]

            def scores(i):
                hd, half, qb = sc[i]
                g = s0 + i
                pair = pair_index(kind, hd)
                pe.wait_ge(low_done, first_low + 2 * pair)
                if g >= 2:
                    pe.wait_ge(exp_ready, g - 1)
                if i == 0 and kind == "fox":
                    pe.wait_ge(cr_act, 2)
                    pe.wait_ge(cr_dve, 2)
                k0, k1 = keys_of(kind, qb)
                n = (k1 - k0) * P
                out = PS[:, SCO + g % 2, 0:n]
                r = slice(half * HD, half * HD + HD)
                q = slice(qb * P, qb * P + P)
                ks = slice(k0 * P, k1 * P)
                par = pair % 2
                pe.matmul(out, mem["QH"][r, par, q], mem["KH"][r, par, ks], start=True, stop=False)
                pe.matmul(out, mem["QH"][r, par, q], mem["KL"][r, par, ks], start=False, stop=False)
                pe.matmul(out, mem["QL"][r, par, q], mem["KH"][r, par, ks], start=False, stop=False)
                if kind == "na":
                    m = {0: 1, 1: 0, 2: 0, 3: 2}[qb]
                    ins = pe.matmul(out, IDB[:, :], NMB[:, m, 0:n], start=False, stop=True)
                else:
                    c = hd if kind == "fox" else 8 + hd
                    col = SEL[:, c:c + 1]
                    sel = bass.AP(tensor=col.tensor, offset=col.offset, ap=[list(col.ap[0]), [0, P]])
                    pe.matmul(out, sel, CR[:, 0:n], start=False, stop=False)
                    ins = pe.matmul(PS[:, SCO + g % 2, n - P:n], IDB[:, :], CMB[:, :], start=False, stop=True)
                ins.then_inc(sc_ready, 1)

            def transposes(j):
                hd, qb = tr[j]
                g = t0 + j
                pe.wait_ge(p_ready, g + 1)
                if g >= 2:
                    pe.wait_ge(ptl_done, g - 1)
                k0, k1 = keys_of(kind, qb)
                i = [k for k, v in ready_after.items() if v == j][0]
                slot = (s0 + i - (1 if kind == "diff" else 0)) % 4
                for k in range(k1 - k0):
                    ins = pe.transpose(PS[:, TRB + g % 2, k * P:(k + 1) * P], PR[:, slot, k * P:(k + 1) * P], IDF[:, :])
                ins.then_inc(tr_ready, 1)

            def pv(hd):
                g = o0 + hd
                pe.wait_ge(ptl_done, t0 + 4 * hd + 4)
                if g >= 2:
                    pe.wait_ge(o_free, g - 1)
                vc = slice(hd * P, hd * P + P) if kind == "diff" else slice((hd // 2) * P, (hd // 2) * P + P)
                for n, kc in enumerate((1, 0, 2, 3) if kind == "na" else range(4)):
                    qs = [qb for qb in range(4) if keys_of(kind, qb)[0] <= kc < keys_of(kind, qb)[1]]
                    q = slice(0, S) if n == 0 else slice(qs[0] * P, (qs[-1] + 1) * P)
                    ins = mm3(PS[:, OB + g % 2, q], mem["VH"][:, kc, vc], mem["VL"][:, kc, vc],
                              mem["PTH"][:, kc, q], mem["PTL"][:, kc, q], n == 0, n == 3)
                ins.then_inc(pv_ready, 1)

            def odsum(hd):
                pe.wait_ge(od_sq, hd + 1)
                g = o0 + hd
                pe.matmul(PS[:, OB + g % 2, :], ONE[:, :], SQ[:, 0, :], start=True, stop=True).then_inc(od_ps, 1)

            n = len(sc)
            odq = []
            for i in range(n + 3):
                if i < n:
                    scores(i)
                for it in fill_plan(kind):
                    if not it["s0"] <= i <= it["s1"]:
                        continue
                    if it["what"] == "v":
                        v_tile("v2", it["idx"])
                        continue
                    u, bank = it["unit"], it["a"] % 2
                    if i == it["s0"]:
                        pe.wait_ge(w_lo, u + 1)
                        need_acc(it["a"])
                    if it["what"] == "oa":
                        ks = fill_chunks(it, i, 4)
                        ins = fm_chunks(u // 4, u % 4, bank, 0, ks, MH, ML, i == it["s0"], i == it["s1"], 256,
                                        P * (it["idx"] % 2))
                    else:
                        ks = fill_chunks(it, i, KD)
                        ins = fm_chunks(u // 4, u % 4, bank, 0, ks, XH, XL, i == it["s0"], i == it["s1"])
                    if i == it["s1"]:
                        ins.then_inc(w_used if it["ends"] else part_ready, 1)
                for hd in odq:
                    odsum(hd)
                odq = []
                if i - 3 in ready_after and ready_after[i - 3] % 4 == 3:
                    hd = ready_after[i - 3] // 4
                    pv(hd)
                    if kind == "diff":
                        odq = [hd]
                if i - 2 in ready_after:
                    transposes(ready_after[i - 2])
            for hd in odq:
                odsum(hd)

        attention("fox")
        for i in range(3, 8):
            v_tile("v2", i)
        pe.wait_ge(oh_done, 8)
        pe.wait_ge(o_free, 8)
        attention("diff")

        def mixed_ready(k):
            pe.wait_ge(oh_done, 8 + k + 1)
            pe.wait_ge(o_free, 8 + k + 1)

        def half_units(name, bh, bl, k0=0, hook=None, chunk_ready=None):
            for c in range(0, 8, 2):
                u, a = UN[name] + c // 2, TL[name] + c
                pe.wait_ge(w_lo, u + 1)
                if c == 0:
                    need_acc(a)
                    need_acc(a + 1)
                    for k in range(4):
                        if chunk_ready:
                            chunk_ready(k)
                        for h in range(2):
                            ins = fm_chunks(u // 4, u % 4, h, k0, [k], bh, bl, k == 0, k == 3, 256, P * h)
                            if k == 3:
                                ins.then_inc(w_used if h else part_ready, 1)
                else:
                    for h in range(2):
                        need_acc(a + h)
                        ins = fm_chunks(u // 4, u % 4, h, k0, range(4), bh, bl, True, True, 256, P * h)
                        ins.then_inc(w_used if h else part_ready, 1)
                if hook:
                    hook(c)

        half_units("out1", MH, ML, 4, chunk_ready=mixed_ready)

        def pairs_with_norm(name, ss, base):
            first_pair(UN[name], TL[name], XH, XL, low(base))
            norm_sum(ss)
            for s in range(2, 4):
                fm_tile(UN[name] // 4, s, TL[name] + s - 2, bank=early_bank(s))
            with pe.Fori(1, KF // 2) as i:
                for s in range(4):
                    fm_tile(i + UN[name] // 4, s, 4 * i + s + TL[name])

        def down(name, base):
            for c in range(KD):
                a = TL[name] + c
                for j in range(3):
                    u = UN[name] + 3 * c + j
                    pe.wait_ge(w_lo, u + 1)
                    if j == 0:
                        need_acc(a)
                    nk = units[u][2]
                    for k in range(nk):
                        if c == 0:
                            pe.wait_ge(low_done, base + 8 * j + k + 1)
                        ins = fm_chunks(u // 4, u % 4, a % 2, 8 * j, [k], HH, HL, j == 0 and k == 0, j == 2 and k == nk - 1)
                    ins.then_inc(w_used, 1)

        pairs_with_norm("ffn1", 16, L0["out1"])
        down("down1", L0["ffn1"])

        first_pair(UN["cab"], TL["cab"], XH, XL, low(L0["down1"]))
        norm_sum(32, 0)
        norm_sum(32, 1)
        for i in range(2, 8):
            u = UN["cab"] + i
            fm_tile(u // 4, u % 4, TL["cab"] + (i - 2 if i < 4 else i), bank=early_bank(i) if i < 4 else None)
        v_tile("v3", 0)
        pe.wait_ge(r_mix, 4)
        rt_transposes(RP)
        for i in range(1, 8):
            v_tile("v3", i)
        for i in range(2):
            u = UN["na0"] + i
            fm_tile(u // 4, u % 4, TL["na0"] + i)
        attention("na")
        for c in range(6, KD):
            u = UN["gates_b"] + c
            fm_tile(u // 4, u % 4, TL["gates_b"] + c)
        with pe.Fori(0, 2) as i:
            for s in range(4):
                fm_tile(i + UN["gates_a"] // 4, s, 4 * i + s + TL["gates_a"])

        def layernorm_sums(c):
            if c == 0:
                pe.wait_ge(ln_sum, 3)
                pe.matmul(PS[:, SCO, :], ONE[:, :], LSUM[:, :], start=True, stop=True).then_inc(ln_ps, 1)
            if c == 4:
                pe.wait_ge(ss_done, 36)
                pe.matmul(PS[:, SCO + 1, :], ONE[:, :], LSUM[:, :], start=True, stop=True).then_inc(ln_ps, 1)

        pe.wait_ge(oh_done, 20)
        pe.wait_ge(o_free, 20)
        half_units("na_out", NAH, NAL, hook=layernorm_sums)
        half_units("conv_out", CH, CL, chunk_ready=lambda k: pe.wait_ge(cl_done, k + 1))
        first_pair(UN["out2"], TL["out2"], MH2, ML2, low(L0["conv_out"]))
        for c in range(2, KD):
            u = UN["out2"] + c
            fm_tile(u // 4, u % 4, TL["out2"] + c, MH2, ML2)
        pairs_with_norm("ffn2", 44, L0["out2"])
        down("down2", L0["ffn2"])
        norm_sum(52)
        for g in range(8):
            t, half = g // 2, g % 2
            if g >= 4:
                pe.wait_ge(out_ready, g - 3)
            for c in range(4):
                if g < 2:
                    pe.wait_ge(low_done, L0["down2"] + 4 * half + c + 1)
                ins = pe.transpose(PS[:, 4 + g % 4, c * P:(c + 1) * P], YF[:, 4 * half + c, t * P:(t + 1) * P], IDF[:, :])
            ins.then_inc(out_ps, 1)
            if g == 3:
                pe.wait_ge(r_ready, 6)
                rt_transposes(R)

    @block.scalar
    def _(act):
        def hi_part(n, s, width=UNIT):
            u = 4 * n + s
            act.wait_ge(w_landed[s % 2], 16 * (2 * n + s // 2 + 1))
            if not (isinstance(n, int) and n == 0):
                act.wait_ge(w_used, u - 3)
            act.activation(WH[:, s, 0:width], RAW[:, s % 2, 0:width], ACT.Copy).then_inc(w_hi, 1)

        def hi_next(u):
            if u + 4 < NU:
                hi_part(u // 4 + 1, u % 4, units[u + 4][2] * units[u + 4][4])

        def rstd(dst, k, scale, psum):
            act.wait_ge(norm_ps, k)
            act.activation(dst, psum, ACT.Ln, bias=BT[:, 0:1], scale=scale).then_inc(ln_done, 1)
            act.wait_ge(ln_done, k)
            act.activation(dst, dst, ACT.Exp, scale=-0.5).then_inc(r_ready, 1)

        def tile_t(a, n=S):
            return T[:, a % 4, 4:4 + n]

        def gain_and_square(a, c, gain, sq0, i):
            act.activation(XH[:, c, :], X[:, c, :], ACT.Copy, scale=gain).then_inc(act_done, 1)
            if i >= 2:
                act.wait_ge(ss_done, sq0 + i - 1)
            act.activation(SQ[:, i % 2, :], X[:, c, :], ACT.Square).then_inc(sq_ready, 1)

        for name, r0, k, n in vec_loads:
            act.dma_start(ROWV[n % P:n % P + k, n // P, :],
                          d[name].rearrange("(a b) -> a b", b=P)[r0:r0 + k, :]).then_inc(rows_in, 16)
        act.dma_start(BFG[:, :], d["b_forget"].partition_broadcast(P)).then_inc(consts_in, 16)
        for i, name in enumerate(("lambda_q1", "lambda_k1", "lambda_q2", "lambda_k2")):
            act.dma_start(LAMV[:, i, :], d[name].partition_broadcast(P)).then_inc(consts_in, 16)
        for s in range(2):
            hi_part(0, s)
        act.wait_ge(vec_ready, 1)
        act.wait_ge(dve_made, 1)
        for c in range(KD):
            act.wait_ge(acc_free, c + 1)
            gain_and_square(c, c, vcol("mix_norm_g", c), 0, c)
            if c == 1:
                for s in range(2, 4):
                    hi_part(0, s)

        def v_parts(name, mem, n_pv):
            if n_pv:
                act.wait_ge(pv_ready, n_pv)
            for i in range(8):
                a = TL[name] + i
                act.wait_ge(acc_free, a + 1)
                c0 = 256 * (i // 4)
                act.activation(mem["VH"][:, i % 4, c0:c0 + 256], tile_t(a, 256), ACT.Copy).then_inc(act_done, 1)
                if i % 4 == 3:
                    hi_next(UN[name] + 2 * (i // 4))
                    hi_next(UN[name] + 2 * (i // 4) + 1)

        def qk_part(kind, a, par, i, bias=None):
            buf = FAM[kind]["mem"]["QH" if i % 2 == 0 else "KH"]
            act.wait_ge(acc_free, a + 1)
            if bias is None:
                act.activation(buf[:, par, :], tile_t(a), ACT.Copy).then_inc(act_done, 1)
            else:
                act.activation(buf[:, par, :], tile_t(a), ACT.Identity, bias=bias).then_inc(act_done, 1)

        def na_bias(i, pair):
            return B8[:, pair:pair + 1] if i % 2 == 0 else vcol("b_in_2", 4 + pair)

        act.wait_ge(wf_in, 16)
        act.activation(WFH[:, :, :], WFR[:, :, :], ACT.Copy).then_inc(wf_split, 1)
        rstd(R[:, :], 1, 1.0 / D, PS[:, SCO, :])
        for i in range(2):
            hi_next(UN["fox0"] + i)
            qk_part("fox", TL["fox0"] + i, 0, i)
        v_parts("v1", M1, 0)
        act.wait_ge(fl_step, 2)
        act.activation(LAM[:, 2:4], LAM[:, 0:2], ACT.Exp).then_inc(fl_act, 1)
        act.wait_ge(fl_step, 8)
        act.activation(Z[:, 2, :], Z[:, 1, :], ACT.Exp, scale=-1.0).then_inc(fl_act, 1)
        act.wait_ge(fl_act, 2)
        act.activation(Z[:, 2, :], Z[:, 2, :], ACT.Ln, bias=1.0).then_inc(fl_act, 1)
        act.wait_ge(cum_ps, 1)
        act.wait_ge(cr_dve, 1)
        act.activation(CR[0:8, :], PS[0:8, TRB + 1, :], ACT.Copy).then_inc(cr_act, 1)
        act.activation(CT[32:40, :], PS[32:40, TRB + 1, :], ACT.Copy).then_inc(cr_act, 1)

        def gate_part(c):
            a = TL["gates_b"] + c
            act.wait_ge(acc_free, a + 1)
            act.activation(SG[:, gate_place(c), :], tile_t(a), ACT.Identity,
                           bias=vcol("b_in_2", 28 + c)).then_inc(act_done, 1)

        def attention(kind):
            f = FAM[kind]
            sc, tr, ready_after = family(kind)
            mem, s0, t0, o0 = f["mem"], f["s0"], f["t0"], f["o0"]
            n = len(sc)
            norm_q = []
            for i in range(n + 4):
                if i < n:
                    hd, half, qb = sc[i]
                    g = s0 + i
                    k0, k1 = keys_of(kind, qb)
                    w = (k1 - k0) * P
                    act.wait_ge(max_ready, g + 1)
                    if slot_free(kind, i):
                        act.wait_ge(tr_ready, slot_free(kind, i))
                    src = PR[:, g % 4, 0:w] if kind == "na" else PS[:, SCO + g % 2, 0:w]
                    act.activation(PR[:, g % 4, 0:w], src, ACT.Exp, scale=-1.0 if kind == "na" else 1.0, bias=NM[:, g % 4:g % 4 + 1],
                                   accum_out=RS[:, g % 4:g % 4 + 1]).then_inc(exp_ready, 1)
                for it in fills_done(kind, i):
                    fl = it["idx"]
                    if it["what"] == "qk":
                        bias = na_bias(fl, fl // 2 + 1) if kind == "na" else None
                        qk_part(kind, it["a"], parity_of_filler(kind, fl), fl, bias)
                    elif it["what"] == "gb":
                        gate_part(fl)
                    if it["ends"]:
                        hi_next(it["unit"])
                if i - 2 in ready_after:
                    j = ready_after[i - 2]
                    hd, qb = tr[j]
                    g = t0 + j
                    k0, k1 = keys_of(kind, qb)
                    act.wait_ge(tr_ready, g + 1)
                    if o0 + hd > 0:
                        act.wait_ge(pv_ready, o0 + hd)
                    act.activation(mem["PTH"][:, k0:k1, qb * P:(qb + 1) * P],
                                   PS[:, TRB + g % 2, 0:(k1 - k0) * P].rearrange("p (k q) -> p k q", q=P),
                                   ACT.Copy).then_inc(pth_done, 1)
                for hd in norm_q:
                    act.wait_ge(od_ps, hd + 1)
                    act.activation(SQ[:, 1, :], PS[:, OB + (o0 + hd) % 2, :], ACT.Ln, bias=BT[:, 0:1],
                                   scale=1.0 / P).then_inc(od_r, 1)
                    act.wait_ge(od_r, 2 * hd + 1)
                    act.activation(SQ[:, 1, :], SQ[:, 1, :], ACT.Exp, scale=-0.5).then_inc(od_r, 1)
                    act.wait_ge(od_scaled, hd + 1)
                    act.activation(MH[:, 4 + hd, :], OD[:, :], ACT.Copy, scale=GD[:, 0:1]).then_inc(oh_done, 1)
                norm_q = []
                if i - 3 in ready_after and ready_after[i - 3] % 4 == 3:
                    hd = ready_after[i - 3] // 4
                    if kind == "diff":
                        norm_q = [hd]
                    else:
                        act.wait_ge(pv_ready, o0 + hd + 1)
                        r = slice((hd % 2) * HD, (hd % 2) * HD + HD)
                        src = PS[r, OB + (o0 + hd) % 2, :]
                        if kind == "fox":
                            dst = MH[r, hd // 2, :]
                        else:
                            dst, src = grid3(NAH[r, hd // 2, :], "natural"), natural_of(src)
                        act.activation(dst, src, ACT.Copy).then_inc(oh_done, 1)

        attention("fox")
        v_parts("v2", M1, 8)
        attention("diff")

        def residual_tiles(name, gain, sq0, per_tile_units):
            for c in range(KD):
                for u in per_tile_units(c):
                    hi_next(u)
                act.wait_ge(acc_free, TL[name] + c + 1)
                gain_and_square(TL[name] + c, c, vcol(gain, c), sq0, c)

        residual_tiles("out1", "ffn_norm_g", 8, lambda c: [UN["out1"] + c // 2] if c % 2 else [])
        def swiglu_group(i):
            for j in range(2):
                a, b = 2 * j, 2 * j + 1
                t = 4 * i + TL["ffn1"]
                hi_part(i + UN["ffn1"] // 4 + 1, a)
                act.wait_ge(acc_free, t + a + 1)
                act.activation(T[:, a, 4:4 + S], T[:, a, 4:4 + S], ACT.Silu).then_inc(act_done, 1)
                hi_part(i + UN["ffn1"] // 4 + 1, b)
                act.wait_ge(prod, 2 * i + j + 1)
                act.activation(HH[:, bass.ds(2 * i + j, 1), :], T[:, b, 4:4 + S], ACT.Copy).then_inc(act_done, 1)

        def swiglu_last(i):
            for j in range(2):
                a, b = 2 * j, 2 * j + 1
                t = 4 * i + TL["ffn1"]
                hi_next(UN["ffn1"] + 4 * i + a)
                act.wait_ge(acc_free, t + a + 1)
                act.activation(T[:, a, 4:4 + S], T[:, a, 4:4 + S], ACT.Silu).then_inc(act_done, 1)
                hi_next(UN["ffn1"] + 4 * i + b)
                act.wait_ge(prod, 2 * i + j + 1)
                act.activation(HH[:, 2 * i + j, :], T[:, b, 4:4 + S], ACT.Copy).then_inc(act_done, 1)

        rstd(R[:, :], 2, 1.0 / D, PS[:, SCO, :])
        with act.Fori(0, KF // 2 - 1) as i:
            swiglu_group(i)
        swiglu_last(KF // 2 - 1)
        for c in range(KD):
            for j in range(3):
                hi_next(UN["down1"] + 3 * c + j)
            a = TL["down1"] + c
            act.wait_ge(acc_free, a + 1)
            if c >= 4:
                act.wait_ge(low_done, L0["down1"] + c - 3)
            act.activation(grid3(tile_t(a), "perm"), perm_of(X[:, c, :]), ACT.Copy,
                           scale=GG[:, c:c + 1]).then_inc(xg_ready, 1)
            act.wait_ge(xg_ready, c + 1)
            act.activation(XH[:, c, :], tile_t(a), ACT.Copy).then_inc(act_done, 1)
            act.wait_ge(ss_done, 16 + 2 * c)
            act.activation(SQ[:, 0, :], X[:, c, :], ACT.Square).then_inc(sq_ready, 1)
            act.activation(SQ[:, 1, :], X[:, c, :], ACT.Square, scale=vcol("final_norm_g", c)).then_inc(sq_ready, 1)

        rstd(R[:, :], 3, 1.0 / D, PS[:, SCO, :])
        act.wait_ge(r_mix, 2)
        act.activation(RP[:, :], SQ[:, 0, :], ACT.Ln, bias=BT[:, 0:1], scale=1.0 / D).then_inc(ln_done, 1)
        act.wait_ge(ln_done, 4)
        act.activation(RP[:, :], RP[:, :], ACT.Exp, scale=-0.5).then_inc(r_ready, 1)
        for i in range(8):
            a = TL["cab"] + i
            hi_next(UN["cab"] + i)
            act.wait_ge(acc_free, a + 1)
            func = ACT.Sigmoid if i % 2 else ACT.Identity
            act.activation(tile_t(a), tile_t(a), func,
                           bias=vcol("b_in_2", (12 if i % 2 == 0 else 16) + i // 2)).then_inc(act_done, 1)
            if i == 3:
                act.wait_ge(bias_in, 16 * 16)
                for r in range(ROWS):
                    act.activation(BN[:, :, :].rearrange("p h (g r c) -> p h g r c", r=ROWS, c=8)[:, :, :, r, :],
                                   BNR[:, r, :, :].rearrange("p h (g c) -> p h g c", c=8),
                                   ACT.Copy).then_inc(bias_ready, 1)
        v_parts("v3", M2, 0)
        for i in range(2):
            qk_part("na", TL["na0"] + i, 0, i, na_bias(i, 0))
            hi_next(UN["na0"] + i)
        attention("na")
        for c in range(6, KD):
            gate_part(c)
            hi_next(UN["gates_b"] + c)
        for c in range(KD):
            act.wait_ge(act_done, H0["gates_b"] + c + 1)
            act.activation(SG[:, gate_place(c), :], SG[:, gate_place(c), :], ACT.Sigmoid).then_inc(gate_ready, 1)
        with act.Fori(0, 2) as i:
            for s in range(4):
                hi_part(i + UN["gates_a"] // 4 + 1, s)
                act.wait_ge(acc_free, 4 * i + s + TL["gates_a"] + 1)
                act.activation(SG[:, bass.ds(4 * i + s, 1), :], T[:, s, 4:4 + S], ACT.Sigmoid,
                               bias=VEC[:, bass.ds(4 * i + s + vec_at["b_in_2"] + 20, 1)]).then_inc(act_done, 1)
        for c in range(4):
            hi_next(UN["na_out"] + c)
            if c == 0:
                for k in range(4):
                    act.wait_ge(ln_d, k + 1)
                    if k >= 2:
                        act.wait_ge(ss_done, 32 + k - 1)
                    act.activation(LSQ[:, k % 2, :], Y[k], ACT.Square).then_inc(sq_ready, 1)
        act.wait_ge(ln_ps, 2)
        act.activation(LR[:, :], PS[:, SCO + 1, :], ACT.Ln, bias=BT[:, 0:1], scale=1.0 / S).then_inc(ln_r, 1)
        act.wait_ge(ln_r, 1)
        act.activation(LR[:, :], LR[:, :], ACT.Exp, scale=-0.5).then_inc(ln_r, 1)
        for k in range(4):
            act.wait_ge(ln_n, k + 1)
            act.activation(Y[k], Y[k], ACT.Silu, scale=vcol("conv_ln_g_2", k),
                           bias=vcol("conv_ln_b_2", k)).then_inc(silu_done, 1)
            act.wait_ge(silu_done, k + 1)
            act.activation(CH[:, k, :], Y[k], ACT.Copy).then_inc(ch_done, 1)
        for c in range(8):
            if c % 2:
                hi_next(UN["conv_out"] + c // 2)
            act.wait_ge(merged, c + 1)
            act.activation(MH2[:, c, :], tile_t(TL["conv_out"] + c), ACT.Copy).then_inc(act_done, 1)
        residual_tiles("out2", "norm2_g_2", 36, lambda c: [UN["out2"] + c])
        rstd(R[:, :], 5, 1.0 / D, PS[:, SCO, :])

        def geglu_group(i, static):
            for j in range(2):
                for v in range(2):
                    s = 2 * j + v
                    if static:
                        hi_next(UN["ffn2"] + 4 * i + s)
                        wcol = vcol("ffn_dw_w_2", 44 + 22 * v + 2 * i + j)
                        bcol = vcol("ffn_dw_b_2", 22 * v + 2 * i + j)
                    else:
                        hi_part(i + UN["ffn2"] // 4 + 1, s)
                        wcol = VEC[:, bass.ds(2 * i + j + vec_at["ffn_dw_w_2"] + 44 + 22 * v, 1)]
                        bcol = VEC[:, bass.ds(2 * i + j + vec_at["ffn_dw_b_2"] + 22 * v, 1)]
                    act.wait_ge(acc_free, 4 * i + s + TL["ffn2"] + 1)
                    if not (static and i == 0):
                        act.wait_ge(low_done, 2 * i + j + L0["ffn2"] - 1)
                    act.activation(CZ[j][v][:, :], T[:, s, 4:4 + S], ACT.Identity, scale=wcol, bias=bcol).then_inc(cz_mid, 1)
                act.wait_ge(cz_taps, 4 * i + 2 * j + 1)
                act.activation(CZ[j][0][:, :], CZ[j][0][:, :], ACT.Gelu).then_inc(gelu_done, 1)
                act.wait_ge(glu_ready, 2 * i + j + 1)
                dst = HH[:, 2 * i + j, :] if static else HH[:, bass.ds(2 * i + j, 1), :]
                act.activation(dst, CZ[j][1][:, :], ACT.Copy).then_inc(hid_hi, 1)

        geglu_group(0, True)
        with act.Fori(1, KF // 2 - 1) as i:
            geglu_group(i, False)
        geglu_group(KF // 2 - 1, True)
        for c in range(KD):
            for j in range(3):
                hi_next(UN["down2"] + 3 * c + j)
            act.wait_ge(acc_free, TL["down2"] + c + 1)
            if c >= 2:
                act.wait_ge(ss_done, 44 + c - 1)
            act.activation(SQ[:, c % 2, :], X[:, c, :], ACT.Square).then_inc(sq_ready, 1)
        rstd(R[:, :], 6, 1.0 / D, PS[:, SCO, :])

    @block.vector
    def _(dve):
        made = [0]

        def step(ins):
            made[0] += 1
            ins.then_inc(dve_made, 1)
            dve.wait_ge(dve_made, made[0])

        def tile_t(a, n=S):
            return T[:, a % 4, 4:4 + n]

        def ps(a, n=S):
            return PS[:, ACC + a % 2, 0:n]

        def tile_ready(name, i):
            if name == "init":
                dve.wait_ge(part_ready, i + 1)
            elif name[0] == "v":
                half, t = i // 4, i % 4
                if t < 3:
                    dve.wait_ge(part_ready, PT0[name] + 3 * half + t + 1)
                else:
                    dve.wait_ge(w_used, UN[name] + 2 * half + 2)
            elif name in ("out1", "na_out", "conv_out"):
                if i % 2 == 0:
                    dve.wait_ge(part_ready, PT0[name] + i // 2 + 1)
                else:
                    dve.wait_ge(w_used, UN[name] + i // 2 + 1)
            elif name[:4] == "down":
                dve.wait_ge(w_used, UN[name] + 3 * i + 3)
            else:
                dve.wait_ge(w_used, UN[name] + i + 1)

        def slots_drained(name):
            dve.wait_ge(act_done, H0[name])
            dve.wait_ge(low_done, L0[name])

        step(dve.memset(BT[:, :], EPS))
        step(dve.memset(T[:, :, 0:4], 0.0))
        step(dve.memset(T[:, :, 516:520], 0.0))
        step(dve.memset(CR[:, :].bitcast(F32), 0.0))
        dve.wait_ge(pool_made, 18)
        step(dve.tensor_copy(IDB[:, :], IDF[:, :]))
        step(dve.tensor_copy(CMB[:, :], CST[:, :]))
        step(dve.tensor_copy(SEL[:, :], SELF[:, :]))
        step(dve.tensor_copy(CR[64:65, :], POS[64:65, :]))

        def add_square(k, i, which=0, slot=0, total=None, squares=SQ):
            total = SS[:, which, :] if total is None else total
            dve.wait_ge(sq_ready, k)
            if i == 0:
                dve.tensor_copy(total, squares[:, slot, :]).then_inc(ss_done, 1)
            else:
                dve.wait_ge(ss_done, k - 1)
                dve.tensor_tensor(total, total, squares[:, slot, :], ALU.add).then_inc(ss_done, 1)

        def low_of_gain(name, gain, c):
            dve.wait_ge(act_done, H0[name] + c + 1)
            dve.scalar_tensor_tensor(out=XL[:, c, :], in0=X[:, c, :], scalar=vcol(gain, c), in1=XH[:, c, :].bitcast(F32),
                                     op0=ALU.mult, op1=ALU.subtract).then_inc(low_done, 1)

        for c in range(KD):
            tile_ready("init", c)
            dve.tensor_copy(X[:, c, :], PS[:, TRB + c % 2, :]).then_inc(acc_free, 1)
            if c == 1:
                dve.wait_ge(rpb_in, 16 * RPR)
                dve.tensor_scalar(RPP[:, :], RPP[:, :], -1.0, None, ALU.mult).then_inc(rpb_negated, 1)
            if c == 0:
                dve.wait_ge(vec_t, 1)
                dve.tensor_copy(VEC[:, :], PS[:, OB, 0:n_vec]).then_inc(vec_ready, 1)
                dve.wait_ge(vec_ready, 1)
            else:
                low_of_gain("init", "mix_norm_g", c - 1)
                add_square(c, c - 1, 0, (c - 1) % 2)
        low_of_gain("init", "mix_norm_g", KD - 1)
        add_square(KD, KD - 1, 0, 1)
        dve.wait_ge(wf_split, 1)
        dve.tensor_tensor(WFL[:, :, :], WFR[:, :, :], WFH[:, :, :].bitcast(F32), ALU.subtract).then_inc(wf_split, 1)
        def rt_copy(k):
            dve.wait_ge(rt_ps, k)
            dve.tensor_copy(RT[:, :], PS[:, SCO + 1, :].rearrange("p (t q) -> p t q", q=P)[:, :, 0]).then_inc(rt_ready, 1)
            dve.wait_ge(rt_ready, k)

        def v_take(name, i, bias=False):
            a, c0, t = TL[name] + i, 256 * (i // 4), i % 4
            tile_ready(name, i)
            if i >= 4:
                dve.wait_ge(low_done, L0[name] + i - 3)
            if bias:
                dve.scalar_tensor_tensor(out=tile_t(a, 256), in0=ps(a, 256), scalar=RT[:, t:t + 1],
                                         in1=BVB[:, c0:c0 + 256], op0=ALU.mult, op1=ALU.add).then_inc(acc_free, 1)
            else:
                dve.tensor_scalar(tile_t(a, 256), ps(a, 256), RT[:, t:t + 1], None, ALU.mult).then_inc(acc_free, 1)

        def v_phase(name, mem, bias, extra=None, taken=0):
            if taken == 0:
                slots_drained(name)
            for i in range(8 + 1):
                if taken <= i < 8:
                    v_take(name, i, bias)
                if i >= 1:
                    a, c0, t = TL[name] + i - 1, 256 * ((i - 1) // 4), (i - 1) % 4
                    dve.wait_ge(act_done, H0[name] + i)
                    dve.tensor_tensor(mem["VL"][:, t, c0:c0 + 256], tile_t(a, 256), mem["VH"][:, t, c0:c0 + 256].bitcast(F32),
                                      ALU.subtract).then_inc(low_done, 1)
                if extra:
                    extra(i)

        def qk_take(name, i, r):
            tile_ready(name, i)
            qk_scale(TL[name] + i, i, r, name == "na0")

        def qk_scale(a, i, r, negate):
            if i % 2 == 0:
                ins = dve.scalar_tensor_tensor(out=tile_t(a), in0=ps(a), scalar=(-1 if negate else 1) * HD ** -0.5, in1=r, op0=ALU.mult, op1=ALU.mult)
            else:
                ins = dve.tensor_tensor(tile_t(a), ps(a), r, ALU.mult)
            ins.then_inc(acc_free, 1)

        def qk_low(name, i, par, mem, pair=None, a=None):
            a = TL[name] + i if a is None else a
            hi, lo = (mem["QH"], mem["QL"]) if i % 2 == 0 else (mem["KH"], mem["KL"])
            dve.wait_ge(act_done, H0[name] + i + 1)
            if pair is None:
                ins = dve.tensor_tensor(lo[:, par, :], tile_t(a), hi[:, par, :].bitcast(F32), ALU.subtract)
            else:
                b = B8[:, pair:pair + 1] if i % 2 == 0 else vcol("b_in_2", 4 + pair)
                ins = dve.scalar_tensor_tensor(out=lo[:, par, :], in0=tile_t(a), scalar=b, in1=hi[:, par, :].bitcast(F32),
                                               op0=ALU.add, op1=ALU.subtract)
            ins.then_inc(low_done, 1)

        def log_forget(i):
            if i == 1:
                dve.wait_ge(fl_ps, 1)
                for t in range(TC):
                    dve.scalar_tensor_tensor(out=Z[:, 0, 8 * t:8 * t + 8], in0=PS[:, TRB, 8 * t:8 * t + 8],
                                             scalar=RT[:, t:t + 1], in1=BFG[:, :], op0=ALU.mult,
                                             op1=ALU.add).then_inc(fl_step, 1)
                dve.wait_ge(fl_step, 6)
                dve.scalar_tensor_tensor(out=Z[:, 1, :], in0=Z[:, 0, :], scalar=-1.0, in1=Z[:, 0, :], op0=ALU.mult,
                                         op1=ALU.max).then_inc(fl_step, 1)
                dve.tensor_scalar(Z[:, 3, :], Z[:, 0, :], 0.0, None, ALU.min).then_inc(fl_step, 1)

        slots_drained("fox0")
        for i in range(2):
            if i == 0:
                dve.wait_ge(r_ready, 1)
            qk_take("fox0", i, R[:, :])
        rt_copy(1)
        for i in range(2):
            qk_low("fox0", i, 0, M1)
        dve.wait_ge(consts_in, 16 * 5)
        for i in range(2):
            dve.tensor_tensor_reduce(out=LAMV[:, 2 * i, :], in0=LAMV[:, 2 * i, :], in1=LAMV[:, 2 * i + 1, :], scale=1.0,
                                     scalar=0.0, op0=ALU.mult, op1=ALU.add, accum_out=LAM[:, i:i + 1]).then_inc(fl_step, 1)
        step(dve.tensor_tensor(GG[:, :], vcol("final_norm_g", 0, 8), vcol("norm1_g_2", 0, 8), ALU.mult))
        step(dve.tensor_scalar(B8[:, :], vcol("b_in_2", 0, 4), -HD ** -0.5, None, ALU.mult))
        step(dve.tensor_scalar(GD[:, :], vcol("diff_norm_g", 0), 1.0 - LAM_INIT, None, ALU.mult))
        step(dve.tensor_copy(TRI[:, :], STG[:, :]))
        step(dve.memset(LFH[:, :, :].bitcast(F32), 0.0))
        step(dve.memset(LFL[:, :, :].bitcast(F32), 0.0))
        v_phase("v1", M1, False, log_forget)
        dve.wait_ge(fl_act, 1)
        dve.tensor_tensor(LAM[:, 4:5], LAM[:, 3:4], LAM[:, 2:3], ALU.subtract).then_inc(lam_ready, 1)
        dve.wait_ge(lam_ready, 1)
        dve.tensor_scalar(LAM[:, 5:6], LAM[:, 4:5], LAM_INIT, None, ALU.subtract).then_inc(lam_ready, 1)
        dve.wait_ge(fl_act, 3)
        dve.tensor_tensor(Z[:, 2, :], Z[:, 2, :], Z[:, 3, :], ALU.subtract).then_inc(fl_step, 1)
        dve.wait_ge(fl_step, 9)
        nlf = Z[:, 2, :].rearrange("p (t h) -> p t h", h=8)
        for i, c in enumerate((0, 32)):
            dve.tensor_copy(LFH[:, :, c:c + 8], nlf).then_inc(fl_step, 1)
            dve.wait_ge(fl_step, 10 + i)
            dve.tensor_tensor(LFL[:, :, c:c + 8], nlf, LFH[:, :, c:c + 8].bitcast(F32), ALU.subtract).then_inc(lf_ready, 1)
        dve.wait_ge(cum_ps, 1)
        dve.tensor_copy(RI[:, 0:1], BT[:, :]).then_inc(cr_dve, 1)
        dve.wait_ge(cr_act, 2)
        dve.tensor_tensor(CR[32:40, :], PS[32:40, TRB + 1, :], CT[32:40, :].bitcast(F32), ALU.subtract).then_inc(cr_dve, 1)
        dve.wait_ge(rpb_out, 16 * 8)

        def fill_take(it, kind, r):
            what, i, a = it["what"], it["idx"], it["a"]
            if what == "qk":
                if it["ends"]:
                    dve.wait_ge(w_used, it["unit"] + 1)
                users = [x for x in fill_plan(kind) if x["what"] == "qk" and x["a"] < a and x["a"] % 4 == a % 4]
                if users:
                    dve.wait_ge(low_done, L0[FAM[kind]["fill"]] + users[-1]["idx"] + 1)
                qk_scale(a, i, r, kind == "na")
            elif what == "v":
                if i == 0:
                    slots_drained("v2")
                v_take("v2", i)
            elif what == "gb":
                gate_take(i)
            else:
                if it["ends"]:
                    dve.wait_ge(w_used, it["unit"] + 1)
                else:
                    dve.wait_ge(part_ready, it["part"])
                dve.tensor_tensor(X[:, i, :], ps(a), X[:, i, :], ALU.add).then_inc(acc_free, 1)

        def gate_take(c):
            a = TL["gates_b"] + c
            dve.wait_ge(w_used, UN["gates_b"] + c + 1)
            if c < 4:
                dve.wait_ge(low_done, L0["gates_b"])
            else:
                dve.wait_ge(act_done, H0["gates_b"] + c - 3)
            dve.tensor_tensor(grid3(tile_t(a), "natural"), natural_of(ps(a)), grid3(RN2, "natural"),
                              ALU.mult).then_inc(acc_free, 1)

        def attention(kind, r, behind=None):
            f = FAM[kind]
            sc, tr, ready_after = family(kind)
            mem, s0, t0, o0, name = f["mem"], f["s0"], f["t0"], f["o0"], f["fill"]
            n = len(sc)
            late = []
            slots_drained(name)
            for i in range(n + 4):
                if i < n:
                    hd, half, qb = sc[i]
                    g = s0 + i
                    k0, k1 = keys_of(kind, qb)
                    w = (k1 - k0) * P
                    dve.wait_ge(sc_ready, g + 1)
                    src = PS[:, SCO + g % 2, 0:w]
                    if kind == "na":
                        if slot_free(kind, i):
                            dve.wait_ge(tr_ready, slot_free(kind, i))
                        first = 2 * 8 * ROWS if qb == 0 else 0
                        bias = BN[:, hd, first:first + w]
                        dve.wait_ge(exp_ready, g - 3)
                        dve.tensor_tensor_reduce(out=PR[:, g % 4, 0:w], in0=src, in1=bias, scale=1.0,
                                                 scalar=-NEG, op0=ALU.add, op1=ALU.min,
                                                 accum_out=NM[:, g % 4:g % 4 + 1]).then_inc(max_ready, 1)
                    elif g >= 4:
                        dve.wait_ge(exp_ready, g - 3)
                    if kind != "na":
                        dve.tensor_reduce(NM[:, g % 4:g % 4 + 1], src, AX, ALU.max, negate=True).then_inc(max_ready, 1)
                if 1 <= i <= n:
                    g = s0 + i - 1
                    hd, half, qb = sc[i - 1]
                    k0, k1 = keys_of(kind, qb)
                    w = (k1 - k0) * P
                    dve.wait_ge(exp_ready, g + 1)
                    if g >= 4:
                        dve.wait_ge(p_ready, t0 if i - 1 < 4 else slot_free(kind, i - 1))
                    dve.reciprocal(RI[:, g % 4:g % 4 + 1], RS[:, g % 4:g % 4 + 1]).then_inc(rinv_done, 1)
                    ri = RI[:, g % 4:g % 4 + 1]
                    if kind == "diff" and half == 1:
                        dve.wait_ge(rinv_done, g + 1)
                        dve.tensor_tensor(ri, ri, LAM[:, 5:6], ALU.mult).then_inc(lam_ready, 1)
                        dve.wait_ge(lam_ready, 2 + i // 2)
                        dve.wait_ge(p_half, i // 2)
                        dve.scalar_tensor_tensor(out=PR[:, (g - 1) % 4, 0:w], in0=PR[:, g % 4, 0:w], scalar=ri,
                                                 in1=PR[:, (g - 1) % 4, 0:w], op0=ALU.mult,
                                                 op1=ALU.add).then_inc(p_ready, 1)
                    else:
                        dve.wait_ge(rinv_done, g + 1)
                        dve.tensor_scalar(PR[:, g % 4, 0:w], PR[:, g % 4, 0:w], ri, None,
                                          ALU.mult).then_inc(p_half if kind == "diff" else p_ready, 1)
                for it in fills_done(kind, i):
                    fill_take(it, kind, r)
                if i - 2 in ready_after:
                    j = ready_after[i - 2]
                    hd, qb = tr[j]
                    g = t0 + j
                    k0, k1 = keys_of(kind, qb)
                    dve.wait_ge(pth_done, g + 1)
                    q = slice(qb * P, (qb + 1) * P)
                    dve.tensor_tensor(mem["PTL"][:, k0:k1, q],
                                      PS[:, TRB + g % 2, 0:(k1 - k0) * P].rearrange("p (k q) -> p k q", q=P),
                                      mem["PTH"][:, k0:k1, q].bitcast(F32), ALU.subtract).then_inc(ptl_done, 1)
                for it in fills_done(kind, i):
                    if it["what"] == "qk":
                        fl = it["idx"]
                        qk_low(name, fl, parity_of_filler(kind, fl), mem, fl // 2 + 1 if kind == "na" else None, it["a"])
                if behind:
                    behind(i)
                for hd in late:
                    dve.wait_ge(od_r, 2 * hd + 2)
                    dve.tensor_tensor(OD[:, :], OD[:, :], SQ[:, 1, :], ALU.mult).then_inc(od_scaled, 1)
                    dve.wait_ge(oh_done, o0 + hd + 1)
                    dve.scalar_tensor_tensor(out=ML[:, 4 + hd, :], in0=OD[:, :], scalar=GD[:, 0:1],
                                             in1=MH[:, 4 + hd, :].bitcast(F32), op0=ALU.mult,
                                             op1=ALU.subtract).then_inc(o_free, 1)
                late = []
                if i - 3 in ready_after and ready_after[i - 3] % 4 == 3:
                    hd = ready_after[i - 3] // 4
                    bank = PS[:, OB + (o0 + hd) % 2, :]
                    if kind == "diff":
                        dve.wait_ge(pv_ready, o0 + hd + 1)
                        if hd:
                            dve.wait_ge(o_free, o0 + hd)
                        dve.tensor_copy(OD[:, :], bank).then_inc(od_copy, 1)
                        dve.wait_ge(od_copy, hd + 1)
                        dve.tensor_tensor(SQ[:, 0, :], OD[:, :], OD[:, :], ALU.mult).then_inc(od_sq, 1)
                        late = [hd]
                    else:
                        dve.wait_ge(oh_done, o0 + hd + 1)
                        rr = slice((hd % 2) * HD, (hd % 2) * HD + HD)
                        if kind == "fox":
                            dve.tensor_tensor(ML[rr, hd // 2, :], bank[rr, :], MH[rr, hd // 2, :].bitcast(F32),
                                              ALU.subtract).then_inc(o_free, 1)
                        else:
                            dve.tensor_tensor(grid3(NAL[rr, hd // 2, :], "natural"), natural_of(bank[rr, :]),
                                              grid3(NAH[rr, hd // 2, :].bitcast(F32), "natural"),
                                              ALU.subtract).then_inc(o_free, 1)

        attention("fox", R[:, :])
        v_take("v2", 3)
        v_phase("v2", M1, False, taken=4)
        attention("diff", R[:, :])

        def clause(dst, src, op, bound):
            step(dve.tensor_scalar(MKS[:, dst, :], src, bound, None, op))

        def combine(dst, other, op):
            step(dve.tensor_tensor(MKS[:, dst, :], MKS[:, dst, :], MKS[:, other, :], op))

        def as_mask(m):
            step(dve.tensor_scalar(NMB[:, m, :], MKS[:, 1, :], NEG, -NEG, ALU.mult, ALU.add))

        def window_masks(part):
            diff_, keyc = MKS[:, 0, :], KC[:, :]
            if part == 0:
                step(dve.tensor_scalar(QI[:, 1:2], QI[:, 0:1], 7, None, ALU.bitwise_and))
                step(dve.tensor_copy(QC[:, :], QI[:, 1:2]))
                step(dve.tensor_scalar(QC[64:128, :], QC[64:128, :], 8.0, None, ALU.add))
                step(dve.tensor_scalar(diff_, KC[:, :], QC[:, 0:1], None, ALU.subtract))
            elif part == 1:
                clause(1, diff_, ALU.is_ge, 8.0)
                clause(2, diff_, ALU.is_le, 23.0)
                combine(1, 2, ALU.mult)
                as_mask(0)
            elif part == 2:
                clause(1, diff_, ALU.is_ge, -8.0)
                clause(2, diff_, ALU.is_le, 7.0)
                clause(3, keyc, ALU.is_le, 15.0)
                combine(2, 3, ALU.max)
                combine(1, 2, ALU.mult)
                as_mask(1)
            elif part == 3:
                clause(1, diff_, ALU.is_ge, 8.0)
                clause(3, keyc, ALU.is_ge, 16.0)
                combine(1, 3, ALU.max)
                clause(2, diff_, ALU.is_le, 23.0)
                combine(1, 2, ALU.mult)
                as_mask(2)

        def residual(name, gain, sq0, behind=None):
            for c in range(KD + 1):
                if c < KD:
                    tile_ready(name, c)
                    dve.tensor_tensor(X[:, c, :], ps(TL[name] + c), X[:, c, :], ALU.add).then_inc(acc_free, 1)
                if c:
                    low_of_gain(name, gain, c - 1)
                    add_square(sq0 + c, c - 1, 0, (c - 1) % 2)
                if behind:
                    behind(c)

        residual("out1", "ffn_norm_g", 8, lambda c: window_masks(c // 2) if c % 2 == 0 else None)

        def swiglu_low(q, dst, src, b):
            dve.wait_ge(act_done, 2 * q + 2 + H0["ffn1"])
            dve.tensor_tensor(dst, T[:, b, 4:4 + S], src.bitcast(F32), ALU.subtract).then_inc(low_done, 1)

        def swiglu_pair(i, j, first):
            q = 2 * i + j
            for v in range(2):
                s = 2 * j + v
                dve.wait_ge(w_used, 4 * i + s + UN["ffn1"] + 1)
                if not first:
                    dve.wait_ge(low_done, q - 1 + L0["ffn1"])
                src = PS[:, early_bank(s) if first else ACC + s % 2, :]
                dve.tensor_tensor(T[:, s, 4:4 + S], src, R[:, :], ALU.mult).then_inc(acc_free, 1)
                if v == 0 and not (first and j == 0):
                    if isinstance(i, int):
                        swiglu_low(q - 1, HL[:, q - 1, :], HH[:, q - 1, :], (s - 1) % 4)
                    else:
                        swiglu_low(q - 1, HL[:, bass.ds(q - 1, 1), :], HH[:, bass.ds(q - 1, 1), :], (s - 1) % 4)
            dve.wait_ge(act_done, 4 * i + 2 * j + 1 + H0["ffn1"])
            dve.wait_ge(acc_free, 4 * i + 2 * j + 2 + TL["ffn1"])
            dve.tensor_tensor(T[:, 2 * j + 1, 4:4 + S], T[:, 2 * j + 1, 4:4 + S], T[:, 2 * j, 4:4 + S],
                              ALU.mult).then_inc(prod, 1)

        dve.wait_ge(r_ready, 2)
        for j in range(2):
            swiglu_pair(0, j, True)
        with dve.Fori(1, KF // 2) as i:
            for j in range(2):
                swiglu_pair(i, j, False)
        swiglu_low(KF - 1, HL[:, KF - 1, :], HH[:, KF - 1, :], 3)

        for c in range(KD + 1):
            if c < KD:
                tile_ready("down1", c)
                dve.tensor_tensor(X[:, c, :], ps(TL["down1"] + c), X[:, c, :], ALU.add).then_inc(acc_free, 1)
            if c:
                k = c - 1
                dve.wait_ge(act_done, H0["down1"] + k + 1)
                dve.tensor_tensor(XL[:, k, :], tile_t(TL["down1"] + k), XH[:, k, :].bitcast(F32),
                                  ALU.subtract).then_inc(low_done, 1)
                add_square(16 + 2 * k + 1, k, 0, 0)
                add_square(16 + 2 * k + 2, k, 1, 1)
        dve.wait_ge(r_ready, 3)
        dve.wait_ge(norm_ps, 4)
        dve.tensor_tensor(SQ[:, 0, :], PS[:, SCO + 1, :], R[:, :], ALU.mult).then_inc(r_mix, 1)
        dve.wait_ge(r_mix, 1)
        dve.tensor_tensor(SQ[:, 0, :], SQ[:, 0, :], R[:, :], ALU.mult).then_inc(r_mix, 1)
        dve.wait_ge(r_ready, 4)
        dve.tensor_tensor(RN2, R[:, :], RP[:, :], ALU.mult).then_inc(r_mix, 1)
        dve.wait_ge(r_mix, 3)
        dve.tensor_copy(grid3(RP[:, :], "perm"), perm_of(RN2)).then_inc(r_mix, 1)

        slots_drained("cab")
        step(dve.memset(U[:, :, 0:UO], 0.0))
        step(dve.memset(U[:, :, UO + S:UW], 0.0))
        for i in range(8 + 1):
            if i < 8:
                a = TL["cab"] + i
                tile_ready("cab", i)
                if i >= 4:
                    dve.wait_ge(low_done, L0["cab"] + (i - 4) // 2 + 1)
                src = PS[:, early_bank(i), :] if i < 4 else ps(a)
                dve.tensor_tensor(grid3(tile_t(a), "natural"), natural_of(src), grid3(RN2, "natural"),
                                  ALU.mult).then_inc(acc_free, 1)
                dve.scalar_tensor_tensor(out=X[:, i, :], in0=X[:, i, :], scalar=vcol("final_norm_g", i), in1=R[:, :],
                                         op0=ALU.mult, op1=ALU.mult).then_inc(x1_done, 1)
            if i >= 2 and i % 2 == 0:
                c, a = i // 2 - 1, TL["cab"] + i - 1
                dve.wait_ge(act_done, H0["cab"] + i)
                dve.tensor_tensor(U[:, c, UO:UO + S], tile_t(a - 1), tile_t(a), ALU.mult).then_inc(low_done, 1)

        dve.wait_ge(x1_done, KD)
        early = 6
        taps = [(t, c) for t in range(early) for c in range(3)]
        taps += [(t - early * (c == 3), c) for t in range(early, TAPS) for c in range(4)]
        taps += [(t, 3) for t in range(TAPS - early, TAPS)]
        assert sorted(taps) == [(t, c) for t in range(TAPS) for c in range(4)]
        n_taps = [0]

        def conv_taps(n):
            for k in range(n_taps[0], min(n_taps[0] + n, len(taps))):
                n_taps[0] += 1
                t, c = taps[k]
                src = U[:, c, UO - TAPS // 2 + t:UO - TAPS // 2 + t + S]
                w = vcol("conv_dw_w_2", 4 * t + c)
                if t == 0:
                    dve.wait_ge(low_done, L0["v3"])
                    if c == 3:
                        dve.wait_ge(acc_free, TL["v3"] + 8)
                    dve.tensor_scalar(Y[c], src, w, vcol("conv_dw_b_2", c), ALU.mult, ALU.add).then_inc(conv_done, 1)
                else:
                    dve.wait_ge(conv_done, taps.index((t - 1, c)) + 1)
                    dve.scalar_tensor_tensor(out=Y[c], in0=src, scalar=w, in1=Y[c], op0=ALU.mult,
                                             op1=ALU.add).then_inc(conv_done, 1)

        rt_copy(2)
        dve.wait_ge(bv_in, 16)
        v_phase("v3", M2, True, lambda i: conv_taps(2))
        dve.wait_ge(bias_ready, ROWS)
        for part in ("PTH", "PTL"):
            step(dve.memset(M2[part][:, 1, 3 * P:S].bitcast(F32), 0.0))
        slots_drained("na0")
        for i in range(2):
            qk_take("na0", i, RP[:, :])
            qk_low("na0", i, 0, M2, 0)
        attention("na", RP[:, :], lambda i: conv_taps(1 + i % 2 if i < N_SCORES - 8 else 3))
        for c in range(6, KD):
            gate_take(c)
            conv_taps(4)
        for i in range(8):
            a = TL["gates_a"] + i
            tile_ready("gates_a", i)
            dve.wait_ge(act_done, H0["gates_a"] + i - 3)
            dve.tensor_tensor(grid3(tile_t(a), "natural"), natural_of(ps(a)), grid3(RN2, "natural"),
                              ALU.mult).then_inc(acc_free, 1)
            conv_taps(4)
        conv_taps(len(taps))
        dve.wait_ge(conv_done, len(taps))
        dve.tensor_tensor(LSUM[:, :], Y[0], Y[1], ALU.add).then_inc(ln_sum, 1)
        for k in (2, 3):
            dve.wait_ge(ln_sum, k - 1)
            dve.tensor_tensor(LSUM[:, :], LSUM[:, :], Y[k], ALU.add).then_inc(ln_sum, 1)

        def na_out_take(c):
            tile_ready("na_out", c)
            if c == 0:
                dve.wait_ge(act_done, H0["na_out"])
            dve.tensor_tensor(SG[:, c, :], ps(TL["na_out"] + c), SG[:, c, :], ALU.mult).then_inc(acc_free, 1)

        na_out_take(0)
        na_out_take(1)
        dve.wait_ge(ln_ps, 1)
        for k in range(4):
            dve.scalar_tensor_tensor(out=Y[k], in0=PS[:, SCO, :], scalar=-1.0 / S, in1=Y[k], op0=ALU.mult,
                                     op1=ALU.add).then_inc(ln_d, 1)
        na_out_take(2)
        na_out_take(3)
        for k in range(4):
            add_square(32 + k + 1, k, 0, k % 2, LSUM[:, :], LSQ)
        na_out_take(4)
        na_out_take(5)
        dve.wait_ge(ln_r, 2)
        for k in range(4):
            dve.tensor_tensor(Y[k], Y[k], LR[:, :], ALU.mult).then_inc(ln_n, 1)
        na_out_take(6)
        na_out_take(7)
        for k in range(4):
            dve.wait_ge(ch_done, k + 1)
            dve.tensor_tensor(CL[:, k, :], Y[k], CH[:, k, :].bitcast(F32), ALU.subtract).then_inc(cl_done, 1)
        for c in range(8 + 1):
            if c < 8:
                a = TL["conv_out"] + c
                tile_ready("conv_out", c)
                if c >= 4:
                    dve.wait_ge(low_done, L0["conv_out"] + c - 3)
                if c == 0:
                    dve.wait_ge(gate_ready, KD)
                dve.tensor_tensor(tile_t(a), ps(a), SG[:, gate_place(c), :], ALU.mult).then_inc(acc_free, 1)
                dve.wait_ge(acc_free, a + 1)
                dve.tensor_tensor(tile_t(a), tile_t(a), SG[:, c, :], ALU.add).then_inc(merged, 1)
            if c:
                a = TL["conv_out"] + c - 1
                dve.wait_ge(act_done, H0["conv_out"] + c)
                dve.tensor_tensor(ML2[:, c - 1, :], tile_t(a), MH2[:, c - 1, :].bitcast(F32),
                                  ALU.subtract).then_inc(low_done, 1)
        dve.wait_ge(x1_done, 8)
        residual("out2", "norm2_g_2", 36)

        def geglu_low(q, dst, src, j):
            dve.wait_ge(hid_hi, q + 1)
            dve.tensor_tensor(dst, CZ[j][1][:, :], src.bitcast(F32), ALU.subtract).then_inc(low_done, 1)

        def geglu_pair(i, j, first):
            q = 2 * i + j
            static = isinstance(i, int)
            for v in range(2):
                s = 2 * j + v
                dve.wait_ge(w_used, 4 * i + s + UN["ffn2"] + 1)
                if not first:
                    dve.wait_ge(cz_taps, 4 * i + s - 3)
                src = PS[:, early_bank(s) if first else ACC + s % 2, :]
                dve.tensor_tensor(T[:, s, 4:4 + S], src, R[:, :], ALU.mult).then_inc(acc_free, 1)
                if v == 0 and not (first and j == 0):
                    if static:
                        geglu_low(q - 1, HL[:, q - 1, :], HH[:, q - 1, :], 1 - j)
                    else:
                        geglu_low(q - 1, HL[:, bass.ds(q - 1, 1), :], HH[:, bass.ds(q - 1, 1), :], 1 - j)
                z = CZ[j][v][:, :]

                def w(tap):
                    c = 2 * i + (j + vec_at["ffn_dw_w_2"] + 2 * KF * tap + KF * v)
                    return VEC[:, c:c + 1] if static else VEC[:, bass.ds(c, 1)]

                dve.wait_ge(cz_mid, 4 * i + s + 1)
                dve.scalar_tensor_tensor(out=z, in0=T[:, s, 3:3 + S], scalar=w(0), in1=z, op0=ALU.mult,
                                         op1=ALU.add).then_inc(cz_tap, 1)
                dve.wait_ge(cz_tap, 4 * i + s + 1)
                dve.scalar_tensor_tensor(out=z, in0=T[:, s, 5:5 + S], scalar=w(2), in1=z, op0=ALU.mult,
                                         op1=ALU.add).then_inc(cz_taps, 1)
            dve.wait_ge(gelu_done, q + 1)
            dve.wait_ge(cz_taps, 4 * i + 2 * j + 2)
            dve.tensor_tensor(CZ[j][1][:, :], CZ[j][1][:, :], CZ[j][0][:, :], ALU.mult).then_inc(glu_ready, 1)

        dve.wait_ge(r_ready, 5)
        slots_drained("ffn2")
        for j in range(2):
            geglu_pair(0, j, True)
        with dve.Fori(1, KF // 2) as i:
            for j in range(2):
                geglu_pair(i, j, False)
        geglu_low(KF - 1, HL[:, KF - 1, :], HH[:, KF - 1, :], 1)

        for c in range(KD + 1):
            if c < KD:
                a = TL["down2"] + c
                tile_ready("down2", c)
                dve.tensor_tensor(X[:, c, :], ps(a), X[:, c, :], ALU.add).then_inc(acc_free, 1)
                dve.wait_ge(acc_free, a + 1)
                dve.tensor_scalar(YF[:, c, :], X[:, c, :], vcol("norm_f_g_2", c), None, ALU.mult).then_inc(low_done, 1)
            if c:
                add_square(44 + c, c - 1, 0, (c - 1) % 2)
        rt_copy(3)
        for g in range(8):
            t, half = g // 2, g % 2
            dve.wait_ge(out_ps, g + 1)
            dve.tensor_scalar(OUT[:, t, half * S:half * S + S], PS[:, 4 + g % 4, :], RT[:, t:t + 1], None,
                              ALU.mult).then_inc(out_ready, 1)

    ctx.close()


_INS = {"x": (S, D), "w_in": None, "b_forget": (8,), "lambda_q1": (HD,), "lambda_k1": (HD,), "lambda_q2": (HD,),
        "lambda_k2": (HD,), "mix_norm_g": (D,), "diff_norm_g": (P,), "w_out": None, "ffn_norm_g": (D,),
        "w_gate": None, "w_up": None, "w_down": None, "final_norm_g": (D,), "norm1_g_2": (D,), "w_in_2": None,
        "b_in_2": (36 * P,), "rpb_2": (8, RPR, RPC), "w_na_out_2": None, "conv_dw_w_2": (TAPS * 4 * P,),
        "conv_dw_b_2": (4 * P,), "conv_ln_g_2": (4 * P,), "conv_ln_b_2": (4 * P,), "w_conv_out_2": None,
        "w_out_2": None, "norm2_g_2": (D,), "w_up_2": None, "ffn_dw_w_2": (3 * 2 * FF,), "ffn_dw_b_2": (2 * FF,),
        "w_down_2": None, "norm_f_g_2": (D,)}


def kernel(**inputs):
    import concourse.bacc as bacc
    from concourse.bass_utils import run_bass_kernel_spmd

    nc = bacc.Bacc("TRN2", target_bir_lowering=False, num_devices=1)
    arrays, d = {}, {}
    for name, shape in _INS.items():
        a = np.ascontiguousarray(inputs[name])
        a = a.reshape(shape or a.shape[1:])
        arrays["in_" + name] = a
        d[name] = nc.dram_tensor("in_" + name, a.shape, mybir.dt.from_np(a.dtype), kind="ExternalInput").ap()
    d["out"] = nc.dram_tensor("out_x", (S, D), F32, kind="ExternalOutput").ap()
    program(nc, d)
    r = run_bass_kernel_spmd(nc, [arrays], core_ids=[0])
    return r.results[0]["out_x"].reshape(inputs["x"].shape)
```

```python
from contextlib import ExitStack

import numpy as np

import concourse.bass as bass
from concourse import mybir

F32 = mybir.dt.float32
F32R = mybir.dt.float32r
BF16 = mybir.dt.bfloat16
I32 = mybir.dt.int32
ALU = mybir.AluOpType
ACT = mybir.ActivationFunctionType
AX = mybir.AxisListType.X

P = 128
S = 512
D = 1024
KD = D // P
TC = S // P
FF = 2816
KF = FF // P
HD = 64
EPS = 1e-6
NEG = -1e30
UNIT = 1024
LAM_INIT = 0.2
GRID = 64
ROWS = S // GRID
RH, CW = 8, 16
RPR, RPC = 2 * RH - 1, 2 * CW - 1
TAPS = 31
WIN = 48


def plan_units():
    u = []
    v = lambda m, c0: [(m, 4 * k, 4, c0 + 256 * h, 256) for h in range(2) for k in range(2)]
    col = lambda m, c0: [(m, 0, 8, c0, 128)]
    FOX_Q, FOX_K, FOX_V, DQ, DK, DV = 0, 512, 1024, 1544, 2056, 2568
    u += col("w_in", FOX_Q) + col("w_in", FOX_K)
    u += v("w_in", FOX_V)
    for j in range(1, 4):
        u += col("w_in", FOX_Q + P * j) + col("w_in", FOX_K + P * j)
    u += col("w_in", DQ) + col("w_in", DK)
    u += v("w_in", DV)
    out_a = [("w_out", 0, 4, 256 * c, 256) for c in range(4)]
    for j in range(1, 4):
        u += col("w_in", DQ + P * j) + col("w_in", DK + P * j)
        if j == 2:
            u += out_a[:1]
    u += out_a[1:]
    u += [("w_out", 4, 4, 256 * c, 256) for c in range(4)]
    marks = {"ffn1": len(u)}
    for j in range(KF):
        u += col("w_gate", P * j) + col("w_up", P * j)
    marks["down1"] = len(u)
    for c in range(KD):
        u += [("w_down", 0, 8, P * c, P), ("w_down", 8, 8, P * c, P), ("w_down", 16, 6, P * c, P)]
    NQ, NK, NV, CA, CB, GA, GB = 0, 512, 1024, 1536, 2048, 2560, 3584
    for j in range(4):
        u += col("w_in_2", CA + P * j) + col("w_in_2", CB + P * j)
    for j in range(4):
        u += col("w_in_2", NQ + P * j) + col("w_in_2", NK + P * j)
        if j == 0:
            u += v("w_in_2", NV)
    marks["gates"] = len(u)
    for c in range(KD):
        u += col("w_in_2", GB + P * c)
    for c in range(KD):
        u += col("w_in_2", GA + P * c)
    marks["na_out"] = len(u)
    u += [("w_na_out_2", 0, 4, 256 * c, 256) for c in range(4)]
    u += [("w_conv_out_2", 0, 4, 256 * c, 256) for c in range(4)]
    for c in range(KD):
        u += col("w_out_2", P * c)
    marks["ffn2"] = len(u)
    for j in range(KF):
        u += col("w_up_2", P * j) + col("w_up_2", FF + P * j)
    marks["down2"] = len(u)
    for c in range(KD):
        u += [("w_down_2", 0, 8, P * c, P), ("w_down_2", 8, 8, P * c, P), ("w_down_2", 16, 6, P * c, P)]
    marks["end"] = len(u)
    return u, marks


VECS = [("conv_dw_w_2", 4 * TAPS), ("ffn_dw_w_2", 3 * 2 * KF), ("ffn_dw_b_2", 2 * KF), ("b_in_2", 36),
        ("mix_norm_g", 8), ("ffn_norm_g", 8), ("final_norm_g", 8), ("norm1_g_2", 8), ("norm2_g_2", 8),
        ("norm_f_g_2", 8), ("conv_dw_b_2", 4), ("conv_ln_g_2", 4), ("conv_ln_b_2", 4), ("diff_norm_g", 1)]


def plan_vectors():
    at, loads, n = {}, [], 0
    for name, rows in VECS:
        at[name] = n
        done = 0
        while done < rows:
            k = min(rows - done, P - n % P)
            loads.append((name, done, k, n))
            done += k
            n += k
    return at, loads, n


def program(nc, d):
    units, marks = plan_units()
    NU = len(units)
    vec_at, vec_loads, n_vec = plan_vectors()
    ctx = ExitStack()
    base = 16512

    def at(name, off, shape, dt):
        return nc.alloc_sbuf_tensor_at(name, shape, dt, offset=base + off)

    XH = at("XH", 0, [P, KD, S], F32R)
    XL = at("XL", 16384, [P, KD, S], F32R)
    YF = at("YF", 0, [P, KD, S], F32)
    OUT = at("OUT", 16384, [P, TC, D], F32)
    WH = at("WH", 32768, [P, 4, UNIT], F32R)
    WL = at("WL", 49152, [P, 4, UNIT], F32R)
    RAW = at("RAW", 65536, [P, 2, UNIT], F32)
    X = at("X", 73728, [P, KD, S], F32)
    T = at("T", 90112, [P, 4, 520], F32)
    R = at("R", 98432, [P, S], F32)
    RP = at("RP", 100480, [P, S], F32)
    SS = at("SS", 102528, [P, 2, S], F32)
    SQ = at("SQ", 106624, [P, 2, S], F32)
    small = [110720]

    def tiny(name, shape, dt):
        n = int(np.prod(shape[1:])) * (2 if dt == BF16 else 4)
        o = small[0]
        small[0] += (n + 31) // 32 * 32
        assert small[0] <= 117760, name
        return at(name, o, shape, dt)

    PR = at("PR", 117760, [P, 4, S], F32)
    BVB = at("BVB", 102528, [P, S], F32)
    HH = at("HH", 117760, [P, KF, S], F32R)
    HL = at("HL", 117760 + 45056, [P, KF, S], F32R)
    BIG = 125952
    XTM = at("XTM", BIG, [P, TC, D], F32)
    MH = at("MH", BIG, [P, KD, S], F32R)
    ML = at("ML", BIG + 16384, [P, KD, S], F32R)

    def heads_memory(tag, o):
        return dict(VH=at("VH" + tag, o, [P, TC, S], F32R), VL=at("VL" + tag, o + 8192, [P, TC, S], F32R),
                    QH=at("QH" + tag, o + 16384, [P, 2, S], F32R), QL=at("QL" + tag, o + 20480, [P, 2, S], F32R),
                    KH=at("KH" + tag, o + 24576, [P, 2, S], F32R), KL=at("KL" + tag, o + 28672, [P, 2, S], F32R),
                    PTH=at("PTH" + tag, o + 32768, [P, TC, S], F32R), PTL=at("PTL" + tag, o + 40960, [P, TC, S], F32R))

    M1 = heads_memory("1", BIG + 32768)
    ODR = at("ODR", BIG + 8192, [P, 4, S], F32)
    ODN = at("ODN", BIG + 24576, [P, 4, S], F32)
    OF = [RP[:, :], SS[:, 1, :], SQ[:, 1, :], R[:, :]]
    CR = at("CR", BIG + 81920, [P, S], F32R)
    TRI = at("TRI", BIG + 65536, [P, 896], F32R)
    LFH = at("LFH", BIG + 65536 + 3584, [P, TC, P], F32R)
    LFL = at("LFL", BIG + 65536 + 5632, [P, TC, P], F32R)
    CT = at("CT", BIG + 73728, [P, S], F32R)
    STG = at("STG", BIG + 73728 + 2048, [P, 896], F32)
    ROWV = at("ROWV", 117760, [P, 4, P], F32)
    WFR = at("WFR", 119808, [P, KD, 8], F32)
    WFH = at("WFH", 120064, [P, KD, 8], F32R)
    WFL = at("WFL", 120320, [P, KD, 8], F32R)
    Z = at("Z", 120576, [P, 4, TC * 8], F32)
    LAMV = at("LAMV", 121088, [P, 4, HD], F32)
    MKS = at("MKS", 100480, [P, 4, 384], F32)
    FLR = at("FLR", 122112, [P, S], F32)
    KC = at("KC", BIG + 83968, [P, 384], F32)
    NAH = at("NAH", BIG, [P, 4, S], F32R)
    NAL = at("NAL", BIG + 8192, [P, 4, S], F32R)
    BN = at("BN", BIG + 16384, [P, 8, WIN * ROWS], F32)
    BNR = at("BNR", BIG + 70144, [P, ROWS, 8, WIN], F32)
    UW = 544
    UO = 16
    U = at("U", BIG + 28672, [P, 4, UW], F32)
    M2 = heads_memory("2", BIG + 37376)
    SG = at("SG", BIG + 37376, [P, 2 * KD, S], F32)
    LSQ = at("LSQ", BIG + 70144, [P, 2, S], F32)
    LSUM = at("LSUM", BIG + 70144 + 4096, [P, S], F32)
    LR = at("LR", BIG + 70144 + 6144, [P, S], F32)
    CH = at("CH", BIG + 28672, [P, 4, S], F32R)
    CL = at("CL", BIG + 78336, [P, 4, S], F32R)
    MH2 = at("MH2", BIG - 8192, [P, KD, S], F32R)
    ML2 = at("ML2", BIG + 8192, [P, KD, S], F32R)

    IDF = tiny("IDF", [P, P], F32)
    ONE = tiny("ONE", [P, P], F32)
    IDB = tiny("IDB", [P, P], BF16)
    CMB = tiny("CMB", [P, P], BF16)
    NMB = tiny("NMB", [P, 3, 384], BF16)
    VEC = tiny("VEC", [P, n_vec], F32)
    SELF = tiny("SELF", [P, 12], F32)
    SEL = tiny("SEL", [P, 12], F32R)
    BFG = tiny("BFG", [P, 8], F32)
    NM = tiny("NM", [P, 4], F32)
    RS = tiny("RS", [P, 4], F32)
    RI = tiny("RI", [P, 4], F32)
    RT = tiny("RT", [P, TC], F32)
    LAM = tiny("LAM", [P, 8], F32)
    GG = tiny("GG", [P, 8], F32)
    B8 = tiny("B8", [P, 4], F32)
    GD = tiny("GD", [P, 1], F32)
    QC = tiny("QC", [P, 1], F32)
    QI = tiny("QI", [P, 2], I32)
    BT = tiny("BT", [P, 1], F32)
    RPP = at("RPP", BIG + 79872, [P, GRID], F32)
    CST = at("CST", BIG + 79360, [P, P], F32)
    POS = at("POS", BIG + 32768 + 7680, [P, S], F32)
    CZ = [[at("CZ00", 100480, [P, S], F32), at("CZ01", 104576, [P, S], F32)],
          [at("CZ10", 106624, [P, S], F32), at("CZ11", 108672, [P, S], F32)]]
    SHIFT = 56
    scratch = nc.dram_tensor("rpb_shifted", [8, 8 * RPR, SHIFT], F32, kind="Internal").ap()

    Y = [SQ[:, 0, :], SQ[:, 1, :], R[:, :], SS[:, 0, :]]
    RN2 = SS[:, 1, :]

    PS = ctx.enter_context(nc.psum_tensor("PS", [P, 8, S], F32))
    ACC, SCO, TRB, OB = 0, 2, 4, 6

    def vcol(name, c, n=1):
        return VEC[:, vec_at[name] + c:vec_at[name] + c + n]

    sems = {}

    def sem(name):
        sems[name] = ctx.enter_context(nc.semaphore(name))
        return sems[name]

    x_in = sem("x_in")
    consts_in = sem("consts_in")
    rows_in = sem("rows_in")
    wf_in = sem("wf_in")
    rpb_in = sem("rpb_in")
    rpb_negated = sem("rpb_negated")
    rpb_out = sem("rpb_out")
    bias_in = sem("bias_in")
    bias_ready = sem("bias_ready")
    bv_in = sem("bv_in")
    w_landed = [sem(f"w_landed{i}") for i in range(2)]
    w_hi = sem("w_hi")
    w_lo = sem("w_lo")
    w_used = sem("w_used")
    pool_made = sem("pool_made")
    dve_made = sem("dve_made")
    vec_t = sem("vec_t")
    vec_ready = sem("vec_ready")
    part_ready = sem("part_ready")
    acc_free = sem("acc_free")
    prod = sem("prod")
    act_done = sem("act_done")
    low_done = sem("low_done")
    sq_ready = sem("sq_ready")
    ss_done = sem("ss_done")
    norm_ps = sem("norm_ps")
    ln_done = sem("ln_done")
    r_ready = sem("r_ready")
    rt_ps = sem("rt_ps")
    rt_ready = sem("rt_ready")
    r_mix = sem("r_mix")
    fl_ps = sem("fl_ps")
    fl_row = sem("fl_row")
    fl_step = sem("fl_step")
    fl_act = sem("fl_act")
    lf_ready = sem("lf_ready")
    cum_ps = sem("cum_ps")
    cr_act = sem("cr_act")
    cr_dve = sem("cr_dve")
    wf_split = sem("wf_split")
    sc_ready = sem("sc_ready")
    xg_ready = sem("xg_ready")
    merged = sem("merged")
    cz_mid = sem("cz_mid")
    cz_tap = sem("cz_tap")
    cz_taps = sem("cz_taps")
    gelu_done = sem("gelu_done")
    glu_ready = sem("glu_ready")
    hid_hi = sem("hid_hi")
    x1_done = sem("x1_done")
    lam_ready = sem("lam_ready")
    max_ready = sem("max_ready")
    exp_ready = sem("exp_ready")
    rinv_done = sem("rinv_done")
    p_half = sem("p_half")
    p_ready = sem("p_ready")
    tr_ready = sem("tr_ready")
    pth_done = sem("pth_done")
    ptl_done = sem("ptl_done")
    pv_ready = sem("pv_ready")
    oh_done = sem("oh_done")
    o_free = sem("o_free")
    od_copy = sem("od_copy")
    od_sum = sem("od_sum")
    od_sq = sem("od_sq")
    od_ps = sem("od_ps")
    od_r = sem("od_r")
    od_scaled = sem("od_scaled")
    conv_done = sem("conv_done")
    gate_ready = sem("gate_ready")
    ln_sum = sem("ln_sum")
    ln_ps = sem("ln_ps")
    ln_d = sem("ln_d")
    ln_r = sem("ln_r")
    ln_n = sem("ln_n")
    silu_done = sem("silu_done")
    ch_done = sem("ch_done")
    cl_done = sem("cl_done")
    out_ps = sem("out_ps")
    out_ready = [sem("out_ready_dve"), sem("out_ready_act")]
    stored = sem("stored")

    def perm_of(ap):
        return ap.rearrange("p (r g c) -> p g r c", r=ROWS, c=8)

    def natural_of(ap):
        return ap.rearrange("p (g r c) -> p r g c", r=ROWS, c=8)

    def grid3(ap, order):
        a, b = (GRID // 8, ROWS) if order == "perm" else (ROWS, GRID // 8)
        return ap.rearrange("p (a b c) -> p a b c", a=a, b=b)

    TL = {}
    n_tile = 0
    for name, n in [("init", 8), ("fox0", 2), ("v1", 8), ("foxf", 8), ("v2", 8), ("difff", 14), ("out1", 8),
                    ("ffn1", 44), ("down1", 8), ("cab", 8), ("na0", 2), ("v3", 8), ("naf", 6), ("gates_b", 8),
                    ("gates_a", 8),
                    ("na_out", 8), ("conv_out", 8), ("out2", 8), ("ffn2", 44), ("down2", 8)]:
        TL[name] = n_tile
        n_tile += n
    UN = {"fox0": 0, "v1": 2, "foxf": 6, "v2": 14, "difff": 18, "out1": 28, "ffn1": marks["ffn1"],
          "down1": marks["down1"], "cab": marks["down1"] + 24, "na0": marks["down1"] + 32,
          "v3": marks["down1"] + 34, "naf": marks["down1"] + 38, "gates_b": marks["gates"], "gates_a": marks["gates"] + 8,
          "na_out": marks["na_out"], "conv_out": marks["na_out"] + 4, "out2": marks["na_out"] + 8,
          "ffn2": marks["ffn2"], "down2": marks["down2"]}
    assert UN["out1"] + 4 == UN["ffn1"] and UN["naf"] + 6 == UN["gates_b"]

    PT0, n_part = {}, 0
    for name in TL:
        PT0[name] = n_part
        n_part += {"init": 8, "v": 6, "difff": 4, "out1": 4, "na_out": 4, "conv_out": 4}.get("v" if name[0] == "v" else name, 0)

    per = {"init": (8, 8), "v1": (8, 8), "fox0": (2, 2), "foxf": (8, 8), "v2": (8, 8), "difff": (6, 6),
           "out1": (8, 8), "ffn1": (44, 22), "down1": (8, 8), "cab": (8, 4), "v3": (8, 8), "na0": (2, 2),
           "naf": (6, 6), "gates_b": (8, 0), "gates_a": (8, 0), "na_out": (0, 0), "conv_out": (8, 8), "out2": (8, 8),
           "ffn2": (0, 22), "down2": (0, 9)}
    H0, L0 = {}, {}
    h = l = 0
    for name in TL:
        H0[name], L0[name] = h, l
        h += per[name][0]
        l += per[name][1]

    def src_of(spec):
        m, k0, nk, c0, nc_ = spec
        return d[m].rearrange("(k p) n -> p k n", p=P)[:, k0:k0 + nk, c0:c0 + nc_]

    block = ctx.enter_context(nc.Block())

    @block.sync
    def _(sp):
        def load(n, s, src, width=UNIT, ncols=P):
            u = 4 * n + s
            if not (isinstance(n, int) and u < 2):
                sp.wait_ge(w_lo, u - 1)
            dst = RAW[:, s % 2, 0:width].rearrange("p (k n) -> p k n", n=ncols)
            sp.dma_start(dst, src).then_inc(w_landed[s % 2], 16)

        def load_units(lo, hi):
            for u in range(lo, hi):
                m, k0, nk, c0, ncol = units[u]
                load(u // 4, u % 4, src_of(units[u]), nk * ncol, ncol)

        load_units(0, 2)
        for t in range(TC):
            sp.dma_start(XTM[:, t, :], d["x"][t * P:(t + 1) * P, :]).then_inc(x_in, 16)
        for name, r0, k, n in vec_loads:
            sp.dma_start(ROWV[n % P:n % P + k, n // P, :],
                          d[name].rearrange("(a b) -> a b", b=P)[r0:r0 + k, :]).then_inc(rows_in, 16)
        sp.dma_start(WFR[:, :, :], d["w_in"].rearrange("(k p) n -> p k n", p=P)[:, :, 1536:1544]).then_inc(wf_in, 16)
        load_units(2, 4)
        sp.dma_start(BFG[:, :], d["b_forget"].partition_broadcast(P)).then_inc(consts_in, 16)
        for i, name in enumerate(("lambda_q1", "lambda_k1", "lambda_q2", "lambda_k2")):
            sp.dma_start(LAMV[:, i, :], d[name].partition_broadcast(P)).then_inc(consts_in, 16)
        load_units(4, 6)
        sp.wait_ge(pool_made, 1)
        for o in range(RPR):
            sp.dma_start(RPP[8 * o:8 * o + 8, 16:16 + RPC], d["rpb_2"][:, o, :]).then_inc(rpb_in, 16)
        sp.wait_ge(rpb_negated, 1)
        for cq in range(8):
            sp.dma_start(scratch[cq], RPP[0:8 * RPR, 7 - cq:7 - cq + SHIFT]).then_inc(rpb_out, 16)
        load_units(6, marks["ffn1"])

        def looped(lo, count, mats):
            with sp.Fori(0, count) as i:
                for s, (m, off, step) in enumerate(mats):
                    src = d[m].rearrange("(k p) n -> p k n", p=P)[:, 0:KD, bass.ds(i * step + off, P)]
                    load(i + lo // 4, s, src)

        looped(marks["ffn1"], KF // 2, [("w_gate", 0, 256), ("w_up", 0, 256), ("w_gate", P, 256), ("w_up", P, 256)])
        load_units(marks["down1"], marks["down1"] + 28)
        sp.wait_ge(w_used, UN["down1"] + 24)
        sp.wait_ge(rpb_out, 16 * 8)
        for gq in range(2):
            for qr in range(ROWS):
                off = (RH - 1 - qr) * 8 * SHIFT + 8 - 8 * gq
                src = bass.AP(tensor=scratch.tensor, offset=off,
                              ap=[[8 * RPR * SHIFT, 8], [SHIFT, ROWS * 8], [1, WIN]])
                q0 = gq * 64 + qr * 8
                sp.dma_start(BNR[q0:q0 + 8, :, :, :].rearrange("p r h c -> p (r h) c"), src).then_inc(bias_in, 16)
        sp.wait_ge(norm_ps, 4)
        sp.dma_start(BVB[:, :], d["b_in_2"][1024:1536].partition_broadcast(P)).then_inc(bv_in, 16)
        load_units(marks["down1"] + 28, UN["gates_a"])
        looped(UN["gates_a"], 2, [("w_in_2", 2560 + P * s, 512) for s in range(4)])
        load_units(marks["na_out"], marks["ffn2"])
        looped(marks["ffn2"], KF // 2, [("w_up_2", 0, 256), ("w_up_2", FF, 256), ("w_up_2", P, 256), ("w_up_2", FF + P, 256)])
        load_units(marks["down2"], NU)
        for t in range(TC):
            for half in range(2):
                sp.wait_ge(out_ready[half], t + 1)
            sp.dma_start(d["out"][t * P:(t + 1) * P, :], OUT[:, t, :]).then_inc(stored, 16)
        sp.wait_ge(stored, 16 * TC)

    @block.gpsimd
    def _(pool):
        made = [0]

        def step(ins, wait=True):
            made[0] += 1
            ins.then_inc(pool_made, 1)
            if wait:
                pool.wait_ge(pool_made, made[0])

        step(pool.memset(RPP[:, :], 0.0))
        step(pool.memset(IDF[:, :], 0.0))
        step(pool.affine_select(out=IDF[:, :], in_=IDF[:, :], compare_op=ALU.not_equal, fill=1.0, base=0,
                                pattern=[[-1, P]], channel_multiplier=1))
        step(pool.memset(ONE[:, :], 1.0))
        step(pool.memset(SELF[:, :], 0.0))
        for b in (0, -32):
            step(pool.affine_select(out=SELF[:, 0:8], in_=SELF[:, 0:8], compare_op=ALU.not_equal, fill=1.0, base=b,
                                    pattern=[[-1, 8]], channel_multiplier=1))
        for j in range(4):
            step(pool.memset(SELF[64:65, 8 + j:9 + j], 2.0 ** (-2 * (j + 1))))
        step(pool.memset(STG[:, :], 0.0))
        step(pool.affine_select(out=STG[:, :], in_=STG[:, :], compare_op=ALU.is_gt, fill=1.0, base=384,
                                pattern=[[-1, 896]], channel_multiplier=1))
        step(pool.memset(CST[:, :], 0.0))
        step(pool.affine_select(out=CST[:, :], in_=CST[:, :], compare_op=ALU.is_ge, fill=NEG, base=0,
                                pattern=[[-1, P]], channel_multiplier=1))
        step(pool.iota(POS[:, :], [[1, S]], base=0, channel_multiplier=0, allow_small_or_imprecise_dtypes=True))
        step(pool.iota(KC[:, :].rearrange("p (g r c) -> p g r c", g=6, r=ROWS), [[8, 6], [0, ROWS], [1, 8]], base=0,
                       channel_multiplier=0, allow_small_or_imprecise_dtypes=True))
        step(pool.iota(QI[:, 0:1], [[0, 1]], base=0, channel_multiplier=1))

        def lo_part(n, s, width=UNIT):
            u = 4 * n + s
            pool.wait_ge(w_hi, u + 1)
            if not (isinstance(n, int) and n == 0):
                pool.wait_ge(w_used, u - 3)
            pool.tensor_tensor(WL[:, s, 0:width], RAW[:, s % 2, 0:width], WH[:, s, 0:width].bitcast(F32),
                               ALU.subtract).then_inc(w_lo, 1)

        def lo_parts(g0, g1):
            if g0 == 0:
                for s in range(4):
                    lo_part(0, s)
                g0 = 1
            with pool.Fori(g0, g1) as i:
                for s in range(4):
                    lo_part(i, s)

        def lo_down(u0):
            for u in range(u0, u0 + 24):
                lo_part(u // 4, u % 4, units[u][2] * P)

        lo_parts(0, marks["down1"] // 4)
        lo_down(marks["down1"])
        lo_parts(marks["down1"] // 4 + 6, marks["down2"] // 4)
        lo_down(marks["down2"])

    NA_KEYS = [(0, 2), (0, 3), (1, 4), (2, 4)]

    def family(kind):
        if kind == "diff":
            sc = [(hd, comp, qb) for hd in range(4) for qb in range(4) for comp in range(2)]
            tr = [(hd, qb) for hd in range(4) for qb in range(4)]
            ready_after = {2 * i + 1: i for i in range(16)}
        else:
            sc = [(hd, hd % 2, qb) for hd in range(8) for qb in range(4)]
            tr = [(hd, qb) for hd in range(8) for qb in range(4)]
            ready_after = {i: i for i in range(32)}
        return sc, tr, ready_after

    FAM = {"fox": dict(mem=M1, fill="foxf", v="v1", s0=0, t0=0, o0=0),
           "diff": dict(mem=M1, fill="difff", v="v2", s0=32, t0=32, o0=8),
           "na": dict(mem=M2, fill="naf", v="v3", s0=64, t0=48, o0=12)}
    N_SCORES = 32
    LAST_STEP = N_SCORES + 4

    def fill_plan(kind):
        items = []

        def add(what, idx, a, unit, s0, s1, ends=True, part=0):
            items.append(dict(what=what, idx=idx, a=a, unit=unit, s0=s0, s1=s1, ends=ends, part=part))

        a, u = TL[FAM[kind]["fill"]], UN[FAM[kind]["fill"]]
        qk_steps = [(max(4 * f - 1, 0), 4 * f + 2) for f in range(8)]
        if kind == "fox":
            for f in range(8):
                add("qk", f, a + f, u + f, *qk_steps[f])
            for i in range(3):
                add("v", i, TL["v2"] + i, UN["v2"], N_SCORES + i, N_SCORES + i, False, PT0["v2"] + i + 1)
        elif kind == "na":
            for f in range(6):
                add("qk", f, a + f, u + f, *qk_steps[f])
            for c in range(6):
                s0 = N_SCORES - 8 + 2 * c
                add("gb", c, TL["gates_b"] + c, UN["gates_b"] + c, s0, min(s0 + 1, N_SCORES + 2))
        else:
            order = [("qk", 0, 0, 2), ("qk", 1, 3, 6), ("qk", 2, 7, 9), ("qk", 3, 10, 12), ("oa", 0, 13, 13),
                     ("oa", 1, 14, 14), ("qk", 4, 15, 18), ("qk", 5, 19, 22), ("oa", 2, 24, 26), ("oa", 3, 27, 29),
                     ("oa", 4, 30, 32), ("oa", 5, 33, 34), ("oa", 6, 35, 35), ("oa", 7, LAST_STEP, LAST_STEP)]
            for what, idx, s0, s1 in order:
                ends = what == "qk" or idx % 2 == 1
                add(what, idx, a, u, s0, s1, ends, PT0["difff"] + idx // 2 + 1)
                a += 1
                u += ends
        return items

    def fills_done(kind, step):
        return [it for it in fill_plan(kind) if it["s1"] == step]

    def fill_chunks(it, step, n):
        k = it["s1"] - it["s0"] + 1
        i = step - it["s0"]
        return range(n * i // k, n * (i + 1) // k)

    def gate_place(c):
        return KD + 2 * c if c < 4 else KD + 1 + 2 * (c - 4)

    def init_bank(c):
        return (3, 4, 5, 6, 7, 3, 4, 5)[c]

    def out_bank(t, half):
        return (3, 1, 4, 5)[t] if half else 4 + t

    def early_bank(s):
        return (ACC, ACC + 1, OB, OB + 1)[s]

    def keys_of(kind, qb):
        return NA_KEYS[qb] if kind == "na" else (0, qb + 1)

    def pair_index(kind, hd):
        return hd if kind == "diff" else hd // 2

    def slot_free(kind, i):
        t0 = FAM[kind]["t0"]
        if i < 4:
            return t0
        return t0 + ((i - 4) // 2 + 1 if kind == "diff" else i - 3)

    def parity_of_filler(kind, f):
        return (f // 2 + 1) % 2

    @block.tensor
    def _(pe):
        def mm3(out, ah, al, bh, bl, start, stop):
            pe.matmul(out, ah, bh, start=start, stop=False)
            pe.matmul(out, ah, bl, start=False, stop=False)
            return pe.matmul(out, al, bh, start=False, stop=stop)

        def need_acc(a):
            if not (isinstance(a, int) and a < 2):
                pe.wait_ge(acc_free, a - 1)

        def fm_chunks(n, s, bank, k0, ks, bh, bl, start, stop, ncols=P, c0=0):
            for k in ks:
                w0 = k * ncols + c0
                ins = mm3(PS[:, ACC + bank, :], WH[:, s, w0:w0 + P], WL[:, s, w0:w0 + P],
                          bh[:, k0 + k, :], bl[:, k0 + k, :], start and k == ks[0], stop and k == ks[-1])
            return ins

        def fm_tile(n, s, a, bh=XH, bl=XL, bank=None):
            pe.wait_ge(w_lo, 4 * n + s + 1)
            need_acc(a)
            bank = s % 2 if bank is None else bank
            fm_chunks(n, s, bank, 0, range(KD), bh, bl, True, True).then_inc(w_used, 1)

        def first_pair(u, a, bh, bl, chunk_ready):
            for s in range(2):
                need_acc(a + s)
            pe.wait_ge(w_lo, u + 2)
            for k in range(KD):
                chunk_ready(k)
                for s in range(2):
                    ins = fm_chunks((u + s) // 4, (u + s) % 4, s, 0, [k], bh, bl, k == 0, k == KD - 1)
                    if k == KD - 1:
                        ins.then_inc(w_used, 1)

        def low(base):
            return lambda k: pe.wait_ge(low_done, base + k + 1)

        def v_tile(name, i):
            half, t, a = i // TC, i % TC, TL[name] + i
            pe.wait_ge(w_lo, UN[name] + 2 * half + 2)
            need_acc(a)
            for k in range(KD):
                u = UN[name] + 2 * half + k // 4
                w = slice((k % 4) * 256, (k % 4) * 256 + 256)
                ins = mm3(PS[:, ACC + a % 2, 0:256], XH[:, k, t * P:(t + 1) * P], XL[:, k, t * P:(t + 1) * P],
                          WH[:, u % 4, w], WL[:, u % 4, w], k == 0, k == KD - 1)
            if t == TC - 1:
                ins.then_inc(w_used, 2)
            else:
                ins.then_inc(part_ready, 1)

        def norm_sum(ss, which=0):
            pe.wait_ge(ss_done, ss)
            pe.matmul(PS[:, SCO + which, :], ONE[:, :], SS[:, which, :], start=True, stop=True).then_inc(norm_ps, 1)

        def rt_transposes(src):
            for t in range(TC):
                ins = pe.transpose(PS[:, SCO + 1, t * P:(t + 1) * P], src[:, t * P:(t + 1) * P], IDF[:, :])
            ins.then_inc(rt_ps, 1)

        pe.wait_ge(pool_made, 4)
        for i in range(44):
            pe.transpose(PS[:, ACC, 0:P], IDF[:, :], IDF[:, :])
        pe.wait_ge(x_in, 16 * TC)
        for c in range(KD):
            if c == 3:
                pe.wait_ge(rows_in, 16 * len(vec_loads))
                for i in range(4):
                    r = min(P, n_vec - i * P)
                    ins = pe.transpose(PS[:, OB + 1, i * P:i * P + r], ROWV[0:r, i, :], IDF[0:r, 0:r])
                ins.then_inc(vec_t, 1)
            if c == 4:
                pe.wait_ge(vec_ready, 1)
            elif c > 4:
                pe.wait_ge(acc_free, c - 4)
            for t in range(TC):
                ins = pe.transpose(PS[:, init_bank(c), t * P:(t + 1) * P], XTM[:, t, c * P:(c + 1) * P], IDF[:, :])
            ins.then_inc(part_ready, 1)
        pe.wait_ge(w_lo, 2)
        for k in range(KD):
            pe.wait_ge(low_done, k + 1)
            for i in range(2):
                ins = fm_chunks(0, i, i, 0, [k], XH, XL, k == 0, k == KD - 1)
                if k == KD - 1:
                    ins.then_inc(w_used, 1)
        norm_sum(8)
        pe.wait_ge(wf_split, 2)
        pe.wait_ge(acc_free, TL["fox0"])
        for k in range(KD):
            ins = mm3(PS[0:8, TRB, :], WFH[:, k, :], WFL[:, k, :], XH[:, k, :], XL[:, k, :], k == 0, k == KD - 1)
        ins.then_inc(fl_ps, 1)
        pe.wait_ge(r_ready, 1)
        rt_transposes(R)
        v_tile("v1", 0)
        pe.wait_ge(fl_row, 1)
        for t in range(TC):
            ins = pe.transpose(PS[:, TRB + 1, 8 * t:8 * t + 8], FLR[0:8, t * P:(t + 1) * P], IDF[0:8, 0:8])
        ins.then_inc(fl_ps, 1)
        for i in range(1, 6):
            v_tile("v1", i)
        pe.wait_ge(lf_ready, 2)
        for t in range(TC):
            for i, part in enumerate((LFH, LFL)):
                ins = pe.matmul(PS[:, TRB + 1, :], part[:, t, :], TRI[:, 384 - P * t:896 - P * t],
                                start=(t == 0 and i == 0), stop=(t == TC - 1 and i == 1))
        ins.then_inc(cum_ps, 1)
        for i in range(6, 8):
            v_tile("v1", i)

        def attention(kind):
            f = FAM[kind]
            sc, tr, ready_after = family(kind)
            mem, s0, t0, o0 = f["mem"], f["s0"], f["t0"], f["o0"]
            first_low = L0[f["fill"]]

            def scores(i):
                hd, half, qb = sc[i]
                g = s0 + i
                pair = pair_index(kind, hd)
                pe.wait_ge(low_done, first_low + 2 * pair if pair else L0[f["v"]])
                if g >= 2:
                    pe.wait_ge(exp_ready, g - 1)
                if i == 0 and kind == "fox":
                    pe.wait_ge(cr_act, 2)
                    pe.wait_ge(cr_dve, 2)
                k0, k1 = keys_of(kind, qb)
                n = (k1 - k0) * P
                wide = max(n, 256)
                out = PS[:, SCO + g % 2, 0:wide]
                r = slice(half * HD, half * HD + HD)
                q = slice(qb * P, qb * P + P)
                ks = slice(k0 * P, k0 * P + wide)
                par = pair % 2
                pe.matmul(out, mem["QH"][r, par, q], mem["KH"][r, par, ks], start=True, stop=False)
                pe.matmul(out, mem["QH"][r, par, q], mem["KL"][r, par, ks], start=False, stop=False)
                pe.matmul(out, mem["QL"][r, par, q], mem["KH"][r, par, ks], start=False, stop=False)
                if kind == "na":
                    m = {0: 1, 1: 0, 2: 0, 3: 2}[qb]
                    ins = pe.matmul(out, IDB[:, :], NMB[:, m, 0:n], start=False, stop=True)
                else:
                    c = hd if kind == "fox" else 8 + hd
                    col = SEL[:, c:c + 1]
                    sel = bass.AP(tensor=col.tensor, offset=col.offset, ap=[list(col.ap[0]), [0, P]])
                    pe.matmul(out, sel, CR[:, 0:wide], start=False, stop=False)
                    ins = pe.matmul(PS[:, SCO + g % 2, n - P:n], IDB[:, :], CMB[:, :], start=False, stop=True)
                ins.then_inc(sc_ready, 1)

            def transposes(j):
                hd, qb = tr[j]
                g = t0 + j
                pe.wait_ge(p_ready, g + 1)
                if g >= 2:
                    pe.wait_ge(ptl_done, g - 1)
                k0, k1 = keys_of(kind, qb)
                i = [k for k, v in ready_after.items() if v == j][0]
                slot = (s0 + i - (1 if kind == "diff" else 0)) % 4
                for k in range(k1 - k0):
                    ins = pe.transpose(PS[:, TRB + g % 2, k * P:(k + 1) * P], PR[:, slot, k * P:(k + 1) * P], IDF[:, :])
                ins.then_inc(tr_ready, 1)

            def pv(hd):
                g = o0 + hd
                pe.wait_ge(ptl_done, t0 + 4 * hd + 4)
                if kind == "diff" and hd >= 2:
                    pe.wait_ge(od_sum, hd - 1)
                elif g >= 2:
                    pe.wait_ge(o_free, g - 1)
                vc = slice(hd * P, hd * P + P) if kind == "diff" else slice((hd // 2) * P, (hd // 2) * P + P)
                for n, kc in enumerate((1, 0, 2, 3) if kind == "na" else range(4)):
                    qs = [qb for qb in range(4) if keys_of(kind, qb)[0] <= kc < keys_of(kind, qb)[1]]
                    if len(qs) == 1:
                        qs = [qs[0] - 1] + qs
                    q = slice(0, S) if n == 0 else slice(qs[0] * P, (qs[-1] + 1) * P)
                    ins = mm3(PS[:, OB + g % 2, q], mem["VH"][:, kc, vc], mem["VL"][:, kc, vc],
                              mem["PTH"][:, kc, q], mem["PTL"][:, kc, q], n == 0, n == 3)
                ins.then_inc(pv_ready, 1)

            def odsum(hd):
                pe.wait_ge(od_sq, hd + 1)
                g = o0 + hd
                pe.matmul(PS[:, OB + g % 2, :], ONE[:, :], SQ[:, 0, :], start=True, stop=True).then_inc(od_ps, 1)

            def outputs(i):
                if kind == "diff" and i - 5 in ready_after and ready_after[i - 5] % 4 == 3:
                    odsum(ready_after[i - 5] // 4)
                if i - 4 in ready_after and ready_after[i - 4] % 4 == 3:
                    pv(ready_after[i - 4] // 4)

            n = len(sc)
            for i in range(LAST_STEP + 1):
                if i < n:
                    scores(i)
                if i >= n:
                    outputs(i)
                for it in fill_plan(kind):
                    if not it["s0"] <= i <= it["s1"]:
                        continue
                    if it["what"] == "v":
                        v_tile("v2", it["idx"])
                        continue
                    u, bank = it["unit"], it["a"] % 2
                    if i == it["s0"]:
                        pe.wait_ge(w_lo, u + 1)
                        need_acc(it["a"])
                    if it["what"] == "oa":
                        ks = fill_chunks(it, i, 4)
                        ins = fm_chunks(u // 4, u % 4, bank, 0, ks, MH, ML, i == it["s0"], i == it["s1"], 256,
                                        P * (it["idx"] % 2))
                    else:
                        ks = fill_chunks(it, i, KD)
                        ins = fm_chunks(u // 4, u % 4, bank, 0, ks, XH, XL, i == it["s0"], i == it["s1"])
                    if i == it["s1"]:
                        ins.then_inc(w_used if it["ends"] else part_ready, 1)
                if i < n:
                    outputs(i)
                if i - 2 in ready_after:
                    transposes(ready_after[i - 2])

        attention("fox")
        for i in range(3, 8):
            v_tile("v2", i)
        pe.wait_ge(oh_done, 8)
        pe.wait_ge(o_free, 8)
        attention("diff")

        def mixed_ready(k):
            pe.wait_ge(oh_done, 8 + k + 1)
            pe.wait_ge(o_free, 8 + k + 1)

        def half_units(name, bh, bl, k0=0, hook=None, chunk_ready=None):
            for c in range(0, 8, 2):
                u, a = UN[name] + c // 2, TL[name] + c
                pe.wait_ge(w_lo, u + 1)
                if c == 0:
                    need_acc(a)
                    need_acc(a + 1)
                    for k in range(4):
                        if chunk_ready:
                            chunk_ready(k)
                        for h in range(2):
                            ins = fm_chunks(u // 4, u % 4, h, k0, [k], bh, bl, k == 0, k == 3, 256, P * h)
                            if k == 3:
                                ins.then_inc(w_used if h else part_ready, 1)
                else:
                    for h in range(2):
                        need_acc(a + h)
                        ins = fm_chunks(u // 4, u % 4, h, k0, range(4), bh, bl, True, True, 256, P * h)
                        ins.then_inc(w_used if h else part_ready, 1)
                        if hook:
                            hook(c + h)

        half_units("out1", MH, ML, 4, chunk_ready=mixed_ready)

        def pairs_with_norm(name, ss, base):
            first_pair(UN[name], TL[name], XH, XL, low(base))
            norm_sum(ss)
            for s in range(2, 4):
                fm_tile(UN[name] // 4, s, TL[name] + s - 2, bank=early_bank(s))
            with pe.Fori(1, KF // 2) as i:
                for s in range(4):
                    fm_tile(i + UN[name] // 4, s, 4 * i + s + TL[name])

        def down(name, base, tiles=KD):
            for c in range(tiles):
                a = TL[name] + c
                for j in range(3):
                    u = UN[name] + 3 * c + j
                    pe.wait_ge(w_lo, u + 1)
                    if j == 0:
                        need_acc(a)
                    nk = units[u][2]
                    for k in range(nk):
                        if c == 0:
                            pe.wait_ge(low_done, base + 8 * j + k + 1)
                        ins = fm_chunks(u // 4, u % 4, a % 2, 8 * j, [k], HH, HL, j == 0 and k == 0, j == 2 and k == nk - 1)
                    ins.then_inc(w_used, 1)

        pairs_with_norm("ffn1", 16, L0["out1"])
        down("down1", L0["ffn1"])

        first_pair(UN["cab"], TL["cab"], XH, XL, low(L0["down1"]))
        norm_sum(32, 0)
        norm_sum(32, 1)
        for i in range(2, 8):
            u = UN["cab"] + i
            fm_tile(u // 4, u % 4, TL["cab"] + (i - 2 if i < 4 else i), bank=early_bank(i) if i < 4 else None)
        for i in range(2):
            u = UN["na0"] + i
            fm_tile(u // 4, u % 4, TL["na0"] + i)
        pe.wait_ge(r_mix, 4)
        rt_transposes(RP)
        for i in range(8):
            v_tile("v3", i)
        attention("na")
        for c in range(6, KD):
            u = UN["gates_b"] + c
            fm_tile(u // 4, u % 4, TL["gates_b"] + c)
        with pe.Fori(0, 2) as i:
            for s in range(4):
                fm_tile(i + UN["gates_a"] // 4, s, 4 * i + s + TL["gates_a"])

        def layernorm_squares(c):
            if c == 2:
                pe.wait_ge(ss_done, 36)
                pe.matmul(PS[:, SCO + 1, :], ONE[:, :], LSUM[:, :], start=True, stop=True).then_inc(ln_ps, 1)

        pe.wait_ge(ln_sum, 3)
        pe.matmul(PS[:, SCO, :], ONE[:, :], LSUM[:, :], start=True, stop=True).then_inc(ln_ps, 1)
        pe.wait_ge(oh_done, 20)
        pe.wait_ge(o_free, 20)
        half_units("na_out", NAH, NAL, hook=layernorm_squares)
        half_units("conv_out", CH, CL, chunk_ready=lambda k: pe.wait_ge(cl_done, k + 1))
        first_pair(UN["out2"], TL["out2"], MH2, ML2, low(L0["conv_out"]))
        for c in range(2, KD):
            u = UN["out2"] + c
            fm_tile(u // 4, u % 4, TL["out2"] + c, MH2, ML2)
        pairs_with_norm("ffn2", 44, L0["out2"])
        def back(t, half):
            for c in range(4):
                if t % 2 == 0:
                    pe.wait_ge(low_done, L0["down2"] + 4 * half + c + 1 + (t == 2 and half == 1 and c == 3))
                ins = pe.transpose(PS[:, out_bank(t, half), c * P:(c + 1) * P], YF[:, 4 * half + c, t * P:(t + 1) * P],
                                   IDF[:, :])
            ins.then_inc(out_ps, 1)

        def token_sums(h):
            pe.wait_ge(ss_done, 51)
            pe.wait_ge(sq_ready, 52 + h)
            for t in range(2 * h, 2 * h + 2):
                q = slice(t * P, (t + 1) * P)
                pe.matmul(PS[:, SCO, t:t + 1], SS[:, 0, q], ONE[:, 0:1], start=True, stop=False)
                ins = pe.matmul(PS[:, SCO, t:t + 1], SQ[:, 1, q], ONE[:, 0:1], start=False, stop=True)
            ins.then_inc(norm_ps, 1)

        down("down2", L0["ffn2"], KD - 1)
        for t in range(TC):
            back(t, 0)
        for h in range(2):
            a, hs = TL["down2"] + KD - 1 + h, slice(256 * h, 256 * h + 256)
            need_acc(a)
            for j in range(3):
                u = UN["down2"] + 3 * (KD - 1) + j
                pe.wait_ge(w_lo, u + 1)
                nk = units[u][2]
                for k in range(nk):
                    w = slice(k * P, k * P + P)
                    ins = mm3(PS[:, ACC + a % 2, hs], WH[:, u % 4, w], WL[:, u % 4, w], HH[:, 8 * j + k, hs],
                              HL[:, 8 * j + k, hs], j == 0 and k == 0, j == 2 and k == nk - 1)
                if h == 1:
                    ins.then_inc(w_used, 1)
                elif j == 2:
                    ins.then_inc(part_ready, 1)
                if h == 1 and j == 0:
                    token_sums(0)
                    back(0, 1)
                    pe.wait_ge(acc_free, a)
                    back(1, 1)
        token_sums(1)
        for t in (2, 3):
            pe.wait_ge(out_ready[0], t - 1)
            back(t, 1)

    @block.scalar
    def _(act):
        def hi_part(n, s, width=UNIT):
            u = 4 * n + s
            act.wait_ge(w_landed[s % 2], 16 * (2 * n + s // 2 + 1))
            if not (isinstance(n, int) and n == 0):
                act.wait_ge(w_used, u - 3)
            act.activation(WH[:, s, 0:width], RAW[:, s % 2, 0:width], ACT.Copy).then_inc(w_hi, 1)

        def hi_next(u):
            if u + 4 < NU:
                hi_part(u // 4 + 1, u % 4, units[u + 4][2] * units[u + 4][4])

        def rstd(dst, k, scale, psum):
            act.wait_ge(norm_ps, k)
            act.activation(dst, psum, ACT.Ln, bias=BT[:, 0:1], scale=scale).then_inc(ln_done, 1)
            act.wait_ge(ln_done, k)
            act.activation(dst, dst, ACT.Exp, scale=-0.5).then_inc(r_ready, 1)

        def tile_t(a, n=S):
            return T[:, a % 4, 4:4 + n]

        def gain_and_square(a, c, gain, sq0, i):
            act.activation(XH[:, c, :], X[:, c, :], ACT.Copy, scale=gain).then_inc(act_done, 1)
            if i >= 2:
                act.wait_ge(ss_done, sq0 + i - 1)
            act.activation(SQ[:, i % 2, :], X[:, c, :], ACT.Square).then_inc(sq_ready, 1)

        for s in range(2):
            hi_part(0, s)
        act.wait_ge(vec_ready, 1)
        act.wait_ge(dve_made, 1)
        for c in range(KD):
            act.wait_ge(acc_free, c + 1)
            gain_and_square(c, c, vcol("mix_norm_g", c), 0, c)
            if c in (5, 7):
                hi_part(0, 2 + c // 7)

        def v_parts(name, mem, n_pv, hook=None):
            if n_pv:
                act.wait_ge(pv_ready, n_pv)
            for i in range(8):
                a = TL[name] + i
                act.wait_ge(acc_free, a + 1)
                if hook:
                    hook(i)
                c0 = 256 * (i // 4)
                act.activation(mem["VH"][:, i % 4, c0:c0 + 256], tile_t(a, 256), ACT.Copy).then_inc(act_done, 1)
                if i % 4 == 3:
                    hi_next(UN[name] + 2 * (i // 4))
                    hi_next(UN[name] + 2 * (i // 4) + 1)

        def qk_part(kind, a, par, i, bias=None):
            buf = FAM[kind]["mem"]["QH" if i % 2 == 0 else "KH"]
            act.wait_ge(acc_free, a + 1)
            if bias is None:
                act.activation(buf[:, par, :], tile_t(a), ACT.Copy).then_inc(act_done, 1)
            else:
                act.activation(buf[:, par, :], tile_t(a), ACT.Identity, bias=bias).then_inc(act_done, 1)

        def na_bias(i, pair):
            return B8[:, pair:pair + 1] if i % 2 == 0 else vcol("b_in_2", 4 + pair)

        act.wait_ge(wf_in, 16)
        act.activation(WFH[:, :, :], WFR[:, :, :], ACT.Copy).then_inc(wf_split, 1)
        rstd(R[:, :], 1, 1.0 / D, PS[:, SCO, :])
        for i in range(2):
            hi_next(UN["fox0"] + i)
            qk_part("fox", TL["fox0"] + i, 0, i)
        def gate_logs(i):
            if i == 3:
                act.wait_ge(fl_step, 2)
                act.activation(LAM[:, 2:4], LAM[:, 0:2], ACT.Exp).then_inc(fl_act, 1)
                act.wait_ge(fl_step, 8)
                act.activation(Z[:, 2, :], Z[:, 1, :], ACT.Exp, scale=-1.0).then_inc(fl_act, 1)
                act.wait_ge(fl_act, 2)
                act.activation(Z[:, 2, :], Z[:, 2, :], ACT.Ln, bias=1.0).then_inc(fl_act, 1)

            if i == 6:
                act.wait_ge(cum_ps, 1)
                act.wait_ge(cr_dve, 1)
                act.activation(CR[0:8, :], PS[0:8, TRB + 1, :], ACT.Copy).then_inc(cr_act, 1)
                act.activation(CT[32:40, :], PS[32:40, TRB + 1, :], ACT.Copy).then_inc(cr_act, 1)

        v_parts("v1", M1, 0, gate_logs)

        def gate_part(c):
            a = TL["gates_b"] + c
            act.wait_ge(acc_free, a + 1)
            act.activation(SG[:, gate_place(c), :], tile_t(a), ACT.Identity,
                           bias=vcol("b_in_2", 28 + c)).then_inc(act_done, 1)

        def diff_hi(hd):
            act.wait_ge(od_scaled, hd + 1)
            act.activation(MH[:, 4 + hd, :], ODN[:, hd, :], ACT.Copy, scale=GD[:, 0:1]).then_inc(oh_done, 1)

        def attention(kind):
            f = FAM[kind]
            sc, tr, ready_after = family(kind)
            mem, s0, t0, o0 = f["mem"], f["s0"], f["t0"], f["o0"]
            n = len(sc)
            norm_q = []
            for i in range(LAST_STEP + 1):
                if i - 3 in ready_after:
                    j = ready_after[i - 3]
                    hd, qb = tr[j]
                    g = t0 + j
                    k0, k1 = keys_of(kind, qb)
                    act.wait_ge(tr_ready, g + 1)
                    if o0 + hd > 0:
                        act.wait_ge(pv_ready, o0 + hd)
                    act.activation(mem["PTH"][:, k0:k1, qb * P:(qb + 1) * P],
                                   PS[:, TRB + g % 2, 0:(k1 - k0) * P].rearrange("p (k q) -> p k q", q=P),
                                   ACT.Copy).then_inc(pth_done, 1)
                if i < n:
                    hd, half, qb = sc[i]
                    g = s0 + i
                    k0, k1 = keys_of(kind, qb)
                    w = (k1 - k0) * P
                    act.wait_ge(max_ready, g + 1)
                    if slot_free(kind, i):
                        act.wait_ge(tr_ready, slot_free(kind, i))
                    src = PR[:, g % 4, 0:w] if kind == "na" else PS[:, SCO + g % 2, 0:w]
                    act.activation(PR[:, g % 4, 0:w], src, ACT.Exp, scale=-1.0 if kind == "na" else 1.0, bias=NM[:, g % 4:g % 4 + 1],
                                   accum_out=RS[:, g % 4:g % 4 + 1]).then_inc(exp_ready, 1)
                for hd in norm_q:
                    act.wait_ge(od_ps, hd + 1)
                    if hd < 3:
                        act.activation(OF[hd], PS[:, OB + (o0 + hd) % 2, :], ACT.Copy).then_inc(od_sum, 1)
                norm_q = []
                if i - 4 in ready_after and ready_after[i - 4] % 4 == 3:
                    hd = ready_after[i - 4] // 4
                    if kind == "diff":
                        norm_q = [hd]
                    else:
                        act.wait_ge(pv_ready, o0 + hd + 1)
                        r = slice((hd % 2) * HD, (hd % 2) * HD + HD)
                        src = PS[r, OB + (o0 + hd) % 2, :]
                        if kind == "fox":
                            dst = MH[r, hd // 2, :]
                        else:
                            dst, src = grid3(NAH[r, hd // 2, :], "natural"), natural_of(src)
                        act.activation(dst, src, ACT.Copy).then_inc(oh_done, 1)
                if kind == "diff" and i == LAST_STEP:
                    for hd in range(3):
                        diff_hi(hd)
                if kind == "diff" and i in (n + 2, LAST_STEP):
                    heads = range(3) if i == n + 2 else range(3, 4)
                    for hd in heads:
                        if hd < 3:
                            act.wait_ge(od_sum, hd + 1)
                        else:
                            act.wait_ge(od_ps, 4)
                        src = OF[hd] if hd < 3 else PS[:, OB + (o0 + hd) % 2, :]
                        act.activation(OF[hd], src, ACT.Ln, bias=BT[:, 0:1], scale=1.0 / P).then_inc(od_r, 1)
                    for hd in heads:
                        act.wait_ge(od_r, hd + 1 if hd < 3 else 7)
                        act.activation(OF[hd], OF[hd], ACT.Exp, scale=-0.5).then_inc(od_r, 1)
                for it in fills_done(kind, i):
                    fl = it["idx"]
                    if it["what"] == "qk":
                        bias = na_bias(fl, fl // 2 + 1) if kind == "na" else None
                        qk_part(kind, it["a"], parity_of_filler(kind, fl), fl, bias)
                    elif it["what"] == "gb":
                        gate_part(fl)
                    if it["ends"] and i < LAST_STEP:
                        hi_next(it["unit"])

        attention("fox")
        v_parts("v2", M1, 8)
        attention("diff")
        diff_hi(3)
        hi_next(fills_done("diff", LAST_STEP)[0]["unit"])

        def residual_tiles(name, gain, sq0, per_tile_units):
            for c in range(KD):
                for u in per_tile_units(c):
                    hi_next(u)
                act.wait_ge(acc_free, TL[name] + c + 1)
                gain_and_square(TL[name] + c, c, vcol(gain, c), sq0, c)

        residual_tiles("out1", "ffn_norm_g", 8, lambda c: [UN["out1"] + c // 2] if c % 2 else [])
        def swiglu_group(i):
            for j in range(2):
                a, b = 2 * j, 2 * j + 1
                t = 4 * i + TL["ffn1"]
                hi_part(i + UN["ffn1"] // 4 + 1, a)
                act.wait_ge(acc_free, t + a + 1)
                act.activation(T[:, a, 4:4 + S], T[:, a, 4:4 + S], ACT.Silu).then_inc(act_done, 1)
                hi_part(i + UN["ffn1"] // 4 + 1, b)
                act.wait_ge(prod, 2 * i + j + 1)
                act.activation(HH[:, bass.ds(2 * i + j, 1), :], T[:, b, 4:4 + S], ACT.Copy).then_inc(act_done, 1)

        def swiglu_last(i):
            for j in range(2):
                a, b = 2 * j, 2 * j + 1
                t = 4 * i + TL["ffn1"]
                hi_next(UN["ffn1"] + 4 * i + a)
                act.wait_ge(acc_free, t + a + 1)
                act.activation(T[:, a, 4:4 + S], T[:, a, 4:4 + S], ACT.Silu).then_inc(act_done, 1)
                hi_next(UN["ffn1"] + 4 * i + b)
                act.wait_ge(prod, 2 * i + j + 1)
                act.activation(HH[:, 2 * i + j, :], T[:, b, 4:4 + S], ACT.Copy).then_inc(act_done, 1)

        rstd(R[:, :], 2, 1.0 / D, PS[:, SCO, :])
        with act.Fori(0, KF // 2 - 1) as i:
            swiglu_group(i)
        swiglu_last(KF // 2 - 1)
        for c in range(KD):
            for j in range(3):
                hi_next(UN["down1"] + 3 * c + j)
            a = TL["down1"] + c
            act.wait_ge(acc_free, a + 1)
            if c >= 4:
                act.wait_ge(low_done, L0["down1"] + c - 3)
            act.activation(grid3(tile_t(a), "perm"), perm_of(X[:, c, :]), ACT.Copy,
                           scale=GG[:, c:c + 1]).then_inc(xg_ready, 1)
            act.wait_ge(xg_ready, c + 1)
            act.activation(XH[:, c, :], tile_t(a), ACT.Copy).then_inc(act_done, 1)
            act.wait_ge(ss_done, 16 + 2 * c)
            act.activation(SQ[:, 0, :], X[:, c, :], ACT.Square).then_inc(sq_ready, 1)
            act.activation(SQ[:, 1, :], X[:, c, :], ACT.Square, scale=vcol("final_norm_g", c)).then_inc(sq_ready, 1)

        rstd(R[:, :], 3, 1.0 / D, PS[:, SCO, :])
        act.wait_ge(r_mix, 2)
        act.activation(RP[:, :], SQ[:, 0, :], ACT.Ln, bias=BT[:, 0:1], scale=1.0 / D).then_inc(ln_done, 1)
        act.wait_ge(ln_done, 4)
        act.activation(RP[:, :], RP[:, :], ACT.Exp, scale=-0.5).then_inc(r_ready, 1)
        for i in range(8):
            a = TL["cab"] + i
            hi_next(UN["cab"] + i)
            act.wait_ge(acc_free, a + 1)
            func = ACT.Sigmoid if i % 2 else ACT.Identity
            act.activation(tile_t(a), tile_t(a), func,
                           bias=vcol("b_in_2", (12 if i % 2 == 0 else 16) + i // 2)).then_inc(act_done, 1)
            if i == 3:
                act.wait_ge(bias_in, 16 * 16)
                for r in range(ROWS):
                    act.activation(BN[:, :, :].rearrange("p h (g r c) -> p h g r c", r=ROWS, c=8)[:, :, :, r, :],
                                   BNR[:, r, :, :].rearrange("p h (g c) -> p h g c", c=8),
                                   ACT.Copy).then_inc(bias_ready, 1)
        for i in range(2):
            qk_part("na", TL["na0"] + i, 0, i, na_bias(i, 0))
            hi_next(UN["na0"] + i)
        v_parts("v3", M2, 0)
        attention("na")
        for c in range(6, KD):
            gate_part(c)
            hi_next(UN["gates_b"] + c)
        for c in range(KD):
            act.wait_ge(act_done, H0["gates_b"] + c + 1)
            act.activation(SG[:, gate_place(c), :], SG[:, gate_place(c), :], ACT.Sigmoid).then_inc(gate_ready, 1)
        with act.Fori(0, 2) as i:
            for s in range(4):
                hi_part(i + UN["gates_a"] // 4 + 1, s)
                act.wait_ge(acc_free, 4 * i + s + TL["gates_a"] + 1)
                act.activation(SG[:, bass.ds(4 * i + s, 1), :], T[:, s, 4:4 + S], ACT.Sigmoid,
                               bias=VEC[:, bass.ds(4 * i + s + vec_at["b_in_2"] + 20, 1)]).then_inc(act_done, 1)
        for k in range(4):
            act.wait_ge(ln_d, k + 1)
            if k >= 2:
                act.wait_ge(ss_done, 32 + k - 1)
            act.activation(LSQ[:, k % 2, :], Y[k], ACT.Square).then_inc(sq_ready, 1)
        hi_next(UN["na_out"])
        act.wait_ge(ln_ps, 2)
        act.activation(LR[:, :], PS[:, SCO + 1, :], ACT.Ln, bias=BT[:, 0:1], scale=1.0 / S).then_inc(ln_r, 1)
        act.wait_ge(ln_r, 1)
        act.activation(LR[:, :], LR[:, :], ACT.Exp, scale=-0.5).then_inc(ln_r, 1)
        hi_next(UN["na_out"] + 1)
        for k in range(4):
            if k == 2:
                hi_next(UN["na_out"] + 2)
            act.wait_ge(ln_n, k + 1)
            act.activation(Y[k], Y[k], ACT.Silu, scale=vcol("conv_ln_g_2", k),
                           bias=vcol("conv_ln_b_2", k)).then_inc(silu_done, 1)
            act.wait_ge(silu_done, k + 1)
            act.activation(CH[:, k, :], Y[k], ACT.Copy).then_inc(ch_done, 1)
        hi_next(UN["na_out"] + 3)
        for c in range(8):
            if c % 2:
                hi_next(UN["conv_out"] + c // 2)
            act.wait_ge(merged, c + 1)
            act.activation(MH2[:, c, :], tile_t(TL["conv_out"] + c), ACT.Copy).then_inc(act_done, 1)
        residual_tiles("out2", "norm2_g_2", 36, lambda c: [UN["out2"] + c])
        rstd(R[:, :], 5, 1.0 / D, PS[:, SCO, :])

        def geglu_group(i, static):
            for j in range(2):
                for v in range(2):
                    s = 2 * j + v
                    if static:
                        hi_next(UN["ffn2"] + 4 * i + s)
                        wcol = vcol("ffn_dw_w_2", 44 + 22 * v + 2 * i + j)
                        bcol = vcol("ffn_dw_b_2", 22 * v + 2 * i + j)
                    else:
                        hi_part(i + UN["ffn2"] // 4 + 1, s)
                        wcol = VEC[:, bass.ds(2 * i + j + vec_at["ffn_dw_w_2"] + 44 + 22 * v, 1)]
                        bcol = VEC[:, bass.ds(2 * i + j + vec_at["ffn_dw_b_2"] + 22 * v, 1)]
                    act.wait_ge(acc_free, 4 * i + s + TL["ffn2"] + 1)
                    if not (static and i == 0):
                        act.wait_ge(low_done, 2 * i + j + L0["ffn2"] - 1)
                    act.activation(CZ[j][v][:, :], T[:, s, 4:4 + S], ACT.Identity, scale=wcol, bias=bcol).then_inc(cz_mid, 1)
                act.wait_ge(cz_taps, 4 * i + 2 * j + 1)
                act.activation(CZ[j][0][:, :], CZ[j][0][:, :], ACT.Gelu).then_inc(gelu_done, 1)
                act.wait_ge(glu_ready, 2 * i + j + 1)
                dst = HH[:, 2 * i + j, :] if static else HH[:, bass.ds(2 * i + j, 1), :]
                act.activation(dst, CZ[j][1][:, :], ACT.Copy).then_inc(hid_hi, 1)

        geglu_group(0, True)
        with act.Fori(1, KF // 2 - 1) as i:
            geglu_group(i, False)
        geglu_group(KF // 2 - 1, True)
        for c in range(KD - 1):
            for j in range(3):
                hi_next(UN["down2"] + 3 * c + j)
            act.wait_ge(acc_free, TL["down2"] + c + 1)
            if c >= 2:
                act.wait_ge(ss_done, 44 + c - 1)
            act.activation(SQ[:, c % 2, :], X[:, c, :], ACT.Square).then_inc(sq_ready, 1)
        for h in range(2):
            act.activation((QC, GD)[h][:, :], BT[:, :], ACT.Ln)
            act.wait_ge(acc_free, TL["down2"] + KD + h)
            act.wait_ge(ss_done, 50)
            hs = slice(256 * h, 256 * h + 256)
            act.activation(SQ[:, 1, hs], X[:, KD - 1, hs], ACT.Square).then_inc(sq_ready, 1)
            rstd(RT[:, 2 * h:2 * h + 2], 6 + h, 1.0 / D, PS[:, SCO, 2 * h:2 * h + 2])
            act.wait_ge(r_ready, 6 + h)
            for t in range(2 * h, 2 * h + 2):
                act.wait_ge(out_ps, TC + t + 1)
                act.activation(OUT[:, t, S:2 * S], PS[:, out_bank(t, 1), :], ACT.Copy,
                               scale=RT[:, t:t + 1]).then_inc(out_ready[1], 1)

    @block.vector
    def _(dve):
        made = [0]

        def step(ins):
            made[0] += 1
            ins.then_inc(dve_made, 1)
            dve.wait_ge(dve_made, made[0])

        def tile_t(a, n=S):
            return T[:, a % 4, 4:4 + n]

        def ps(a, n=S):
            return PS[:, ACC + a % 2, 0:n]

        def tile_ready(name, i):
            if name == "init":
                dve.wait_ge(part_ready, i + 1)
            elif name[0] == "v":
                half, t = i // 4, i % 4
                if t < 3:
                    dve.wait_ge(part_ready, PT0[name] + 3 * half + t + 1)
                else:
                    dve.wait_ge(w_used, UN[name] + 2 * half + 2)
            elif name in ("out1", "na_out", "conv_out"):
                if i % 2 == 0:
                    dve.wait_ge(part_ready, PT0[name] + i // 2 + 1)
                else:
                    dve.wait_ge(w_used, UN[name] + i // 2 + 1)
            elif name[:4] == "down":
                dve.wait_ge(w_used, UN[name] + 3 * i + 3)
            else:
                dve.wait_ge(w_used, UN[name] + i + 1)

        def slots_drained(name):
            dve.wait_ge(act_done, H0[name])
            dve.wait_ge(low_done, L0[name])

        step(dve.memset(BT[:, :], EPS))
        step(dve.memset(T[:, :, 0:4], 0.0))
        step(dve.memset(T[:, :, 516:520], 0.0))
        step(dve.memset(CR[:, :].bitcast(F32), 0.0))
        dve.wait_ge(pool_made, 18)
        step(dve.tensor_copy(IDB[:, :], IDF[:, :]))
        step(dve.tensor_copy(CMB[:, :], CST[:, :]))
        step(dve.tensor_copy(SEL[:, :], SELF[:, :]))
        step(dve.tensor_copy(CR[64:65, :], POS[64:65, :]))

        def add_square(k, i, which=0, slot=0, total=None, squares=SQ):
            total = SS[:, which, :] if total is None else total
            dve.wait_ge(sq_ready, k)
            if i == 0:
                dve.tensor_copy(total, squares[:, slot, :]).then_inc(ss_done, 1)
            else:
                dve.wait_ge(ss_done, k - 1)
                dve.tensor_tensor(total, total, squares[:, slot, :], ALU.add).then_inc(ss_done, 1)

        def low_of_gain(name, gain, c):
            dve.wait_ge(act_done, H0[name] + c + 1)
            dve.scalar_tensor_tensor(out=XL[:, c, :], in0=X[:, c, :], scalar=vcol(gain, c), in1=XH[:, c, :].bitcast(F32),
                                     op0=ALU.mult, op1=ALU.subtract).then_inc(low_done, 1)

        for c in range(KD):
            tile_ready("init", c)
            dve.tensor_copy(X[:, c, :], PS[:, init_bank(c), :]).then_inc(acc_free, 1)
            if c == 1:
                dve.wait_ge(vec_t, 1)
                dve.tensor_copy(VEC[:, :], PS[:, OB + 1, 0:n_vec]).then_inc(vec_ready, 1)
                dve.wait_ge(vec_ready, 1)
            if c:
                low_of_gain("init", "mix_norm_g", c - 1)
            if c > 1:
                add_square(c - 1, c - 2, 0, c % 2)
        low_of_gain("init", "mix_norm_g", KD - 1)
        for c in range(KD - 2, KD):
            add_square(c + 1, c, 0, c % 2)
        dve.wait_ge(wf_split, 1)
        dve.tensor_tensor(WFL[:, :, :], WFR[:, :, :], WFH[:, :, :].bitcast(F32), ALU.subtract).then_inc(wf_split, 1)
        def rt_copy(k):
            dve.wait_ge(rt_ps, k)
            dve.tensor_copy(RT[:, :], PS[:, SCO + 1, :].rearrange("p (t q) -> p t q", q=P)[:, :, 0]).then_inc(rt_ready, 1)
            dve.wait_ge(rt_ready, k)

        def v_take(name, i, bias=False):
            a, c0, t = TL[name] + i, 256 * (i // 4), i % 4
            tile_ready(name, i)
            if i >= 4:
                dve.wait_ge(low_done, L0[name] + i - 3)
            if bias:
                dve.scalar_tensor_tensor(out=tile_t(a, 256), in0=ps(a, 256), scalar=RT[:, t:t + 1],
                                         in1=BVB[:, c0:c0 + 256], op0=ALU.mult, op1=ALU.add).then_inc(acc_free, 1)
            else:
                dve.tensor_scalar(tile_t(a, 256), ps(a, 256), RT[:, t:t + 1], None, ALU.mult).then_inc(acc_free, 1)

        def v_phase(name, mem, bias, extra=None, taken=0):
            if taken == 0:
                slots_drained(name)
            for i in range(8 + 1):
                if taken <= i < 8:
                    v_take(name, i, bias)
                if i >= 1:
                    a, c0, t = TL[name] + i - 1, 256 * ((i - 1) // 4), (i - 1) % 4
                    dve.wait_ge(act_done, H0[name] + i)
                    dve.tensor_tensor(mem["VL"][:, t, c0:c0 + 256], tile_t(a, 256), mem["VH"][:, t, c0:c0 + 256].bitcast(F32),
                                      ALU.subtract).then_inc(low_done, 1)
                if extra:
                    extra(i)

        def qk_take(name, i, r):
            tile_ready(name, i)
            qk_scale(TL[name] + i, i, r, name == "na0")

        def qk_scale(a, i, r, negate):
            if i % 2 == 0:
                ins = dve.scalar_tensor_tensor(out=tile_t(a), in0=ps(a), scalar=(-1 if negate else 1) * HD ** -0.5, in1=r, op0=ALU.mult, op1=ALU.mult)
            else:
                ins = dve.tensor_tensor(tile_t(a), ps(a), r, ALU.mult)
            ins.then_inc(acc_free, 1)

        def qk_low(name, i, par, mem, pair=None, a=None):
            a = TL[name] + i if a is None else a
            hi, lo = (mem["QH"], mem["QL"]) if i % 2 == 0 else (mem["KH"], mem["KL"])
            dve.wait_ge(act_done, H0[name] + i + 1)
            if pair is None:
                ins = dve.tensor_tensor(lo[:, par, :], tile_t(a), hi[:, par, :].bitcast(F32), ALU.subtract)
            else:
                b = B8[:, pair:pair + 1] if i % 2 == 0 else vcol("b_in_2", 4 + pair)
                ins = dve.scalar_tensor_tensor(out=lo[:, par, :], in0=tile_t(a), scalar=b, in1=hi[:, par, :].bitcast(F32),
                                               op0=ALU.add, op1=ALU.subtract)
            ins.then_inc(low_done, 1)

        def log_forget(i):
            if i == 1:
                dve.wait_ge(fl_ps, 2)
                for t in range(TC):
                    dve.tensor_tensor(Z[:, 0, 8 * t:8 * t + 8], PS[:, TRB + 1, 8 * t:8 * t + 8], BFG[:, :],
                                      ALU.add).then_inc(fl_step, 1)
                dve.wait_ge(fl_step, 6)
                dve.scalar_tensor_tensor(out=Z[:, 1, :], in0=Z[:, 0, :], scalar=-1.0, in1=Z[:, 0, :], op0=ALU.mult,
                                         op1=ALU.max).then_inc(fl_step, 1)
                dve.tensor_scalar(Z[:, 3, :], Z[:, 0, :], 0.0, None, ALU.min).then_inc(fl_step, 1)
            if i == 4:
                dve.wait_ge(fl_act, 3)
                dve.tensor_tensor(Z[:, 2, :], Z[:, 2, :], Z[:, 3, :], ALU.subtract).then_inc(fl_step, 1)
                dve.wait_ge(fl_step, 9)
                nlf = Z[:, 2, :].rearrange("p (t h) -> p t h", h=8)
                for i, c in enumerate((0, 32)):
                    dve.tensor_copy(LFH[:, :, c:c + 8], nlf).then_inc(fl_step, 1)
                    dve.wait_ge(fl_step, 10 + i)
                    dve.tensor_tensor(LFL[:, :, c:c + 8], nlf, LFH[:, :, c:c + 8].bitcast(F32), ALU.subtract).then_inc(lf_ready, 1)
            if i == 5:
                dve.wait_ge(fl_act, 1)
                dve.tensor_tensor(LAM[:, 4:5], LAM[:, 3:4], LAM[:, 2:3], ALU.subtract).then_inc(lam_ready, 1)
                dve.wait_ge(lam_ready, 1)
                dve.tensor_scalar(LAM[:, 5:6], LAM[:, 4:5], LAM_INIT, None, ALU.subtract).then_inc(lam_ready, 1)
                dve.tensor_copy(RI[:, 0:1], BT[:, :]).then_inc(cr_dve, 1)
            if i == 7:
                dve.wait_ge(cr_act, 2)
                dve.tensor_tensor(CR[32:40, :], PS[32:40, TRB + 1, :], CT[32:40, :].bitcast(F32),
                                  ALU.subtract).then_inc(cr_dve, 1)
            if i == 2:
                dve.wait_ge(rpb_in, 16 * RPR)
                dve.tensor_scalar(RPP[:, :], RPP[:, :], -1.0, None, ALU.mult).then_inc(rpb_negated, 1)

        slots_drained("fox0")
        for i in range(2):
            if i == 0:
                dve.wait_ge(r_ready, 1)
            qk_take("fox0", i, R[:, :])
        for i in range(2):
            qk_low("fox0", i, 0, M1)
        dve.wait_ge(fl_ps, 1)
        dve.tensor_tensor(FLR[0:8, :], PS[0:8, TRB, :], R[0:8, :], ALU.mult).then_inc(fl_row, 1)
        rt_copy(1)
        dve.wait_ge(consts_in, 16 * 5)
        for i in range(2):
            dve.tensor_tensor_reduce(out=LAMV[:, 2 * i, :], in0=LAMV[:, 2 * i, :], in1=LAMV[:, 2 * i + 1, :], scale=1.0,
                                     scalar=0.0, op0=ALU.mult, op1=ALU.add, accum_out=LAM[:, i:i + 1]).then_inc(fl_step, 1)
        step(dve.tensor_tensor(GG[:, :], vcol("final_norm_g", 0, 8), vcol("norm1_g_2", 0, 8), ALU.mult))
        step(dve.tensor_scalar(B8[:, :], vcol("b_in_2", 0, 4), -HD ** -0.5, None, ALU.mult))
        step(dve.tensor_scalar(GD[:, :], vcol("diff_norm_g", 0), 1.0 - LAM_INIT, None, ALU.mult))
        step(dve.tensor_copy(TRI[:, :], STG[:, :]))
        step(dve.memset(LFH[:, :, :].bitcast(F32), 0.0))
        step(dve.memset(LFL[:, :, :].bitcast(F32), 0.0))
        v_phase("v1", M1, False, log_forget)
        for part in ("PTH", "PTL"):
            step(dve.memset(M1[part][:, 3, 2 * P:3 * P].bitcast(F32), 0.0))
        dve.wait_ge(rpb_out, 16 * 8)

        def fill_take(it, kind, r):
            what, i, a = it["what"], it["idx"], it["a"]
            if what == "qk":
                if it["ends"]:
                    dve.wait_ge(w_used, it["unit"] + 1)
                users = [x for x in fill_plan(kind) if x["what"] == "qk" and x["a"] < a and x["a"] % 4 == a % 4]
                if users:
                    dve.wait_ge(low_done, L0[FAM[kind]["fill"]] + users[-1]["idx"] + 1)
                qk_scale(a, i, r, kind == "na")
            elif what == "v":
                if i == 0:
                    slots_drained("v2")
                v_take("v2", i)
            elif what == "gb":
                gate_take(i)
            else:
                if it["ends"]:
                    dve.wait_ge(w_used, it["unit"] + 1)
                else:
                    dve.wait_ge(part_ready, it["part"])
                dve.tensor_tensor(X[:, i, :], ps(a), X[:, i, :], ALU.add).then_inc(acc_free, 1)

        def gate_take(c):
            a = TL["gates_b"] + c
            dve.wait_ge(w_used, UN["gates_b"] + c + 1)
            if c < 4:
                dve.wait_ge(low_done, L0["gates_b"])
            else:
                dve.wait_ge(act_done, H0["gates_b"] + c - 3)
            dve.tensor_tensor(grid3(tile_t(a), "natural"), natural_of(ps(a)), grid3(RN2, "natural"),
                              ALU.mult).then_inc(acc_free, 1)

        def diff_normed(hd):
            dve.wait_ge(od_r, 4 + hd if hd < 3 else 8)
            dve.tensor_tensor(ODN[:, hd, :], ODR[:, hd, :], OF[hd], ALU.mult).then_inc(od_scaled, 1)

        def diff_low(hd):
            dve.wait_ge(oh_done, 8 + hd + 1)
            dve.scalar_tensor_tensor(out=ML[:, 4 + hd, :], in0=ODN[:, hd, :], scalar=GD[:, 0:1],
                                     in1=MH[:, 4 + hd, :].bitcast(F32), op0=ALU.mult,
                                     op1=ALU.subtract).then_inc(o_free, 1)

        def attention(kind, r, behind=None):
            f = FAM[kind]
            sc, tr, ready_after = family(kind)
            mem, s0, t0, o0, name = f["mem"], f["s0"], f["t0"], f["o0"], f["fill"]
            n = len(sc)
            slots_drained(name)
            for i in range(LAST_STEP + 1):
                if i < n:
                    hd, half, qb = sc[i]
                    g = s0 + i
                    k0, k1 = keys_of(kind, qb)
                    w = (k1 - k0) * P
                    dve.wait_ge(sc_ready, g + 1)
                    src = PS[:, SCO + g % 2, 0:w]
                    if kind == "na":
                        if slot_free(kind, i):
                            dve.wait_ge(tr_ready, slot_free(kind, i))
                        first = 2 * 8 * ROWS if qb == 0 else 0
                        bias = BN[:, hd, first:first + w]
                        dve.wait_ge(exp_ready, g - 3)
                        dve.tensor_tensor_reduce(out=PR[:, g % 4, 0:w], in0=src, in1=bias, scale=1.0,
                                                 scalar=-NEG, op0=ALU.add, op1=ALU.min,
                                                 accum_out=NM[:, g % 4:g % 4 + 1]).then_inc(max_ready, 1)
                    elif g >= 4:
                        dve.wait_ge(exp_ready, g - 3)
                    if kind != "na":
                        dve.tensor_reduce(NM[:, g % 4:g % 4 + 1], src, AX, ALU.max, negate=True).then_inc(max_ready, 1)
                if 1 <= i <= n:
                    g = s0 + i - 1
                    hd, half, qb = sc[i - 1]
                    k0, k1 = keys_of(kind, qb)
                    w = (k1 - k0) * P
                    dve.wait_ge(exp_ready, g + 1)
                    if g >= 4:
                        dve.wait_ge(p_ready, t0 if i - 1 < 4 else slot_free(kind, i - 1))
                    dve.reciprocal(RI[:, g % 4:g % 4 + 1], RS[:, g % 4:g % 4 + 1]).then_inc(rinv_done, 1)
                    ri = RI[:, g % 4:g % 4 + 1]
                    if kind == "diff" and half == 1:
                        dve.wait_ge(rinv_done, g + 1)
                        dve.tensor_tensor(ri, ri, LAM[:, 5:6], ALU.mult).then_inc(lam_ready, 1)
                        dve.wait_ge(lam_ready, 2 + i // 2)
                        dve.wait_ge(p_half, i // 2)
                        dve.scalar_tensor_tensor(out=PR[:, (g - 1) % 4, 0:w], in0=PR[:, g % 4, 0:w], scalar=ri,
                                                 in1=PR[:, (g - 1) % 4, 0:w], op0=ALU.mult,
                                                 op1=ALU.add).then_inc(p_ready, 1)
                    else:
                        dve.wait_ge(rinv_done, g + 1)
                        dve.tensor_scalar(PR[:, g % 4, 0:w], PR[:, g % 4, 0:w], ri, None,
                                          ALU.mult).then_inc(p_half if kind == "diff" else p_ready, 1)
                for it in fills_done(kind, i - 1):
                    if it["what"] == "qk":
                        fl = it["idx"]
                        qk_low(name, fl, parity_of_filler(kind, fl), mem, fl // 2 + 1 if kind == "na" else None, it["a"])
                if behind:
                    behind(i)
                if i - 3 in ready_after:
                    j = ready_after[i - 3]
                    hd, qb = tr[j]
                    g = t0 + j
                    k0, k1 = keys_of(kind, qb)
                    dve.wait_ge(pth_done, g + 1)
                    q = slice(qb * P, (qb + 1) * P)
                    dve.tensor_tensor(mem["PTL"][:, k0:k1, q],
                                      PS[:, TRB + g % 2, 0:(k1 - k0) * P].rearrange("p (k q) -> p k q", q=P),
                                      mem["PTH"][:, k0:k1, q].bitcast(F32), ALU.subtract).then_inc(ptl_done, 1)
                if i - 4 in ready_after and ready_after[i - 4] % 4 == 3:
                    hd = ready_after[i - 4] // 4
                    bank = PS[:, OB + (o0 + hd) % 2, :]
                    if kind == "diff":
                        dve.wait_ge(pv_ready, o0 + hd + 1)
                        dve.tensor_copy(ODR[:, hd, :], bank).then_inc(od_copy, 1)
                        dve.wait_ge(od_copy, hd + 1)
                        if hd:
                            dve.wait_ge(od_ps, hd)
                        dve.tensor_tensor(SQ[:, 0, :], ODR[:, hd, :], ODR[:, hd, :], ALU.mult).then_inc(od_sq, 1)
                    else:
                        dve.wait_ge(oh_done, o0 + hd + 1)
                        rr = slice((hd % 2) * HD, (hd % 2) * HD + HD)
                        if kind == "fox":
                            dve.tensor_tensor(ML[rr, hd // 2, :], bank[rr, :], MH[rr, hd // 2, :].bitcast(F32),
                                              ALU.subtract).then_inc(o_free, 1)
                        else:
                            dve.tensor_tensor(grid3(NAL[rr, hd // 2, :], "natural"), natural_of(bank[rr, :]),
                                              grid3(NAH[rr, hd // 2, :].bitcast(F32), "natural"),
                                              ALU.subtract).then_inc(o_free, 1)
                if kind == "diff" and i == LAST_STEP:
                    for h in range(3):
                        diff_normed(h)
                    for h in range(3):
                        diff_low(h)
                for it in fills_done(kind, i):
                    fill_take(it, kind, r)

        diff_, keyc = MKS[:, 0, :], KC[:, :]

        def clause(dst, src, op, bound):
            return lambda: step(dve.tensor_scalar(MKS[:, dst, :], src, bound, None, op))

        def combine(dst, other, op):
            return lambda: step(dve.tensor_tensor(MKS[:, dst, :], MKS[:, dst, :], MKS[:, other, :], op))

        def as_mask(m):
            return lambda: step(dve.tensor_scalar(NMB[:, m, :], MKS[:, 1, :], NEG, -NEG, ALU.mult, ALU.add))

        def query_column():
            step(dve.tensor_scalar(QI[:, 1:2], QI[:, 0:1], 7, None, ALU.bitwise_and))
            step(dve.tensor_copy(QC[:, :], QI[:, 1:2]))
            step(dve.tensor_scalar(QC[64:128, :], QC[64:128, :], 8.0, None, ALU.add))

        mask_steps = [
            query_column,
            lambda: step(dve.tensor_scalar(diff_, KC[:, :], QC[:, 0:1], None, ALU.subtract)),
            clause(1, diff_, ALU.is_ge, 8.0), clause(2, diff_, ALU.is_le, 23.0), combine(1, 2, ALU.mult), as_mask(0),
            clause(1, diff_, ALU.is_ge, -8.0), clause(2, diff_, ALU.is_le, 7.0), clause(3, keyc, ALU.is_le, 15.0),
            combine(2, 3, ALU.max), combine(1, 2, ALU.mult), as_mask(1),
            clause(1, diff_, ALU.is_ge, 8.0), clause(3, keyc, ALU.is_ge, 16.0), combine(1, 3, ALU.max),
            clause(2, diff_, ALU.is_le, 23.0), combine(1, 2, ALU.mult), as_mask(2)]

        attention("fox", R[:, :], lambda i: mask_steps[i]() if i < len(mask_steps) else None)
        v_take("v2", 3)
        v_phase("v2", M1, False, taken=4)
        attention("diff", R[:, :])
        diff_normed(3)
        diff_low(3)

        def residual(name, gain, sq0):
            for c in range(KD + 1):
                if c < KD:
                    tile_ready(name, c)
                    dve.tensor_tensor(X[:, c, :], ps(TL[name] + c), X[:, c, :], ALU.add).then_inc(acc_free, 1)
                if c:
                    low_of_gain(name, gain, c - 1)
                    add_square(sq0 + c, c - 1, 0, (c - 1) % 2)

        residual("out1", "ffn_norm_g", 8)

        def swiglu_low(q, dst, src, b):
            dve.wait_ge(act_done, 2 * q + 2 + H0["ffn1"])
            dve.tensor_tensor(dst, T[:, b, 4:4 + S], src.bitcast(F32), ALU.subtract).then_inc(low_done, 1)

        def swiglu_pair(i, j, first):
            q = 2 * i + j
            for v in range(2):
                s = 2 * j + v
                dve.wait_ge(w_used, 4 * i + s + UN["ffn1"] + 1)
                if not first:
                    dve.wait_ge(low_done, q - 1 + L0["ffn1"])
                src = PS[:, early_bank(s) if first else ACC + s % 2, :]
                dve.tensor_tensor(T[:, s, 4:4 + S], src, R[:, :], ALU.mult).then_inc(acc_free, 1)
                if v == 0 and not (first and j == 0):
                    if isinstance(i, int):
                        swiglu_low(q - 1, HL[:, q - 1, :], HH[:, q - 1, :], (s - 1) % 4)
                    else:
                        swiglu_low(q - 1, HL[:, bass.ds(q - 1, 1), :], HH[:, bass.ds(q - 1, 1), :], (s - 1) % 4)
            dve.wait_ge(act_done, 4 * i + 2 * j + 1 + H0["ffn1"])
            dve.wait_ge(acc_free, 4 * i + 2 * j + 2 + TL["ffn1"])
            dve.tensor_tensor(T[:, 2 * j + 1, 4:4 + S], T[:, 2 * j + 1, 4:4 + S], T[:, 2 * j, 4:4 + S],
                              ALU.mult).then_inc(prod, 1)

        dve.wait_ge(r_ready, 2)
        for j in range(2):
            swiglu_pair(0, j, True)
        with dve.Fori(1, KF // 2) as i:
            for j in range(2):
                swiglu_pair(i, j, False)
        swiglu_low(KF - 1, HL[:, KF - 1, :], HH[:, KF - 1, :], 3)

        for c in range(KD + 1):
            if c < KD:
                tile_ready("down1", c)
                dve.tensor_tensor(X[:, c, :], ps(TL["down1"] + c), X[:, c, :], ALU.add).then_inc(acc_free, 1)
            if c:
                k = c - 1
                dve.wait_ge(act_done, H0["down1"] + k + 1)
                dve.tensor_tensor(XL[:, k, :], tile_t(TL["down1"] + k), XH[:, k, :].bitcast(F32),
                                  ALU.subtract).then_inc(low_done, 1)
                add_square(16 + 2 * k + 1, k, 0, 0)
                add_square(16 + 2 * k + 2, k, 1, 1)
        dve.wait_ge(r_ready, 3)
        dve.wait_ge(norm_ps, 4)
        dve.tensor_tensor(SQ[:, 0, :], PS[:, SCO + 1, :], R[:, :], ALU.mult).then_inc(r_mix, 1)
        dve.wait_ge(r_mix, 1)
        dve.tensor_tensor(SQ[:, 0, :], SQ[:, 0, :], R[:, :], ALU.mult).then_inc(r_mix, 1)
        dve.wait_ge(r_ready, 4)
        dve.tensor_tensor(RN2, R[:, :], RP[:, :], ALU.mult).then_inc(r_mix, 1)
        dve.wait_ge(r_mix, 3)
        dve.tensor_copy(grid3(RP[:, :], "perm"), perm_of(RN2)).then_inc(r_mix, 1)

        taps = [(t, c) for t in range(6) for c in range(2)]
        for j in range(6):
            taps += [(6 + j, 0), (2 * j, 2), (6 + j, 1), (2 * j + 1, 2)]
        before_v = len(taps)
        last = iter(range(TAPS))
        for t in range(12, TAPS):
            taps += [(t, 0), (next(last), 3), (t, 1)] + ([(next(last), 3)] if t < 24 else []) + [(t, 2)]
        assert sorted(taps) == [(t, c) for t in range(TAPS) for c in range(4)]
        n_taps = [0]

        def conv_taps(n, limit=len(taps)):
            for k in range(n_taps[0], min(n_taps[0] + n, limit)):
                n_taps[0] += 1
                t, c = taps[k]
                src = U[:, c, UO - TAPS // 2 + t:UO - TAPS // 2 + t + S]
                w = vcol("conv_dw_w_2", 4 * t + c)
                if t == 0:
                    dve.wait_ge(low_done, L0["cab"] + c + 1)
                    if c == 2:
                        dve.wait_ge(x1_done, KD)
                    if c == 3:
                        dve.wait_ge(acc_free, TL["v3"] + 8)
                    dve.tensor_scalar(Y[c], src, w, vcol("conv_dw_b_2", c), ALU.mult, ALU.add).then_inc(conv_done, 1)
                else:
                    dve.wait_ge(conv_done, taps.index((t - 1, c)) + 1)
                    dve.scalar_tensor_tensor(out=Y[c], in0=src, scalar=w, in1=Y[c], op0=ALU.mult,
                                             op1=ALU.add).then_inc(conv_done, 1)

        slots_drained("cab")
        step(dve.memset(U[:, :, 0:UO], 0.0))
        step(dve.memset(U[:, :, UO + S:UW], 0.0))
        for i in range(8 + 1):
            if i < 8:
                a = TL["cab"] + i
                tile_ready("cab", i)
                if i >= 4:
                    dve.wait_ge(low_done, L0["cab"] + (i - 4) // 2 + 1)
                src = PS[:, early_bank(i), :] if i < 4 else ps(a)
                dve.tensor_tensor(grid3(tile_t(a), "natural"), natural_of(src), grid3(RN2, "natural"),
                                  ALU.mult).then_inc(acc_free, 1)
                dve.scalar_tensor_tensor(out=X[:, i, :], in0=X[:, i, :], scalar=vcol("final_norm_g", i), in1=R[:, :],
                                         op0=ALU.mult, op1=ALU.mult).then_inc(x1_done, 1)
            if i >= 2 and i % 2 == 0:
                c, a = i // 2 - 1, TL["cab"] + i - 1
                dve.wait_ge(act_done, H0["cab"] + i)
                dve.tensor_tensor(U[:, c, UO:UO + S], tile_t(a - 1), tile_t(a), ALU.mult).then_inc(low_done, 1)
            if 4 <= i < 8:
                conv_taps(3, 12)

        slots_drained("na0")
        for i in range(2):
            qk_take("na0", i, RP[:, :])
            qk_low("na0", i, 0, M2, 0)
            conv_taps(4)
        rt_copy(2)
        dve.wait_ge(bv_in, 16)
        v_phase("v3", M2, True, lambda i: conv_taps(2, before_v))
        dve.wait_ge(bias_ready, ROWS)
        for part in ("PTH", "PTL"):
            step(dve.memset(M2[part][:, 1, 3 * P:S].bitcast(F32), 0.0))
        attention("na", RP[:, :], lambda i: conv_taps(2 if N_SCORES - 8 <= i < N_SCORES else int(i % 4 != 3)))
        for c in range(6, KD):
            gate_take(c)
            conv_taps(6)
        for i in range(8):
            a = TL["gates_a"] + i
            tile_ready("gates_a", i)
            dve.wait_ge(act_done, H0["gates_a"] + i - 3)
            dve.tensor_tensor(grid3(tile_t(a), "natural"), natural_of(ps(a)), grid3(RN2, "natural"),
                              ALU.mult).then_inc(acc_free, 1)
            if i < 7:
                conv_taps(6 if i < 6 else len(taps))
            if i == 6:
                dve.wait_ge(conv_done, len(taps))
                dve.tensor_tensor(LSUM[:, :], Y[0], Y[1], ALU.add).then_inc(ln_sum, 1)
                for k in (2, 3):
                    dve.wait_ge(ln_sum, k - 1)
                    dve.tensor_tensor(LSUM[:, :], LSUM[:, :], Y[k], ALU.add).then_inc(ln_sum, 1)

        def na_out_take(c):
            tile_ready("na_out", c)
            if c == 0:
                dve.wait_ge(act_done, H0["na_out"])
            dve.tensor_tensor(SG[:, c, :], ps(TL["na_out"] + c), SG[:, c, :], ALU.mult).then_inc(acc_free, 1)

        dve.wait_ge(ln_ps, 1)
        for k in range(4):
            dve.scalar_tensor_tensor(out=Y[k], in0=PS[:, SCO, :], scalar=-1.0 / S, in1=Y[k], op0=ALU.mult,
                                     op1=ALU.add).then_inc(ln_d, 1)
        for k in range(4):
            add_square(32 + k + 1, k, 0, k % 2, LSUM[:, :], LSQ)
        for c in range(4):
            na_out_take(c)
        dve.wait_ge(ln_r, 2)
        for k in range(4):
            dve.tensor_tensor(Y[k], Y[k], LR[:, :], ALU.mult).then_inc(ln_n, 1)
        na_out_take(4)
        na_out_take(5)

        def branch_low(k):
            dve.wait_ge(ch_done, k + 1)
            dve.tensor_tensor(CL[:, k, :], Y[k], CH[:, k, :].bitcast(F32), ALU.subtract).then_inc(cl_done, 1)

        branch_low(0)
        branch_low(1)
        na_out_take(6)
        branch_low(2)
        branch_low(3)
        na_out_take(7)
        for c in range(8 + 1):
            if c < 8:
                a = TL["conv_out"] + c
                tile_ready("conv_out", c)
                if c >= 4:
                    dve.wait_ge(low_done, L0["conv_out"] + c - 3)
                if c == 0:
                    dve.wait_ge(gate_ready, KD)
                dve.tensor_tensor(tile_t(a), ps(a), SG[:, gate_place(c), :], ALU.mult).then_inc(acc_free, 1)
                dve.wait_ge(acc_free, a + 1)
                dve.tensor_tensor(tile_t(a), tile_t(a), SG[:, c, :], ALU.add).then_inc(merged, 1)
            if c:
                a = TL["conv_out"] + c - 1
                dve.wait_ge(act_done, H0["conv_out"] + c)
                dve.tensor_tensor(ML2[:, c - 1, :], tile_t(a), MH2[:, c - 1, :].bitcast(F32),
                                  ALU.subtract).then_inc(low_done, 1)
        dve.wait_ge(x1_done, 8)
        residual("out2", "norm2_g_2", 36)

        def geglu_low(q, dst, src, j):
            dve.wait_ge(hid_hi, q + 1)
            dve.tensor_tensor(dst, CZ[j][1][:, :], src.bitcast(F32), ALU.subtract).then_inc(low_done, 1)

        def geglu_pair(i, j, first):
            q = 2 * i + j
            static = isinstance(i, int)
            for v in range(2):
                s = 2 * j + v
                dve.wait_ge(w_used, 4 * i + s + UN["ffn2"] + 1)
                if not first:
                    dve.wait_ge(cz_taps, 4 * i + s - 3)
                src = PS[:, early_bank(s) if first else ACC + s % 2, :]
                dve.tensor_tensor(T[:, s, 4:4 + S], src, R[:, :], ALU.mult).then_inc(acc_free, 1)
                if v == 0 and not (first and j == 0):
                    if static:
                        geglu_low(q - 1, HL[:, q - 1, :], HH[:, q - 1, :], 1 - j)
                    else:
                        geglu_low(q - 1, HL[:, bass.ds(q - 1, 1), :], HH[:, bass.ds(q - 1, 1), :], 1 - j)
                z = CZ[j][v][:, :]

                def w(tap):
                    c = 2 * i + (j + vec_at["ffn_dw_w_2"] + 2 * KF * tap + KF * v)
                    return VEC[:, c:c + 1] if static else VEC[:, bass.ds(c, 1)]

                dve.wait_ge(cz_mid, 4 * i + s + 1)
                dve.scalar_tensor_tensor(out=z, in0=T[:, s, 3:3 + S], scalar=w(0), in1=z, op0=ALU.mult,
                                         op1=ALU.add).then_inc(cz_tap, 1)
                dve.wait_ge(cz_tap, 4 * i + s + 1)
                dve.scalar_tensor_tensor(out=z, in0=T[:, s, 5:5 + S], scalar=w(2), in1=z, op0=ALU.mult,
                                         op1=ALU.add).then_inc(cz_taps, 1)
            dve.wait_ge(gelu_done, q + 1)
            dve.wait_ge(cz_taps, 4 * i + 2 * j + 2)
            dve.tensor_tensor(CZ[j][1][:, :], CZ[j][1][:, :], CZ[j][0][:, :], ALU.mult).then_inc(glu_ready, 1)

        dve.wait_ge(r_ready, 5)
        slots_drained("ffn2")
        for j in range(2):
            geglu_pair(0, j, True)
        with dve.Fori(1, KF // 2) as i:
            for j in range(2):
                geglu_pair(i, j, False)
        geglu_low(KF - 1, HL[:, KF - 1, :], HH[:, KF - 1, :], 1)

        for c in range(KD - 1):
            a = TL["down2"] + c
            tile_ready("down2", c)
            dve.tensor_tensor(X[:, c, :], ps(a), X[:, c, :], ALU.add).then_inc(acc_free, 1)
            dve.wait_ge(acc_free, a + 1)
            dve.tensor_scalar(YF[:, c, :], X[:, c, :], vcol("norm_f_g_2", c), None, ALU.mult).then_inc(low_done, 1)
            if c:
                add_square(44 + c, c - 1, 0, (c - 1) % 2)
        for h in range(2):
            c, a, hs = KD - 1, TL["down2"] + KD - 1 + h, slice(256 * h, 256 * h + 256)
            if h == 0:
                dve.wait_ge(part_ready, n_part + 1)
            else:
                tile_ready("down2", c)
            dve.tensor_tensor(X[:, c, hs], PS[:, ACC + a % 2, hs], X[:, c, hs], ALU.add).then_inc(acc_free, 1)
            dve.wait_ge(acc_free, a + 1)
            dve.tensor_scalar(YF[:, c, hs], X[:, c, hs], vcol("norm_f_g_2", c), None, ALU.mult).then_inc(low_done, 1)
            if h == 0:
                add_square(51, KD - 2, 0, 0)
            dve.wait_ge(r_ready, 6 + h)
            for t in range(2 * h, 2 * h + 2):
                dve.wait_ge(out_ps, t + 1)
                dve.tensor_scalar(OUT[:, t, 0:S], PS[:, out_bank(t, 0), :], RT[:, t:t + 1], None,
                                  ALU.mult).then_inc(out_ready[0], 1)

    ctx.close()


_INS = {"x": (S, D), "w_in": None, "b_forget": (8,), "lambda_q1": (HD,), "lambda_k1": (HD,), "lambda_q2": (HD,),
        "lambda_k2": (HD,), "mix_norm_g": (D,), "diff_norm_g": (P,), "w_out": None, "ffn_norm_g": (D,),
        "w_gate": None, "w_up": None, "w_down": None, "final_norm_g": (D,), "norm1_g_2": (D,), "w_in_2": None,
        "b_in_2": (36 * P,), "rpb_2": (8, RPR, RPC), "w_na_out_2": None, "conv_dw_w_2": (TAPS * 4 * P,),
        "conv_dw_b_2": (4 * P,), "conv_ln_g_2": (4 * P,), "conv_ln_b_2": (4 * P,), "w_conv_out_2": None,
        "w_out_2": None, "norm2_g_2": (D,), "w_up_2": None, "ffn_dw_w_2": (3 * 2 * FF,), "ffn_dw_b_2": (2 * FF,),
        "w_down_2": None, "norm_f_g_2": (D,)}


def kernel(**inputs):
    import concourse.bacc as bacc
    from concourse.bass_utils import run_bass_kernel_spmd

    nc = bacc.Bacc("TRN2", target_bir_lowering=False, num_devices=1)
    arrays, d = {}, {}
    for name, shape in _INS.items():
        a = np.ascontiguousarray(inputs[name])
        a = a.reshape(shape or a.shape[1:])
        arrays["in_" + name] = a
        d[name] = nc.dram_tensor("in_" + name, a.shape, mybir.dt.from_np(a.dtype), kind="ExternalInput").ap()
    d["out"] = nc.dram_tensor("out_x", (S, D), F32, kind="ExternalOutput").ap()
    program(nc, d)
    r = run_bass_kernel_spmd(nc, [arrays], core_ids=[0])
    return r.results[0]["out_x"].reshape(inputs["x"].shape)
```
